# Optimizing a Trainium2 kernel written in Bass

```python
import math
import jax, jax.numpy as jnp
from jax import lax
import numpy as np

D_MODEL = 1024
BATCH = 1
SEQ = 1024
DEPTH = 4
DEC_BATCH = 1
DEC_SEQ = 32
PAST_LEN = 512

CHUNK = 64
N_MIXERS = 3
Q_BLOCK = 128
EPS = 1e-6
NEG = -1e30
MIX_W = D_MODEL
MEM_TOKENS = 256
MEM_HEADS = 4
MEM_HEAD_DIM = 64
MEM_W = MEM_HEADS * MEM_HEAD_DIM
BRANCH_W = MIX_W - MEM_W
GATE_W = MIX_W
A_HEADS = 12
A_HEAD_DIM = 64
A_BAND_CHUNKS = 8
A_PAST_ROWS = A_BAND_CHUNKS * CHUNK
A_REL_CLIP = 128
B_HEADS = 6
B_HEAD_DIM = 64
B_V_DIM = 2 * B_HEAD_DIM
C_HEADS = 12
C_NOPE = 64
C_ROPE = 32
C_V = 64
C_Q_LORA = 384
C_KV_LORA = 256
ROPE_BASE = 10000.0
N_A = (DEPTH + 2) // 3
N_B = (DEPTH + 1) // 3
N_C = DEPTH // 3
IN_A = 3 * A_HEADS * A_HEAD_DIM + MEM_W + GATE_W
IN_B = 2 * B_HEADS * 2 * B_HEAD_DIM + B_HEADS * B_V_DIM + MEM_W + GATE_W
IN_C = C_Q_LORA + C_KV_LORA + C_ROPE + MEM_W + GATE_W

kernel_name = "hybrid_chunk_stream_encoder_step"

def _rmsnorm(x, g):
    xf = x.astype(jnp.float32)
    y = xf * lax.rsqrt(jnp.mean(xf * xf, axis=-1, keepdims=True) + EPS)
    return (y * g.astype(jnp.float32)).astype(x.dtype)

def _past_pos(rows):
    return PAST_LEN - rows + jnp.arange(rows)

def _chunk_mask(q_pos, k_pos):
    return (k_pos[None, :] // CHUNK) <= (q_pos[:, None] // CHUNK)

def _sweep_queries(fn, q_pos, *qs):
    T = q_pos.shape[0]
    nb = T // Q_BLOCK
    to_blocks = lambda a: jnp.moveaxis(a.reshape((a.shape[0], nb, Q_BLOCK) + a.shape[2:]), 1, 0)
    out = lax.map(lambda args: fn(*args), (q_pos.reshape(nb, Q_BLOCK),) + tuple(to_blocks(a) for a in qs))
    out = jnp.moveaxis(out, 0, 1)
    return out.reshape((out.shape[0], T) + out.shape[3:])

def _rope(x, pos):
    d = x.shape[-1]
    half = d // 2
    inv = jnp.exp(-math.log(ROPE_BASE) * jnp.arange(half, dtype=jnp.float32) * 2.0 / d)
    ang = pos.astype(jnp.float32)[:, None] * inv[None, :]
    ang = ang.reshape((1, ang.shape[0]) + (1,) * (x.ndim - 3) + (half,))
    cos, sin = jnp.cos(ang), jnp.sin(ang)
    x1 = x[..., :half].astype(jnp.float32)
    x2 = x[..., half:].astype(jnp.float32)
    return jnp.concatenate([x1 * cos - x2 * sin, x2 * cos + x1 * sin], axis=-1).astype(x.dtype)

def _band_attend(q, k, v, q_pos, k_pos, rel_bias):
    s = jnp.einsum('bqhd,bkhd->bhqk', q, k, preferred_element_type=jnp.float32) * (A_HEAD_DIM ** -0.5)
    rel = jnp.clip(q_pos[:, None] - k_pos[None, :], -A_REL_CLIP, A_REL_CLIP) + A_REL_CLIP
    bias = jnp.moveaxis(rel_bias[rel], -1, 0).astype(jnp.float32)
    qc = q_pos[:, None] // CHUNK
    kc = k_pos[None, :] // CHUNK
    valid = (k_pos[None, :] >= 0) & (kc <= qc) & (kc >= qc - A_BAND_CHUNKS)
    p = jax.nn.softmax(jnp.where(valid, s + bias, NEG), axis=-1)
    return jnp.einsum('bhqk,bkhd->bqhd', p, v.astype(jnp.float32))

def _mixer_a(u, pos, rel_bias, past):
    B, T, _ = u.shape
    hd = A_HEADS * A_HEAD_DIM
    q, k, v = (u[..., n * hd:(n + 1) * hd].reshape(B, T, A_HEADS, A_HEAD_DIM) for n in range(3))
    if past is None:
        nc = T // CHUNK
        band = A_PAST_ROWS + CHUNK
        pad = ((0, 0), (A_PAST_ROWS, 0), (0, 0), (0, 0))
        kp, vp = jnp.pad(k, pad), jnp.pad(v, pad)
        qc = jnp.moveaxis(q.reshape(B, nc, CHUNK, A_HEADS, A_HEAD_DIM), 1, 0)

        def one_chunk(args):
            c, qb = args
            start = c * CHUNK
            kb = lax.dynamic_slice_in_dim(kp, start, band, axis=1)
            vb = lax.dynamic_slice_in_dim(vp, start, band, axis=1)
            q_pos = start + jnp.arange(CHUNK)
            k_pos = start - A_PAST_ROWS + jnp.arange(band)
            return _band_attend(qb, kb, vb, q_pos, k_pos, rel_bias)

        o = lax.map(one_chunk, (jnp.arange(nc), qc))
        o = jnp.moveaxis(o, 0, 1).reshape(B, T, hd)
        keep = min(A_PAST_ROWS, T)
        new = (k[:, T - keep:], v[:, T - keep:])
    else:
        ck, cv = past
        kk = jnp.concatenate([ck, k], axis=1)
        vv = jnp.concatenate([cv, v], axis=1)
        k_pos = jnp.concatenate([_past_pos(ck.shape[1]), pos])
        o = _band_attend(q, kk, vv, pos, k_pos, rel_bias).reshape(B, T, hd)
        new = (k, v)
    return o.astype(u.dtype), new

def _mixer_b(u, pos, lam_p, sub_g, lam_init, past):
    B, T, _ = u.shape
    qk_w = B_HEADS * 2 * B_HEAD_DIM
    q = u[..., :qk_w].reshape(B, T, B_HEADS, 2, B_HEAD_DIM)
    k = u[..., qk_w:2 * qk_w].reshape(B, T, B_HEADS, 2, B_HEAD_DIM)
    v = u[..., 2 * qk_w:].reshape(B, T, B_HEADS, B_V_DIM)
    lp = lam_p.astype(jnp.float32)
    lam = jnp.exp(jnp.sum(lp[0] * lp[1])) - jnp.exp(jnp.sum(lp[2] * lp[3])) + lam_init
    slopes = jnp.exp2(-8.0 * jnp.arange(1, B_HEADS + 1, dtype=jnp.float32) / B_HEADS)
    if past is None:
        kk, vv, k_pos = k, v, pos
    else:
        ck, cv = past
        kk = jnp.concatenate([ck, k], axis=1)
        vv = jnp.concatenate([cv, v], axis=1)
        k_pos = jnp.concatenate([_past_pos(ck.shape[1]), pos])

    def attend(q_pos, qb):
        s = jnp.einsum('bqhid,bkhid->bihqk', qb, kk, preferred_element_type=jnp.float32) * (B_HEAD_DIM ** -0.5)
        dist = jnp.abs(q_pos[:, None] - k_pos[None, :]).astype(jnp.float32)
        s = jnp.where(_chunk_mask(q_pos, k_pos), s - slopes[:, None, None] * dist[None], NEG)
        p = jax.nn.softmax(s, axis=-1)
        p_diff = p[:, 0] - lam * p[:, 1]
        return jnp.einsum('bhqk,bkhe->bqhe', p_diff, vv.astype(jnp.float32))

    o = _sweep_queries(attend, pos, q) if past is None else attend(pos, q)
    o = _rmsnorm(o, sub_g) * (1.0 - lam_init)
    return o.reshape(B, T, B_HEADS * B_V_DIM).astype(u.dtype), (k, v)

def _mixer_c(u, pos, q_norm_g, kv_norm_g, w_uq, w_ukv, past):
    B, T, _ = u.shape
    cq = u[..., :C_Q_LORA]
    ckv = u[..., C_Q_LORA:C_Q_LORA + C_KV_LORA]
    kr = u[..., C_Q_LORA + C_KV_LORA:C_Q_LORA + C_KV_LORA + C_ROPE]
    q = (_rmsnorm(cq, q_norm_g) @ w_uq).reshape(B, T, C_HEADS, C_NOPE + C_ROPE)
    q_nope, q_rope = q[..., :C_NOPE], _rope(q[..., C_NOPE:], pos)
    lat = _rmsnorm(ckv, kv_norm_g)
    kr = _rope(kr, pos)
    if past is None:
        lat_all, kr_all, k_pos = lat, kr, pos
    else:
        cl, cr = past
        lat_all = jnp.concatenate([cl, lat], axis=1)
        kr_all = jnp.concatenate([cr, kr], axis=1)
        k_pos = jnp.concatenate([_past_pos(cl.shape[1]), pos])
    kv = (lat_all @ w_ukv).reshape(B, lat_all.shape[1], C_HEADS, C_NOPE + C_V)
    k_nope, v = kv[..., :C_NOPE], kv[..., C_NOPE:]
    scale = (C_NOPE + C_ROPE) ** -0.5

    def attend(q_pos, qn, qr):
        s = (jnp.einsum('bqhd,bkhd->bhqk', qn, k_nope, preferred_element_type=jnp.float32)
             + jnp.einsum('bqhd,bkd->bhqk', qr, kr_all, preferred_element_type=jnp.float32)) * scale
        p = jax.nn.softmax(jnp.where(_chunk_mask(q_pos, k_pos), s, NEG), axis=-1)
        return jnp.einsum('bhqk,bkhd->bqhd', p, v.astype(jnp.float32))

    o = _sweep_queries(attend, pos, q_nope, q_rope) if past is None else attend(pos, q_nope, q_rope)
    return o.reshape(B, T, C_HEADS * C_V).astype(u.dtype), (lat, kr)

def _mem_attend(mq, mk, mv):
    s = jnp.einsum('bqhd,bmhd->bhqm', mq, mk, preferred_element_type=jnp.float32) * (MEM_HEAD_DIM ** -0.5)
    p = jax.nn.softmax(s, axis=-1)
    return jnp.einsum('bhqm,bmhd->bqhd', p, mv.astype(jnp.float32))

def _trunk(x, pos, mem_k, mem_v, past, norm_g, final_g, w_out, w_in_a, rel_bias_a, w_in_b, lambda_b,
           subln_g_b, w_in_c, q_norm_g_c, kv_norm_g_c, w_uq_c, w_ukv_c):
    new_a, new_b, new_c = [], [], []
    B, T, _ = x.shape
    for i in range(DEPTH):
        kind, j = i % N_MIXERS, i // N_MIXERS
        h = _rmsnorm(x, norm_g[i])
        u = h @ (w_in_a, w_in_b, w_in_c)[kind][j]
        n_mix = u.shape[-1] - MEM_W - GATE_W
        mix_u, mq, gate = u[..., :n_mix], u[..., n_mix:n_mix + MEM_W], u[..., n_mix + MEM_W:]
        if kind == 0:
            lp = None if past is None else (past[0][j], past[1][j])
            br, st = _mixer_a(mix_u, pos, rel_bias_a[j], lp)
            new_a.append(st)
        elif kind == 1:
            lp = None if past is None else (past[2][j], past[3][j])
            lam_init = 0.8 - 0.6 * math.exp(-0.3 * i)
            br, st = _mixer_b(mix_u, pos, lambda_b[j], subln_g_b[j], lam_init, lp)
            new_b.append(st)
        else:
            lp = None if past is None else (past[4][j], past[5][j])
            br, st = _mixer_c(mix_u, pos, q_norm_g_c[j], kv_norm_g_c[j], w_uq_c[j], w_ukv_c[j], lp)
            new_c.append(st)
        mo = _mem_attend(mq.reshape(B, T, MEM_HEADS, MEM_HEAD_DIM), mem_k[i], mem_v[i]).reshape(B, T, MEM_W)
        y = jnp.concatenate([br.astype(x.dtype), mo.astype(x.dtype)], axis=-1) * jax.nn.silu(gate)
        x = x + y @ w_out[i]
    return _rmsnorm(x, final_g), new_a, new_b, new_c

def setup_inputs(seed: int = 0) -> dict:
    key = jax.random.key(seed)
    ks = jax.random.split(key, 32)
    nrm = lambda k, shape, s: jax.random.normal(k, shape, jnp.float32) * s
    a_rows = min(A_PAST_ROWS, PAST_LEN)
    return {
        "x_prompt": nrm(ks[0], (BATCH, SEQ, D_MODEL), 1.0),
        "x_sample": nrm(ks[1], (DEC_BATCH, DEC_SEQ, D_MODEL), 1.0),
        "cache_a_k": nrm(ks[2], (N_A, DEC_BATCH, a_rows, A_HEADS, A_HEAD_DIM), 1.0),
        "cache_a_v": nrm(ks[3], (N_A, DEC_BATCH, a_rows, A_HEADS, A_HEAD_DIM), 1.0),
        "cache_b_k": nrm(ks[4], (N_B, DEC_BATCH, PAST_LEN, B_HEADS, 2, B_HEAD_DIM), 1.0),
        "cache_b_v": nrm(ks[5], (N_B, DEC_BATCH, PAST_LEN, B_HEADS, B_V_DIM), 1.0),
        "cache_c_lat": nrm(ks[6], (N_C, DEC_BATCH, PAST_LEN, C_KV_LORA), 1.0),
        "cache_c_rope": nrm(ks[7], (N_C, DEC_BATCH, PAST_LEN, C_ROPE), 1.0),
        "cache_mem_k": nrm(ks[8], (DEPTH, DEC_BATCH, MEM_TOKENS, MEM_HEADS, MEM_HEAD_DIM), 1.0),
        "cache_mem_v": nrm(ks[9], (DEPTH, DEC_BATCH, MEM_TOKENS, MEM_HEADS, MEM_HEAD_DIM), 1.0),
        "mem_prompt": nrm(ks[10], (BATCH, MEM_TOKENS, D_MODEL), 1.0),
        "norm_g": 1.0 + nrm(ks[11], (DEPTH, D_MODEL), 0.02),
        "final_g": 1.0 + nrm(ks[12], (D_MODEL,), 0.02),
        "mem_norm_g": 1.0 + nrm(ks[13], (DEPTH, D_MODEL), 0.02),
        "w_mem_kv": nrm(ks[14], (DEPTH, D_MODEL, 2 * MEM_W), D_MODEL ** -0.5),
        "w_out": nrm(ks[15], (DEPTH, MIX_W, D_MODEL), MIX_W ** -0.5),
        "w_in_a": nrm(ks[16], (N_A, D_MODEL, IN_A), D_MODEL ** -0.5),
        "rel_bias_a": nrm(ks[17], (N_A, 2 * A_REL_CLIP + 1, A_HEADS), 0.2),
        "w_in_b": nrm(ks[18], (N_B, D_MODEL, IN_B), D_MODEL ** -0.5),
        "lambda_b": nrm(ks[19], (N_B, 4, B_HEAD_DIM), 0.1),
        "subln_g_b": 1.0 + nrm(ks[20], (N_B, B_V_DIM), 0.02),
        "w_in_c": nrm(ks[21], (N_C, D_MODEL, IN_C), D_MODEL ** -0.5),
        "q_norm_g_c": 1.0 + nrm(ks[22], (N_C, C_Q_LORA), 0.02),
        "kv_norm_g_c": 1.0 + nrm(ks[23], (N_C, C_KV_LORA), 0.02),
        "w_uq_c": nrm(ks[24], (N_C, C_Q_LORA, C_HEADS * (C_NOPE + C_ROPE)), C_Q_LORA ** -0.5),
        "w_ukv_c": nrm(ks[25], (N_C, C_KV_LORA, C_HEADS * (C_NOPE + C_V)), C_KV_LORA ** -0.5),
    }

def reference(x_prompt, x_sample, cache_a_k, cache_a_v, cache_b_k, cache_b_v, cache_c_lat, cache_c_rope,
              cache_mem_k, cache_mem_v, mem_prompt, norm_g, final_g, mem_norm_g, w_mem_kv, w_out, w_in_a,
              rel_bias_a, w_in_b, lambda_b, subln_g_b, w_in_c, q_norm_g_c, kv_norm_g_c, w_uq_c, w_ukv_c):
    Bp = mem_prompt.shape[0]
    mem_k_p, mem_v_p = [], []
    for i in range(DEPTH):
        mkv = _rmsnorm(mem_prompt, mem_norm_g[i]) @ w_mem_kv[i]
        mem_k_p.append(mkv[..., :MEM_W].reshape(Bp, MEM_TOKENS, MEM_HEADS, MEM_HEAD_DIM))
        mem_v_p.append(mkv[..., MEM_W:].reshape(Bp, MEM_TOKENS, MEM_HEADS, MEM_HEAD_DIM))
    weights = (norm_g, final_g, w_out, w_in_a, rel_bias_a, w_in_b, lambda_b, subln_g_b,
               w_in_c, q_norm_g_c, kv_norm_g_c, w_uq_c, w_ukv_c)
    pos_p = jnp.arange(x_prompt.shape[1])
    y_prompt, na_p, nb_p, nc_p = _trunk(x_prompt, pos_p, mem_k_p, mem_v_p, None, *weights)
    pos_s = PAST_LEN + jnp.arange(x_sample.shape[1])
    past = (cache_a_k, cache_a_v, cache_b_k, cache_b_v, cache_c_lat, cache_c_rope)
    y_sample, na_s, nb_s, nc_s = _trunk(x_sample, pos_s, cache_mem_k, cache_mem_v, past, *weights)
    stk = lambda lst, n: jnp.stack([s[n] for s in lst])
    return (y_prompt, y_sample,
            stk(na_p, 0), stk(na_p, 1), stk(na_s, 0), stk(na_s, 1),
            stk(nb_p, 0), stk(nb_p, 1), stk(nb_s, 0), stk(nb_s, 1),
            stk(nc_p, 0), stk(nc_p, 1), stk(nc_s, 0), stk(nc_s, 1),
            jnp.stack(mem_k_p), jnp.stack(mem_v_p))


_drawn_inputs = setup_inputs


def setup_inputs(seed=0):
    import zlib

    import numpy as np

    out = dict(_drawn_inputs(seed))
    spreads = {}
    factors = {'cache_c_rope': 3.151,
     'final_g': 2.891,
     'mem_norm_g': 2.871,
     'rel_bias_a': 4.475,
     'subln_g_b': 8.0,
     'q_norm_g_c': 8.0,
     'kv_norm_g_c': 2.719}
    for name, (base, spread) in spreads.items():
        noise = np.random.default_rng([zlib.crc32(name.encode()), seed]).standard_normal(out[name].shape)
        drawn = base * np.exp(spread * noise) if base else spread * noise
        out[name] = __import__('jax').numpy.asarray(drawn.astype(out[name].dtype))
    for name, factor in factors.items():
        out[name] = (out[name] * factor).astype(out[name].dtype)
    return out
```

```python
import math
from contextlib import ExitStack

import numpy as np

import concourse.bass as bass
from concourse import mybir

F32 = mybir.dt.float32
F32R = mybir.dt.float32r
ALU = mybir.AluOpType
ACT = mybir.ActivationFunctionType

D = 1024
KT = D // 128
SEQ, DEC, PAST = 1024, 32, 512
TOK = SEQ + DEC
KEYS = TOK + PAST
MEMT = 256
CHUNK_TOK = TOK // 3
CHUNK_KEY = KEYS // 4
DEPTH, CHUNK = 4, 64
BAND = 640
EPS = 1e-6
NEG = -1e30
Q_LORA, KV_LORA, ROPE = 384, 256, 32
SCALE_64 = 64.0 ** -0.5
SCALE_C = 96.0 ** -0.5
KINDS = "ABCA"
LAM_INIT = 0.8 - 0.6 * math.exp(-0.3 * 1)
PASSES = ((0, 0), (0, 1), (1, 0))
G_NORM, G_FINAL, G_MEM, G_SUB, G_Q, G_KV = 0, 32, 40, 72, 73, 76
N_GAINS = 78


class Step:

    def __init__(self, head, tile, which, q0, rows, segs, bias0):
        self.head, self.tile, self.which = head, tile, which
        self.q0, self.rows, self.segs, self.bias0 = q0, rows, segs, bias0
        self.width = segs[-1][1] + segs[-1][2]


class Group:

    def __init__(self, head, parity, steps, chunks, q0, qn):
        self.head, self.parity, self.steps = head, parity, steps
        self.chunks, self.q0, self.qn = chunks, q0, qn


def key_segments(first, count):
    return [(first + a, a, min(512, count - a)) for a in range(0, count, 512)]


def groups_of(kind):
    out = []
    for head in range(1 if kind == "B" else 2):
        for n, g in enumerate([0, 1, 2, 3, 4] if head == 0 else [1, 0, 3, 2, 4]):
            parity = (5 * head + n) % 2
            whiches = (0, 1) if kind == "B" else (0,)
            if g == 4:
                if kind == "M":
                    segs, keys = [(MEMT, 0, MEMT)], [(2, 128), (3, 128)]
                else:
                    segs = [(TOK, 0, PAST), (SEQ, PAST, DEC)]
                    keys = [(8 + i, 128) for i in range(4)] + [(12, DEC)]
                bias0 = {"A": 0, "B": 384, "C": 0, "M": 0}[kind]
                steps = [Step(head, 0, w, SEQ, DEC, segs, bias0) for w in whiches]
                chunks = [[(i, vt, n_k, (i * 128,)) for i, (vt, n_k) in enumerate(keys)]]
                out.append(Group(head, parity, steps, chunks, SEQ, DEC))
                continue
            steps, starts = [], []
            for i in range(2):
                t = 2 * g + i
                if kind == "M":
                    k0, count, bias0 = 0, MEMT, 0
                elif kind == "A":
                    k0 = max(0, t - 4)
                    count, bias0 = (t + 1 - k0) * 128, 128 * (4 - min(t, 4))
                else:
                    k0, count, bias0 = 0, (t + 1) * 128, 128 * (7 - t)
                starts.append((k0, k0 + count // 128))
                steps += [Step(head, i, w, 128 * t, 128, key_segments(128 * k0, count), bias0)
                          for w in whiches]
            tiles = [(vt, tuple((vt - a) * 128 if a <= vt < b else None for a, b in starts))
                     for vt in range(starts[0][0], starts[1][1])]
            chunks = []
            for c in range(0, len(tiles), 2):
                chunk = [(i, vt, 128, cols) for i, (vt, cols) in enumerate(tiles[c:c + 2])]
                chunks.append(sorted(chunk, key=lambda x: None in x[3]))
            out.append(Group(head, parity, steps, chunks, 256 * g, 256))
    return out


GROUPS = {k: groups_of(k) for k in "ABCM"}
V_CHUNKS = {
    "A": [[(4 * c + i, 512 * c + 128 * i, 128) for i in range(4)] for c in range(2)] + [[(12, SEQ, DEC)]],
    "M": [[(i, 128 * i, 128) for i in range(4)]],
}
V_CHUNKS["B"] = V_CHUNKS["A"]
V_CHUNKS["C"] = V_CHUNKS["A"] + [[(8 + i, TOK + 128 * i, 128) for i in range(4)]]


def rectangles(group, chunk):
    if group.qn == DEC:
        full = [x for x in chunk if x[2] == 128]
        rest = [x for x in chunk if x[2] != 128]
        return [(128, 0, DEC * len(full))] + [(n, DEC * i, DEC) for i, _, n, _ in rest]
    found = []
    for i, _, _, cols in sorted(chunk):
        for t in range(2):
            at = 256 * i + 128 * t
            if cols[t] is None:
                continue
            if found and found[-1][1] + found[-1][2] == at:
                found[-1] = (128, found[-1][1], found[-1][2] + 128)
            else:
                found.append((128, at, 128))
    return found


def token_chunks(total, size):
    return [(a, min(size, total - a)) for a in range(0, total, size)]


JOB_PROJ = {
    "A": [(KT, token_chunks(TOK, CHUNK_TOK))] * 3,
    "M": [(KT, token_chunks(TOK, CHUNK_TOK))],
    "C": [(3, token_chunks(TOK, CHUNK_TOK))] * 2 + [(2, token_chunks(KEYS, CHUNK_KEY))] * 2,
}
JOB_PROJ["B"] = JOB_PROJ["A"]
SIDE_PROJ = {"A": [], "B": [], "C": [], "M": [(KT, token_chunks(TOK, CHUNK_TOK))] * 3}
N_SPLITS = {"A": 3, "B": 3, "C": 4, "M": 2}


def side_chunks(kind, h):
    listed = [(t, c) for t, (_, chunks) in enumerate(SIDE_PROJ[kind]) for c in range(len(chunks))]
    n = len(GROUPS[kind])
    first, last = -(-len(listed) * h // n), -(-len(listed) * (h + 1) // n)
    return [(t, c, first + i) for i, (t, c) in enumerate(listed[first:last])]


def output_bank(kind, h):
    return 0 if SIDE_PROJ[kind] else h % 2


def job_counts(kind):
    groups = GROUPS[kind]
    proj = sum(len(c) for _, c in JOB_PROJ[kind])
    att = sum(len(g.chunks) for g in groups)
    v = len(V_CHUNKS[kind])
    steps = sum(len(g.steps) for g in groups)
    proj += sum(len(c) for _, c in SIDE_PROJ[kind])
    c = dict(w=len(JOB_PROJ[kind]) + len(SIDE_PROJ[kind]), acc_ready=proj, acc_read_act=proj,
             acc_read_dve=len(groups), opnd_hi_made=N_SPLITS[kind],
             opnd_lo_made=N_SPLITS[kind], turned_ready=v + att, turned_hi_made=v + att, turned_lo_made=v + att, pv_done=att,
             scores_ready=steps, scores_biased=steps, exps_ready=steps, recips_ready=steps,
             probs_ready=sum(1 + (g.qn > DEC) for g in groups))
    if kind in "AB":
        c.update(kcache_loaded=16, vcache_loaded=16, bias_loaded=16, bias_masked=1, k_stored=16, v_stored=16)
    if kind == "M":
        c.update(kcache_loaded=32, vcache_loaded=32)
    if kind == "B":
        c.update(acc_read_act=proj + 3, acc_read_dve=len(groups) + 1, squares_ready=1, squares_summed=1, rstd_ready=1, recips_ready=steps + 1,
                 lambda_recips_ready=steps // 2)
    if kind == "C":
        c.update(recips_ready=steps + 4)
    return c


def encoder(nc, x_in, mem_in, w8, wc_q, wc_kv, gains_in, lambda_in, rel_in, kcache, vcache, lat_cache,
            rope_cache, memk_cache, memv_cache, ident_in, dist_in, cmask_in, rope_in, slope_in,
            y_out, k_a, v_a, k_b, v_b, lat_out, rope_out, memkv_out, x_scr, rel_scr):
    ctx = ExitStack()
    place = [-(-nc.sbuf_base // 64) * 64]

    def sbuf(name, free, dtype=F32, at=None):
        size = 4 * int(np.prod(free))
        where = place[0] if at is None else at
        if at is None:
            place[0] += -(-size // 32) * 32
        return nc.alloc_sbuf_tensor_at(name, [128, *free], dtype, offset=where)

    h_flat = sbuf("h_split", [2 * KT * TOK], F32R)
    y_sb = sbuf("y_sb", [KT, TOK])
    w_raw = sbuf("w_raw", [2, KT * 128])
    w_hi = sbuf("w_hi", [2, KT * 128], F32R)
    w_lo = sbuf("w_lo", [2, KT * 128], F32R)
    qkv_at = place[0]
    q_sp = sbuf("q_split", [2, TOK], F32R)
    k_sp = sbuf("k_split", [2, KEYS], F32R)
    v_sp = sbuf("v_split", [2, 13, 128], F32R)
    c_tmp = sbuf("c_latents", [6, TOK], F32, at=qkv_at)
    c_cache = sbuf("c_cache", [2, PAST], F32, at=qkv_at + 4 * 6 * TOK)
    raw = [sbuf("raw0", [KEYS]), sbuf("raw1", [KEYS])]
    v_cache = sbuf("v_cache", [4, 128])
    prob = sbuf("prob", [5632])
    qo_sp = sbuf("q_odd_split", [2, TOK], F32R)
    rope_sb = sbuf("rope_sb", [TOK])
    pt = sbuf("pt_split", [2, 2, 512], F32R)
    bias = sbuf("bias", [2 * BAND])
    ident = sbuf("ident", [128])
    ones = sbuf("ones", [128])
    gains = sbuf("gains", [N_GAINS])
    slopes = sbuf("slopes", [6])
    lam = sbuf("lam", [256])
    stat = sbuf("stat", [32])
    small = sbuf("small", [8])
    assert place[0] <= nc.sbuf_usable_end, place[0]
    neg_lam, eps_sb, sub_gain = small[:, 0:1], small[:, 1:2], small[:, 2:3]

    h_v = h_flat[:, :].rearrange("p (s k t) -> p s k t", s=2, k=KT)
    memh_v = h_flat[:, :].rearrange("p (s f) -> p s f", s=2)
    lat_v = h_flat[:, 0:4 * KEYS].rearrange("p (s k t) -> p s k t", s=2, k=2)
    cq_at = 4 * KEYS
    cq_v = h_flat[:, cq_at:cq_at + 6 * TOK].rearrange("p (s k t) -> p s k t", s=2, k=3)
    ko_at = cq_at + 6 * TOK
    ko_v = h_flat[:, ko_at:ko_at + 2 * KEYS].rearrange("p (s t) -> p s t", s=2)
    y_flat = y_sb[:, :, :].rearrange("p k t -> p (k t)")
    mem_x = y_flat[:, 0:KT * MEMT].rearrange("p (k t) -> p k t", k=KT)
    mem_kv = y_flat[:, KT * MEMT:KT * MEMT + 16 * MEMT].rearrange("p (n t) -> p n t", n=16)
    rstd = prob[:, 0:TOK]

    s_ps = [ctx.enter_context(nc.psum_tensor(f"scores{i}", [128, 1024], F32)) for i in range(2)]
    t_ps = [ctx.enter_context(nc.psum_tensor(f"turned{i}", [128, 512], F32)) for i in range(2)]
    acc = [ctx.enter_context(nc.psum_tensor(f"acc{i}", [128, 512], F32)) for i in range(2)]
    sum_banks = [acc[0], acc[1], t_ps[0]]

    def sem(name):
        return ctx.enter_context(nc.semaphore(name))

    consts_loaded = sem("consts_loaded")
    consts_set = sem("consts_set")
    w_loaded = [sem(f"w_loaded{i}") for i in range(2)]
    whi_made, wlo_made = sem("whi_made"), sem("wlo_made")
    acc_ready = sem("acc_ready")
    acc_read_act = sem("acc_read_act")
    acc_read_dve = sem("acc_read_dve")
    opnd_hi_made = sem("opnd_hi_made")
    opnd_lo_made = sem("opnd_lo_made")
    turned_ready = sem("turned_ready")
    turned_hi_made = sem("turned_hi_made")
    turned_lo_made = sem("turned_lo_made")
    pv_done = sem("pv_done")
    gates_ready = sem("gates_ready")
    scores_ready = sem("scores_ready")
    scores_biased = sem("scores_biased")
    exps_ready = sem("exps_ready")
    probs_ready = sem("probs_ready")
    recips_ready = sem("recips_ready")
    lambda_recips_ready = sem("lambda_recips_ready")
    kcache_loaded = sem("kcache_loaded")
    vcache_loaded = sem("vcache_loaded")
    bias_loaded = sem("bias_loaded")
    bias_masked = sem("bias_masked")
    k_stored, v_stored = sem("k_stored"), sem("v_stored")
    squares_ready = sem("squares_ready")
    squares_summed = sem("squares_summed")
    rstd_ready = sem("rstd_ready")
    normed = sem("normed")
    normed_hi, normed_lo = sem("normed_hi"), sem("normed_lo")
    normed_stored = [sem(f"normed_stored{i}") for i in range(2)]
    x_loaded = sem("x_loaded")
    x_stored = sem("x_stored")
    memkv_stored = sem("memkv_stored")
    rel_stored = sem("rel_stored")
    settled = sem("settled")
    xt_in = [sem(f"xt_in{f}") for f in range(KT)]
    block = ctx.enter_context(nc.Block())

    def settle(eng):
        eng.sem_inc(settled, 1)

    def advance(m, counts, times=1):
        for k, v in counts.items():
            m[k] = m[k] + v * times

    def at_iteration(m, counts, it):
        return {k: (v + it * counts[k] if counts.get(k) else v) for k, v in m.items()}

    def norm_counts(tiles, chunks, steps, split=True, store=False):
        c = dict(squares_ready=tiles, squares_summed=tiles, acc_read_act=chunks, rstd_ready=1, normed=steps)
        if split:
            c.update(normed_hi=steps, normed_lo=steps)
        if store:
            c.update(normed_stored0=8 * steps, normed_stored1=8 * steps)
        return c

    MEM_PROJ = dict(w=16, acc_ready=16, acc_read_act=16, memkv_stored=16)
    GATE = dict(w=2, acc_ready=6, acc_read_act=6)
    LATENTS = dict(w=6, acc_ready=18, acc_read_act=18, kcache_loaded=32, bias_loaded=16, opnd_hi_made=1, opnd_lo_made=1)
    KEY_ROPE = dict(recips_ready=2, k_stored=16, opnd_hi_made=4)
    OUT = dict(w=8, acc_ready=24, acc_read_dve=24, normed_hi=8, normed=8, x_stored=16 * 8)

    def double(c):
        return {k: 2 * v for k, v in c.items()}

    COUNTED = (
        "w", "acc_ready", "acc_read_act", "acc_read_dve", "opnd_hi_made", "opnd_lo_made", "turned_ready",
        "turned_hi_made", "turned_lo_made", "pv_done", "scores_ready", "scores_biased", "exps_ready",
        "probs_ready", "recips_ready", "lambda_recips_ready", "kcache_loaded", "vcache_loaded",
        "bias_loaded", "bias_masked", "k_stored", "v_stored", "squares_ready", "squares_summed",
        "rstd_ready", "normed", "normed_hi", "normed_lo", "normed_stored0", "normed_stored1",
        "x_loaded", "x_stored", "memkv_stored", "gates_ready")

    def fresh():
        m = {k: 0 for k in COUNTED}
        m["x_loaded"] = 16
        return m

    def course(m):
        w8_at = 0

        def give(name, counts, times=1, **more):
            start = dict(m)
            advance(m, counts, times)
            return name, start, dict(counts=counts, **more)

        yield give("norm", norm_counts(KT, 1, 4 * KT), what="mem")
        yield give("mem", MEM_PROJ, w8=w8_at)
        w8_at += 16
        yield give("load_x", dict(x_loaded=16))
        yield give("norm", norm_counts(KT, 3, KT), what="h", layer=0)
        for layer, kind in enumerate(KINDS):
            yield give("gate", GATE, w8=w8_at, layer=layer)
            yield give("memory_jobs", {**double(job_counts("M")), "bias_loaded": 16, "gates_ready": 6},
                       w8=w8_at + 2, layer=layer, last=kind)
            w8_at += 10
            if kind == "C":
                yield give("latents", LATENTS, w8=w8_at)
                w8_at += 6
                yield give("norm", norm_counts(3, 3, 3), what="cq")
                yield give("norm", norm_counts(2, 3, 2, store=True), what="lat")
                yield give("key_rope", KEY_ROPE)
            yield give("jobs", double(job_counts(kind)), 3, kind=kind, w8=w8_at, layer=layer)
            w8_at += 0 if kind == "C" else 18
            counts = dict(OUT)
            if layer == DEPTH - 1:
                counts.pop("x_stored")
            yield give("out", counts, w8=w8_at, layer=layer)
            w8_at += 8
            if layer < DEPTH - 1:
                yield give("norm", norm_counts(KT, 3, KT), what="h", layer=layer + 1)
        yield give("norm", norm_counts(KT, 3, KT, split=False, store=True), what="final")

    final_counts = fresh()
    COURSE = list(course(final_counts))
    LAST_W8 = w8.shape[0]

    def phases():
        return COURSE

    def norm_plan(what, layer=0):
        if what == "mem":
            steps = [(mem_x[:, k, :], G_MEM + 8 * i + k,
                      memh_v[:, 0, (8 * i + k) * MEMT:(8 * i + k + 1) * MEMT],
                      memh_v[:, 1, (8 * i + k) * MEMT:(8 * i + k + 1) * MEMT], None)
                     for i in range(DEPTH) for k in range(KT)]
            return [mem_x[:, k, :] for k in range(KT)], D, [(0, MEMT)], steps
        tok = token_chunks(TOK, CHUNK_TOK)
        if what == "h":
            return ([y_sb[:, k, :] for k in range(KT)], D, tok,
                    [(y_sb[:, k, :], G_NORM + 8 * layer + k, h_v[:, 0, k, :], h_v[:, 1, k, :], None)
                     for k in range(KT)])
        if what == "final":
            return ([y_sb[:, k, :] for k in range(KT)], D, tok,
                    [(y_sb[:, k, :], G_FINAL + k, None, None, y_out[k * 128:(k + 1) * 128, :])
                     for k in range(KT)])
        if what == "cq":
            return ([c_tmp[:, k, :] for k in range(3)], Q_LORA, tok,
                    [(c_tmp[:, k, :], G_Q + k, cq_v[:, 0, k, :], cq_v[:, 1, k, :], None) for k in range(3)])
        return ([c_tmp[:, 3 + k, :] for k in range(2)], KV_LORA, tok,
                [(c_tmp[:, 3 + k, :], G_KV + k, lat_v[:, 0, k, 0:TOK], lat_v[:, 1, k, 0:TOK],
                  lat_out[k * 128:(k + 1) * 128, :]) for k in range(2)])

    def prob_at(group, step):
        if step.which:
            at = 3584 + 1024 * step.tile
        else:
            at = (768 if group.parity == 0 else 1024) * step.tile + 1536 * group.parity
        return at

    @block.sync
    def _(sp):
        for dst, src in ((ident[:, :], ident_in), (gains[:, :], gains_in), (slopes[:, :], slope_in),
                         (lam[:, :], lambda_in.partition_broadcast(128)), (rope_sb[:, :], rope_in)):
            sp.dma_start(dst, src).then_inc(consts_loaded, 16)
        sp.dma_start(mem_x, mem_in).then_inc(x_loaded, 16)
        toeplitz = bass.AP(rel_in.tensor, 127, [[768, 24], [-1, 128], [1, BAND]])
        sp.dma_start(rel_scr.rearrange("g h p k -> (g h) p k"), toeplitz).then_inc(rel_stored, 16)

        def weight(n, r, src, width):
            sp.wait_ge(wlo_made, n + r - 1)
            sp.dma_start(w_raw[:, r % 2, 0:width], src).then_inc(w_loaded[r % 2], 16)

        def w8_tile(index):
            return w8[index].rearrange("(o p) f -> (o p) f", o=1)

        def first_gates(w, index):
            for r in range(2):
                weight(w, r, w8[index + r], KT * 128)

        for name, m, o in phases():
            if name == "norm" and o["what"] in ("lat", "final"):
                _, _, _, steps = norm_plan(o["what"])
                for n, step in enumerate(steps):
                    sp.wait_ge(normed, m["normed"] + n + 1)
                    sp.dma_start(step[4], raw[n % 2][:, 0:TOK]).then_inc(normed_stored[n % 2], 16)
            elif name == "mem":
                def body(it):
                    for r in range(2):
                        weight(m["w"] + 2 * it, r, w8[o["w8"] + 2 * it + r], KT * 128)
                for n in range(2):
                    sp.dma_start(w_raw[:, n, :], w8[o["w8"] + n]).then_inc(w_loaded[n], 16)
                with sp.Fori(1, 8) as it:
                    body(it)
                first_gates(m["w"] + 16, o["w8"] + 16)
                sp.wait_ge(acc_read_act, m["acc_read_act"] + 16)
                sp.dma_start(memkv_out, mem_kv).then_inc(memkv_stored, 16)
            elif name == "load_x":
                sp.wait_ge(normed_lo, m["normed_lo"])
                sp.wait_ge(memkv_stored, m["memkv_stored"])
                sp.dma_start(y_sb[:, :, :], x_in).then_inc(x_loaded, 16)
            elif name == "memory_jobs":
                for r in range(2):
                    weight(m["w"], r, w8[o["w8"] + r], KT * 128)
                sp.wait_ge(acc_read_dve, m["acc_read_dve"])
                sp.dma_start(bias[:, 0:MEMT], cmask_in[:, 0:MEMT]).then_inc(bias_loaded, 16)
                sp.wait_ge(normed_lo, m["normed_lo"])
                layer = o["layer"]
                per = job_counts("M")
                for j in range(2):
                    mj = at_iteration(m, per, j)
                    sp.wait_ge(opnd_lo_made, mj["opnd_lo_made"])
                    sp.dma_start(raw[1][:, 0:MEMT], memkv_out[:, 4 * layer + j, :]).then_inc(kcache_loaded, 16)
                    sp.dma_start(raw[1][:, MEMT:2 * MEMT], memk_cache[layer, j]).then_inc(kcache_loaded, 16)
                    sp.wait_ge(opnd_lo_made, mj["opnd_lo_made"] + 1)
                    sp.dma_start(raw[0][:, 0:MEMT], memkv_out[:, 4 * layer + 2 + j, :]).then_inc(vcache_loaded, 16)
                    sp.dma_start(raw[0][:, MEMT:2 * MEMT], memv_cache[layer, j]).then_inc(vcache_loaded, 16)
                    for r in range(4 * j + 2, min(4 * j + 6, 8)):
                        weight(m["w"], r, w8[o["w8"] + r], KT * 128)
            elif name == "latents":
                for r in range(2):
                    weight(m["w"], r, w8[o["w8"] + r], KT * 128)
                sp.wait_ge(opnd_lo_made, m["opnd_lo_made"])
                sp.wait_ge(acc_read_dve, m["acc_read_dve"])
                sp.dma_start(c_cache[:, :, :], lat_cache).then_inc(kcache_loaded, 16)
                sp.dma_start(raw[1][64:96, TOK:KEYS], rope_cache).then_inc(kcache_loaded, 16)
                sp.dma_start(bias[:, 0:1024], cmask_in).then_inc(bias_loaded, 16)
                for r in range(2, 6):
                    weight(m["w"], r, w8[o["w8"] + r], KT * 128)
            elif name == "key_rope":
                sp.wait_ge(recips_ready, m["recips_ready"] + 2)
                sp.dma_start(rope_out, raw[1][64:96, 0:TOK]).then_inc(k_stored, 16)
            elif name == "jobs":
                kind, layer = o["kind"], o["layer"]
                per = job_counts(kind)
                sp.wait_ge(rel_stored, 16)
                with sp.Fori(0, 3) as it:
                    for u in range(2):
                        pair = 2 * it + u
                        mu = at_iteration(at_iteration(m, o["counts"], it), per, u)
                        base = m["w"] + 2 * len(JOB_PROJ[kind]) * it
                        if kind == "C":
                            for i, (src, width) in enumerate(((wc_q[2 * pair], 384), (wc_q[2 * pair + 1], 384),
                                                              (wc_kv[2 * pair], 256), (wc_kv[2 * pair + 1], 256))):
                                weight(base, 4 * u + i, src, width)
                            continue
                        for i in range(3):
                            weight(base, 3 * u + i, w8[o["w8"] + 3 * pair + i], KT * 128)
                        slot = {0: 0, 1: 1, 3: 2}[layer]
                        sp.wait_ge(opnd_lo_made, mu["opnd_lo_made"])
                        sp.dma_start(raw[1][:, TOK:KEYS], kcache[6 * slot + pair]).then_inc(kcache_loaded, 16)
                        sp.dma_start(v_cache[:, :, :], vcache[6 * slot + pair]).then_inc(vcache_loaded, 16)
                        sp.wait_ge(acc_read_dve, mu["acc_read_dve"])
                        if kind == "A":
                            sp.dma_start(bias[:, :].rearrange("p (h k) -> p h k", h=2),
                                         rel_scr[6 * (layer // 3) + pair].rearrange("h p k -> p h k")).then_inc(bias_loaded, 16)
                            k_dst = k_a[layer // 3, pair]
                            v_dst = v_a[layer // 3, pair]
                            first = PAST
                        else:
                            sp.dma_start(bias[:, 0:1024], dist_in).then_inc(bias_loaded, 16)
                            k_dst, v_dst, first = k_b[pair], v_b[pair], 0
                        sp.wait_ge(acc_read_act, mu["acc_read_act"] + 6)
                        sp.dma_start(k_dst, raw[1][:, first:TOK]).then_inc(k_stored, 16)
                        sp.wait_ge(acc_read_act, mu["acc_read_act"] + 9)
                        sp.dma_start(v_dst, raw[0][:, first:TOK]).then_inc(v_stored, 16)
            elif name == "out":
                layer = o["layer"]
                for r in range(2):
                    weight(m["w"], r, w8[o["w8"] + r], KT * 128)
                src = x_in if layer == 0 else x_scr[layer - 1]
                sp.wait_ge(x_stored, m["x_stored"])
                for f in range(KT):
                    sp.wait_ge(normed, m["normed"] + f + 1)
                    sp.dma_start(y_sb[:, f, :], src[:, f, :]).then_inc(xt_in[f], 16)

                def store(f):
                    if layer < DEPTH - 1:
                        sp.wait_ge(acc_read_dve, m["acc_read_dve"] + 3 * (f + 1))
                        sp.dma_start(x_scr[layer][:, f, :], y_sb[:, f, :]).then_inc(x_stored, 16)
                for f in range(KT):
                    if f + 2 < KT:
                        weight(m["w"], f + 2, w8[o["w8"] + f + 2], KT * 128)
                    if f + 2 == KT and layer < DEPTH - 1:
                        first_gates(m["w"] + KT, o["w8"] + KT)
                    store(f)
        sp.wait_ge(normed_stored[0], final_counts["normed_stored0"])
        sp.wait_ge(normed_stored[1], final_counts["normed_stored1"])
        sp.wait_ge(k_stored, final_counts["k_stored"])
        sp.wait_ge(v_stored, final_counts["v_stored"])
        sp.wait_ge(memkv_stored, final_counts["memkv_stored"])
        sp.wait_ge(x_stored, final_counts["x_stored"])

    @block.scalar
    def _(act):
        def split_weight(m, r, wide, end):
            w = m["w"]
            act.wait_ge(w_loaded[r % 2], 8 * w + 16 * (r // 2 + 1))
            act.wait_ge(acc_ready, m["acc_ready"] + end)
            act.activation(w_hi[:, r % 2, 0:wide], w_raw[:, r % 2, 0:wide], ACT.Copy).then_inc(whi_made, 1)

        def norm(m, what, layer=0):
            tiles, width, chunks, steps = norm_plan(what, layer)
            act.wait_ge(x_loaded, m["x_loaded"])
            act.wait_ge(acc_read_dve, m["acc_read_dve"])
            act.wait_ge(acc_read_act, m["acc_read_act"])
            act.wait_ge(k_stored, m["k_stored"])
            act.wait_ge(v_stored, m["v_stored"])
            act.wait_ge(normed_lo, m["normed_lo"])
            act.wait_ge(normed_stored[0], m["normed_stored0"])
            act.wait_ge(normed_stored[1], m["normed_stored1"])
            for k, tile in enumerate(tiles):
                if k >= 2:
                    act.wait_ge(squares_summed, m["squares_summed"] + k - 1)
                n = sum(c for _, c in chunks)
                act.activation(raw[k % 2][:, 0:n], tile, ACT.Square).then_inc(squares_ready, 1)
            act.wait_ge(squares_summed, m["squares_summed"] + len(tiles))
            root(m, chunks, width, len(tiles))
            for n, step in enumerate(steps):
                if step[2] is not None:
                    act.wait_ge(normed, m["normed"] + n + 1)
                    act.activation(step[2], raw[n % 2][:, 0:step[0].shape[-1]], ACT.Copy).then_inc(normed_hi, 1)

        def root(m, chunks, width, used, first=0):
            for c, (a, n) in enumerate(chunks):
                act.activation(rstd[:, a:a + n], sum_banks[c][:, 0:n], ACT.Ln, scale=1.0 / width,
                               bias=eps_sb).then_inc(acc_read_act, 1)
            n = sum(c for _, c in chunks)
            act.wait_ge(acc_read_act, m["acc_read_act"] + first + len(chunks))
            act.activation(rstd[:, 0:n], rstd[:, 0:n], ACT.Exp, scale=-0.5).then_inc(rstd_ready, 1)

        def job(m, kind, r0, it, next_wide, side_out=None):
            groups, proj, side = GROUPS[kind], JOB_PROJ[kind], SIDE_PROJ[kind]
            act.wait_ge(acc_read_dve, m["acc_read_dve"])
            act.wait_ge(k_stored, m["k_stored"])
            act.wait_ge(v_stored, m["v_stored"])
            wm = dict(m, w=it["w"])
            ends = [0]
            for _, chunks in proj:
                ends.append(ends[-1] + len(chunks))
            if kind == "C":
                split_weight(wm, r0, 384, 0)
            done = 0
            for j, (kt, chunks) in enumerate(proj):
                if j + 1 < len(proj):
                    split_weight(wm, r0 + j + 1, 128 * proj[j + 1][0], ends[j])
                elif side:
                    split_weight(wm, r0 + j + 1, 128 * side[0][0], ends[j])
                for c, (a, n) in enumerate(chunks):
                    act.wait_ge(acc_ready, m["acc_ready"] + done + 1)
                    src = acc[done % 2]
                    if kind in "AB" and c == 0 and j == 2:
                        act.wait_ge(opnd_lo_made, m["opnd_lo_made"] + 1)
                    if kind == "C" and c == 0 and j == 1:
                        act.wait_ge(opnd_lo_made, m["opnd_lo_made"] + 1)
                    if kind == "C" and c == 0 and j == 2:
                        act.wait_ge(opnd_lo_made, m["opnd_lo_made"] + 2)
                    if kind == "C" and c == 0 and j == 3:
                        act.wait_ge(opnd_lo_made, m["opnd_lo_made"] + 4)
                    done += 1
                    q_scale = SCALE_C if kind == "C" else SCALE_64
                    if j == 0 or (kind == "C" and j == 1):
                        act.activation(raw[0][:, a:a + n], src[:, 0:n], ACT.Copy, scale=q_scale).then_inc(acc_read_act, 1)
                    elif kind == "C" and j == 2:
                        act.activation(raw[1][0:64, a:a + n], src[0:64, 0:n], ACT.Copy)
                        act.activation(raw[0][0:64, a:a + n], src[64:128, 0:n], ACT.Copy).then_inc(acc_read_act, 1)
                    else:
                        dst = raw[1] if j == 1 else raw[0]
                        act.activation(dst[:, a:a + n], src[:, 0:n], ACT.Copy).then_inc(acc_read_act, 1)
            for v, chunk in enumerate(V_CHUNKS[kind]):
                act.wait_ge(turned_ready, m["turned_ready"] + v + 1)
                rows, n = chunk[0][2], len(chunk)
                act.activation(v_sp[0:rows, 0, chunk[0][0]:chunk[0][0] + n, :],
                               t_ps[v % 2][0:rows, 0:128 * n].rearrange("p (n d) -> p n d", d=128),
                               ACT.Copy).then_inc(turned_hi_made, 1)
            nv = len(V_CHUNKS[kind])
            s = 0
            a_i = 0

            def exponentials(steps, g):
                nonlocal s
                for step in steps:
                    act.wait_ge(scores_biased, m["scores_biased"] + s + 1)
                    at = prob_at(g, step)
                    p = prob[0:step.rows, at:at + step.width]
                    act.activation(p, p, ACT.Exp, scale=-1.0, bias=stat[0:step.rows, s % 8:s % 8 + 1],
                                   accum_out=stat[0:step.rows, 8 + s % 8:9 + s % 8]).then_inc(exps_ready, 1)
                    s += 1

            exponentials(groups[0].steps, groups[0])
            if side:
                split_weight(wm, r0 + len(proj) + 1, 128 * side[1][0], done)
            for h, g in enumerate(groups):
                for c, chunk in enumerate(g.chunks):
                    act.wait_ge(turned_ready, m["turned_ready"] + nv + a_i + 1)
                    act.wait_ge(pv_done, m["pv_done"] + max(a_i - 1, 0))
                    rects = rectangles(g, chunk)
                    for i, (rows, c0, n) in enumerate(rects):
                        ins = act.activation(pt[0:rows, a_i % 2, 0, c0:c0 + n],
                                             t_ps[(nv + a_i) % 2][0:rows, c0:c0 + n], ACT.Copy)
                    ins.then_inc(turned_hi_made, 1)
                    a_i += 1
                    if h + 1 < len(groups):
                        half = len(groups[h + 1].steps) // 2
                        if c == 0:
                            exponentials(groups[h + 1].steps[:half], groups[h + 1])
                        if c == min(1, len(g.chunks) - 1):
                            exponentials(groups[h + 1].steps[half:], groups[h + 1])
                for t, c, i in side_chunks(kind, h):
                    act.wait_ge(acc_ready, m["acc_ready"] + done + i + 1)
                    a, n = side[t][1][c]
                    act.activation(side_out(t, a, n), acc[1][:, 0:n], ACT.Copy).then_inc(acc_read_act, 1)
                    if c == len(side[t][1]) - 1 and t + 1 < len(side):
                        wide = 128 * side[t + 2][0] if t + 2 < len(side) else next_wide
                        split_weight(wm, r0 + len(proj) + t + 2, wide, done + i + 1)
                if h == 1 and next_wide and not side:
                    split_weight(wm, r0 + len(proj), next_wide, ends[-2])
            if kind == "B":
                act.wait_ge(acc_read_dve, m["acc_read_dve"] + len(groups))
                act.wait_ge(k_stored, m["k_stored"] + 16)
                act.activation(raw[1][:, 0:TOK], raw[0][:, 0:TOK], ACT.Square).then_inc(squares_ready, 1)
                act.wait_ge(squares_summed, m["squares_summed"] + 1)
                root(m, token_chunks(TOK, CHUNK_TOK), 128, 1, first=done)

        act.wait_ge(consts_set, 3)
        act.activation(small[:, 5:7], small[:, 3:5], ACT.Exp).then_inc(consts_set, 1)
        split_weight(fresh(), 0, KT * 128, 0)
        for name, m, o in phases():
            if name == "norm":
                norm(m, o["what"], o.get("layer", 0))
            elif name == "mem":
                def pair_of(mi, first=0):
                    for r in range(2):
                        split_weight(dict(mi), r + 1, KT * 128, r)
                        act.wait_ge(acc_ready, mi["acc_ready"] + r + 1)
                        yield r
                per = dict(w=2, acc_ready=2, acc_read_act=2)
                with act.Fori(0, 8) as it:
                    mi = at_iteration(m, per, it)
                    for r in pair_of(mi):
                        act.activation(mem_kv[:, 2 * it + r, :], acc[r][:, 0:MEMT], ACT.Copy).then_inc(acc_read_act, 1)
            elif name == "gate":
                act.wait_ge(x_stored, m["x_stored"])
                for r in range(2):
                    split_weight(m, r + 1, KT * 128, 3 * r)
                    for c, (a, n) in enumerate(token_chunks(TOK, CHUNK_TOK)):
                        act.wait_ge(acc_ready, m["acc_ready"] + 3 * r + c + 1)
                        act.activation(y_sb[:, 6 + r, a:a + n], acc[(3 * r + c) % 2][:, 0:n],
                                       ACT.Silu).then_inc(acc_read_act, 1)
            elif name == "memory_jobs":
                per = job_counts("M")
                for j in range(2):
                    job(at_iteration(m, per, j), "M", 4 * j, dict(w=m["w"]), KT * 128,
                        lambda t, a, n: y_sb[:, 3 * j + t, a:a + n])
                act.wait_ge(acc_read_act, m["acc_read_act"] + 2 * per["acc_read_act"])
                for t in range(6):
                    act.activation(y_sb[:, t, :], y_sb[:, t, :], ACT.Silu).then_inc(gates_ready, 1)
            elif name == "latents":
                act.wait_ge(acc_read_dve, m["acc_read_dve"])
                for t in range(6):
                    if t < 5:
                        split_weight(m, t + 1, KT * 128, 3 * t)
                    for c, (a, n) in enumerate(token_chunks(TOK, CHUNK_TOK)):
                        act.wait_ge(acc_ready, m["acc_ready"] + 3 * t + c + 1)
                        act.activation(c_tmp[:, t, a:a + n], acc[(3 * t + c) % 2][:, 0:n],
                                       ACT.Copy).then_inc(acc_read_act, 1)
            elif name == "jobs":
                per = job_counts(o["kind"])
                n_w = len(JOB_PROJ[o["kind"]])
                with act.Fori(0, 3) as it:
                    mi = at_iteration(m, o["counts"], it)
                    for u in range(2):
                        job(at_iteration(mi, per, u), o["kind"], n_w * u, dict(w=mi["w"]),
                            0 if o["kind"] == "C" else KT * 128)
                if o["kind"] == "C":
                    after = {k: v + 3 * o["counts"].get(k, 0) for k, v in m.items()}
                    split_weight(after, 0, KT * 128, 0)
            elif name == "out":
                act.wait_ge(acc_read_dve, m["acc_read_dve"])
                for k in range(KT):
                    act.activation(h_v[:, 0, k, :], y_sb[:, k, :], ACT.Copy).then_inc(normed_hi, 1)
                for f in range(KT):
                    if o["w8"] + f + 1 < LAST_W8:
                        split_weight(m, f + 1, KT * 128, 3 * f)

    @block.vector
    def _(dve):
        def normalise(m, what, layer=0):
            _, _, _, steps = norm_plan(what, layer)
            dve.wait_ge(rstd_ready, m["rstd_ready"] + 1)
            for n, (tile, g, hi, _, store) in enumerate(steps):
                w = tile.shape[-1]
                if n >= 2 and hi is not None:
                    dve.wait_ge(normed_lo, m["normed_lo"] + n - 1)
                if n >= 2 and store is not None:
                    dve.wait_ge(normed_stored[n % 2], m[f"normed_stored{n % 2}"] + 16 * (n // 2))
                dve.scalar_tensor_tensor(out=raw[n % 2][:, 0:w], in0=tile, scalar=gains[:, g:g + 1],
                                         in1=rstd[:, 0:w], op0=ALU.mult, op1=ALU.mult).then_inc(normed, 1)

        def rotate(m, own, src, dst, tmp, src_rows=64):
            dve.tensor_tensor(tmp[64:96, 0:TOK], src[96:128, 0:TOK], rope_sb[96:128, :], ALU.mult)
            dve.tensor_tensor(dst[64:96, 0:TOK], src[64:96, 0:TOK], rope_sb[64:96, :], ALU.mult).then_inc(recips_ready, 1)
            dve.wait_ge(recips_ready, own + 1)
            dve.tensor_tensor(dst[64:96, 0:TOK], dst[64:96, 0:TOK], tmp[64:96, 0:TOK], ALU.add).then_inc(recips_ready, 1)
            dve.wait_ge(recips_ready, own + 2)

        def job(m, kind, tile):
            groups = GROUPS[kind]
            nv = len(V_CHUNKS[kind])
            r_own = m["recips_ready"]
            dve.wait_ge(acc_read_act, m["acc_read_act"] + 3)
            if kind == "C":
                rotate(m, r_own, raw[0], raw[0], raw[1])
                dve.tensor_copy(q_sp[0:96, 0, :], raw[0][0:96, 0:TOK]).then_inc(opnd_hi_made, 1)
                dve.wait_ge(acc_read_act, m["acc_read_act"] + 6)
                rotate(m, r_own + 2, raw[0], raw[0], raw[1])
                dve.tensor_copy(qo_sp[0:96, 0, :], raw[0][0:96, 0:TOK]).then_inc(opnd_hi_made, 1)
                r_own = r_own + 4
                dve.wait_ge(acc_read_act, m["acc_read_act"] + 10)
                dve.tensor_copy(k_sp[0:64, 0, :], raw[1][0:64, :]).then_inc(opnd_hi_made, 1)
                dve.tensor_copy(ko_v[0:64, 0, :], raw[0][0:64, :]).then_inc(opnd_hi_made, 1)
            else:
                dve.tensor_copy(q_sp[:, 0, :], raw[0][:, 0:TOK]).then_inc(opnd_hi_made, 1)
                if kind != "M":
                    dve.wait_ge(acc_read_act, m["acc_read_act"] + 6)
                dve.wait_ge(kcache_loaded, m["kcache_loaded"] + (32 if kind == "M" else 16))
                n = 2 * MEMT if kind == "M" else KEYS
                dve.tensor_copy(k_sp[:, 0, 0:n], raw[1][:, 0:n]).then_inc(opnd_hi_made, 1)
                if kind != "M":
                    dve.wait_ge(vcache_loaded, m["vcache_loaded"] + 16)
                    dve.tensor_copy(v_sp[:, 0, 8:12, :], v_cache[:, :, :]).then_inc(opnd_hi_made, 1)
            for v, chunk in enumerate(V_CHUNKS[kind]):
                dve.wait_ge(turned_hi_made, m["turned_hi_made"] + v + 1)
                rows, n, vt = chunk[0][2], len(chunk), chunk[0][0]
                dve.tensor_tensor(v_sp[0:rows, 1, vt:vt + n, :],
                                  t_ps[v % 2][0:rows, 0:128 * n].rearrange("p (n d) -> p n d", d=128),
                                  v_sp[0:rows, 0, vt:vt + n, :].bitcast(F32), ALU.subtract).then_inc(turned_lo_made, 1)
            if kind == "A":
                dve.wait_ge(bias_loaded, m["bias_loaded"] + 16)
                both = bias[:, :].rearrange("p (h k) -> p h k", h=2)
                dve.memset(both[64:128, :, 0:CHUNK], NEG)
                dve.memset(both[0:64, :, BAND - CHUNK:BAND], NEG).then_inc(bias_masked, 1)
            if kind == "B":
                dve.wait_ge(bias_loaded, m["bias_loaded"] + 16)
                dve.tensor_scalar(bias[:, 0:1024], bias[:, 0:1024], slopes[:, bass.ds(tile, 1)], None,
                                  ALU.mult).then_inc(bias_masked, 1)
            if kind in "AB":
                dve.wait_ge(bias_masked, m["bias_masked"] + 1)
            else:
                dve.wait_ge(bias_loaded, m["bias_loaded"])
            ends, total = [], 0
            for g in groups:
                total += len(g.chunks)
                ends.append(total)
            s = 0
            normed = 0
            p_done = 0

            def minima(h, g, steps):
                nonlocal s
                for step in steps:
                    dve.wait_ge(scores_ready, m["scores_ready"] + s + 1)
                    if h >= 2:
                        dve.wait_ge(turned_ready, m["turned_ready"] + nv + ends[h - 2])
                    if step.which and h >= 1:
                        dve.wait_ge(probs_ready, m["probs_ready"] + p_done)
                    settle(dve)
                    at = prob_at(g, step)
                    b0 = step.bias0 + (BAND * step.head if kind == "A" else 0)
                    dve.tensor_tensor_reduce(
                        out=prob[0:step.rows, at:at + step.width],
                        in0=s_ps[s % 2][0:step.rows, 0:step.width],
                        in1=bias[0:step.rows, b0:b0 + step.width] if kind != "M" else bias[0:step.rows, 0:MEMT],
                        scale=-1.0, scalar=3e38, op0=ALU.add, op1=ALU.min,
                        accum_out=stat[0:step.rows, s % 8:s % 8 + 1]).then_inc(scores_biased, 1)
                    s += 1

            def probabilities(g):
                nonlocal normed, p_done
                count = 2 if kind == "B" else 1
                for first in range(0, len(g.steps), count):
                    steps = g.steps[first:first + count]
                    rows, width = steps[0].rows, steps[0].width
                    cols = []
                    for i, step in enumerate(steps):
                        n = normed + i
                        dve.wait_ge(exps_ready, m["exps_ready"] + n + 1)
                        cols.append(stat[0:rows, 16 + n % 8:17 + n % 8])
                        dve.reciprocal(cols[i], stat[0:rows, 8 + n % 8:9 + n % 8]).then_inc(recips_ready, 1)
                    at = prob_at(g, steps[0])
                    p = prob[0:rows, at:at + width]
                    if kind == "B":
                        dve.wait_ge(recips_ready, r_own + normed + count)
                        dve.tensor_scalar(p, p, cols[0], None, ALU.mult)
                        lamr = stat[0:rows, 24 + first // 2:25 + first // 2]
                        dve.tensor_scalar(lamr, cols[1], neg_lam[0:rows, :], None, ALU.mult).then_inc(lambda_recips_ready, 1)
                        b_count[0] = b_count[0] + 1
                        dve.wait_ge(lambda_recips_ready, m["lambda_recips_ready"] + b_count[0])
                        at1 = prob_at(g, steps[1])
                        dve.scalar_tensor_tensor(out=p, in0=prob[0:rows, at1:at1 + width], scalar=lamr, in1=p,
                                                 op0=ALU.mult, op1=ALU.add).then_inc(probs_ready, 1)
                    else:
                        dve.wait_ge(recips_ready, r_own + normed + 1)
                        dve.tensor_scalar(p, p, cols[0], None, ALU.mult).then_inc(probs_ready, 1)
                    normed += count
                    p_done += 1

            b_count = [0]
            half = [len(g.steps) // 2 for g in groups]
            minima(0, groups[0], groups[0].steps)
            probabilities(groups[0])
            minima(1, groups[1], groups[1].steps[:half[1]])
            a_i = 0
            for h, g in enumerate(groups):
                for i, chunk in enumerate(g.chunks):
                    dve.wait_ge(turned_hi_made, m["turned_hi_made"] + nv + a_i + 1)
                    for rows, c, n in rectangles(g, chunk):
                        ins = dve.tensor_tensor(pt[0:rows, a_i % 2, 1, c:c + n],
                                                t_ps[(nv + a_i) % 2][0:rows, c:c + n],
                                                pt[0:rows, a_i % 2, 0, c:c + n].bitcast(F32), ALU.subtract)
                    ins.then_inc(turned_lo_made, 1)
                    a_i += 1
                    if i == 0 and h + 1 < len(groups):
                        minima(h + 1, groups[h + 1], groups[h + 1].steps[half[h + 1]:])
                if h + 1 < len(groups):
                    probabilities(groups[h + 1])
                if h + 2 < len(groups):
                    minima(h + 2, groups[h + 2], groups[h + 2].steps[:half[h + 2]])
                dve.wait_ge(pv_done, m["pv_done"] + ends[h])
                o_ps = acc[output_bank(kind, h)]
                if kind == "B":
                    dve.wait_ge(v_stored, m["v_stored"] + 16)
                    dve.tensor_copy(raw[0][:, g.q0:g.q0 + g.qn], o_ps[:, 0:g.qn]).then_inc(acc_read_dve, 1)
                else:
                    r0 = 64 * g.head
                    gate = y_sb[r0:r0 + 64, tile, g.q0:g.q0 + g.qn]
                    dve.tensor_tensor(gate, o_ps[0:64, 0:g.qn], gate, ALU.mult).then_inc(acc_read_dve, 1)
            if kind == "B":
                dve.wait_ge(rstd_ready, m["rstd_ready"] + 1)
                dve.scalar_tensor_tensor(out=raw[0][:, 0:TOK], in0=raw[0][:, 0:TOK], scalar=sub_gain,
                                         in1=rstd, op0=ALU.mult, op1=ALU.mult).then_inc(recips_ready, 1)
                dve.wait_ge(recips_ready, m["recips_ready"] + s + 1)
                gate = y_sb[:, tile, :]
                dve.tensor_tensor(gate, raw[0][:, 0:TOK], gate, ALU.mult).then_inc(acc_read_dve, 1)

        dve.wait_ge(consts_loaded, 16 * 5)
        dve.wait_ge(consts_set, 1)
        for i in range(2):
            dve.tensor_tensor_reduce(out=prob[:, 64 * i:64 * i + 64],
                                     in0=lam[:, 128 * i:128 * i + 64], in1=lam[:, 128 * i + 64:128 * i + 128],
                                     scale=1.0, scalar=0.0, op0=ALU.mult, op1=ALU.add,
                                     accum_out=small[:, 3 + i:4 + i]).then_inc(consts_set, 1)
        dve.wait_ge(consts_set, 4)
        dve.scalar_tensor_tensor(out=neg_lam, in0=small[:, 6:7], scalar=-LAM_INIT, in1=small[:, 5:6],
                                 op0=ALU.add, op1=ALU.subtract).then_inc(consts_set, 1)
        dve.tensor_scalar(sub_gain, gains[:, G_SUB:G_SUB + 1], 1.0 - LAM_INIT, None, ALU.mult).then_inc(consts_set, 1)
        dve.wait_ge(consts_set, 6)
        for name, m, o in phases():
            if name == "norm":
                normalise(m, o["what"], o.get("layer", 0))
            elif name == "memory_jobs":
                per = job_counts("M")
                mb = dict(m, bias_loaded=m["bias_loaded"] + 16)
                for j in range(2):
                    job(at_iteration(mb, per, j), "M", 6 + j)
            elif name == "latents":
                dve.wait_ge(acc_read_act, m["acc_read_act"] + 18)
                dve.wait_ge(kcache_loaded, m["kcache_loaded"] + 32)
                dve.tensor_copy(lat_v[:, 0, :, TOK:KEYS], c_cache[:, :, :]).then_inc(opnd_hi_made, 1)
            elif name == "key_rope":
                dve.wait_ge(normed_stored[0], m["normed_stored0"])
                dve.wait_ge(normed_stored[1], m["normed_stored1"])
                dve.wait_ge(normed_lo, m["normed_lo"])
                rotate(m, m["recips_ready"], c_tmp[:, 5, :], raw[1], raw[0])
                dve.tensor_copy(k_sp[64:96, 0, :], raw[1][64:96, :]).then_inc(opnd_hi_made, 1)
                dve.tensor_copy(ko_v[64:96, 0, :], raw[1][64:96, :]).then_inc(opnd_hi_made, 1)
                dve.wait_ge(opnd_hi_made, m["opnd_hi_made"] + 2)
                for keys in (k_sp, ko_v):
                    dve.tensor_tensor(keys[64:96, 1, :], raw[1][64:96, :], keys[64:96, 0, :].bitcast(F32),
                                      ALU.subtract).then_inc(opnd_hi_made, 1)
            elif name == "jobs":
                per = job_counts(o["kind"])
                dve.wait_ge(gates_ready, m["gates_ready"])
                with dve.Fori(0, 3) as it:
                    mi = at_iteration(m, o["counts"], it)
                    for u in range(2):
                        job(at_iteration(mi, per, u), o["kind"], 2 * it + u)
            elif name == "out":
                for k in range(KT):
                    dve.wait_ge(normed_hi, m["normed_hi"] + k + 1)
                    dve.tensor_tensor(h_v[:, 1, k, :], y_sb[:, k, :], h_v[:, 0, k, :].bitcast(F32),
                                      ALU.subtract).then_inc(normed, 1)
                for f in range(KT):
                    dve.wait_ge(xt_in[f], 16 * (o["layer"] + 1))
                    for c, (a, n) in enumerate(token_chunks(TOK, CHUNK_TOK)):
                        dve.wait_ge(acc_ready, m["acc_ready"] + 3 * f + c + 1)
                        x = y_sb[:, f, a:a + n]
                        dve.tensor_tensor(x, acc[(3 * f + c) % 2][:, 0:n], x, ALU.add).then_inc(acc_read_dve, 1)

    @block.gpsimd
    def _(pool):
        def split_weight(m, r, wide):
            pool.wait_ge(whi_made, m["w"] + r + 1)
            pool.tensor_tensor(w_lo[:, r % 2, 0:wide], w_raw[:, r % 2, 0:wide],
                               w_hi[:, r % 2, 0:wide].bitcast(F32), ALU.subtract).then_inc(wlo_made, 1)

        def low(m, i, out, x, hi):
            pool.wait_ge(opnd_hi_made, m["opnd_hi_made"] + i + 1)
            pool.tensor_tensor(out, x, hi.bitcast(F32), ALU.subtract).then_inc(opnd_lo_made, 1)

        def job(m, kind, r0, w, pair, next_wide):
            proj = JOB_PROJ[kind]
            wm = dict(m, w=w)
            if kind == "C":
                split_weight(wm, r0, 384)
            for j in range(len(proj)):
                if j + 1 < len(proj):
                    split_weight(wm, r0 + j + 1, 128 * proj[j + 1][0])
                if kind == "C":
                    if j == 0:
                        low(m, 0, q_sp[0:96, 1, :], raw[0][0:96, 0:TOK], q_sp[0:96, 0, :])
                    elif j == 1:
                        low(m, 1, qo_sp[0:96, 1, :], raw[0][0:96, 0:TOK], qo_sp[0:96, 0, :])
                    elif j == 2:
                        low(m, 2, k_sp[0:64, 1, :], raw[1][0:64, :], k_sp[0:64, 0, :])
                        low(m, 3, ko_v[0:64, 1, :], raw[0][0:64, :], ko_v[0:64, 0, :])
                elif j == 0:
                    low(m, 0, q_sp[:, 1, :], raw[0][:, 0:TOK], q_sp[:, 0, :])
                elif j == 1:
                    low(m, 1, k_sp[:, 1, :], raw[1][:, :], k_sp[:, 0, :])
                    low(m, 2, v_sp[:, 1, 8:12, :], v_cache[:, :, :], v_sp[:, 0, 8:12, :])
            if kind == "M":
                low(m, 1, k_sp[:, 1, 0:2 * MEMT], raw[1][:, 0:2 * MEMT], k_sp[:, 0, 0:2 * MEMT])
            for t, (kt, _) in enumerate(SIDE_PROJ[kind]):
                split_weight(wm, r0 + len(proj) + t, 128 * kt)
            if next_wide:
                split_weight(wm, r0 + len(proj) + len(SIDE_PROJ[kind]), next_wide)

        pool.memset(ones[:, :], 1.0)
        pool.memset(eps_sb, EPS).then_inc(consts_set, 1)
        pool.wait_ge(consts_loaded, 16 * 5)
        split_weight(fresh(), 0, KT * 128)
        for name, m, o in phases():
            if name == "norm":
                _, _, _, steps = norm_plan(o["what"], o.get("layer", 0))
                for n, (tile, _, hi, lo, _) in enumerate(steps):
                    if hi is not None:
                        pool.wait_ge(normed_hi, m["normed_hi"] + n + 1)
                        pool.tensor_tensor(lo, raw[n % 2][:, 0:tile.shape[-1]], hi.bitcast(F32),
                                           ALU.subtract).then_inc(normed_lo, 1)
            elif name in ("mem", "gate"):
                with pool.Fori(0, 8 if name == "mem" else 1) as it:
                    mi = dict(m, w=m["w"] + 2 * it)
                    for r in range(2):
                        split_weight(mi, r + 1, KT * 128)
            elif name == "memory_jobs":
                per = job_counts("M")
                for j in range(2):
                    job(at_iteration(m, per, j), "M", 4 * j, m["w"], 0, KT * 128)
            elif name == "latents":
                for t in range(5):
                    split_weight(m, t + 1, KT * 128)
                low(m, 0, lat_v[:, 1, :, TOK:KEYS], c_cache[:, :, :], lat_v[:, 0, :, TOK:KEYS])
            elif name == "jobs":
                per = job_counts(o["kind"])
                n_w = len(JOB_PROJ[o["kind"]])
                with pool.Fori(0, 3) as it:
                    mi = at_iteration(m, o["counts"], it)
                    for u in range(2):
                        job(at_iteration(mi, per, u), o["kind"], n_w * u, mi["w"], 2 * it + u,
                            0 if o["kind"] == "C" else KT * 128)
                if o["kind"] == "C":
                    split_weight(dict(m, w=m["w"] + 3 * o["counts"]["w"]), 0, KT * 128)
            elif name == "out":
                for f in range(KT):
                    if o["w8"] + f + 1 < LAST_W8:
                        split_weight(m, f + 1, KT * 128)

    @block.tensor
    def _(pe):
        def project(m, r, kt, chunks, moving, done, freed, freed_before):
            pe.wait_ge(wlo_made, m["w"] + r + 1)
            for a, n in chunks:
                if done >= 2:
                    pe.wait_ge(freed, freed_before + done - 1)
                out = acc[done % 2][:, 0:n]
                for k in range(kt):
                    for i, (ws, xs) in enumerate(PASSES):
                        w = (w_hi, w_lo)[ws][:, r % 2, 128 * k:128 * k + 128]
                        ins = pe.matmul(out, w, moving(xs, k, a, n), start=k == 0 and i == 0,
                                        stop=k == kt - 1 and i == 2)
                ins.then_inc(acc_ready, 1)
                done += 1
            return done

        def banks_free(m):
            pe.wait_ge(acc_read_act, m["acc_read_act"])
            pe.wait_ge(acc_read_dve, m["acc_read_dve"])
            pe.wait_ge(turned_lo_made, m["turned_lo_made"])

        def sums(m, k, slot, chunks, first, last):
            pe.wait_ge(squares_ready, m["squares_ready"] + k + 1)
            for c, (a, n) in enumerate(chunks):
                ins = pe.matmul(sum_banks[c][:, 0:n], ones[:, :], raw[slot][:, a:a + n], start=first, stop=last)
            ins.then_inc(squares_summed, 1)

        def side_part(m, kind, r, done, t, c, number, part, parts):
            kt, chunks = SIDE_PROJ[kind][t]
            a, n = chunks[c]
            passes = [(k, i) for k in range(kt) for i in range(3)]
            if part == 0:
                pe.wait_ge(wlo_made, m["w"] + r + t + 1)
                pe.wait_ge(acc_read_act, m["acc_read_act"] + done + number)
            for k, i in passes[len(passes) * part // parts:len(passes) * (part + 1) // parts]:
                ws, xs = PASSES[i]
                w = (w_hi, w_lo)[ws][:, (r + t) % 2, 128 * k:128 * k + 128]
                ins = pe.matmul(acc[1][:, 0:n], w, h_v[:, xs, k, a:a + n], start=k == 0 and i == 0,
                                stop=k == kt - 1 and i == 2)
            if part == parts - 1:
                ins.then_inc(acc_ready, 1)

        def job(m, kind, r0, w):
            groups, proj, v_chunks = GROUPS[kind], JOB_PROJ[kind], V_CHUNKS[kind]
            wm = dict(m, w=w)
            banks_free(m)
            done = 0
            for j, (kt, chunks) in enumerate(proj):
                if kind == "C":
                    src = cq_v if j < 2 else lat_v
                else:
                    src = h_v
                done = project(wm, r0 + j, kt, chunks, lambda s_, k, a, n: src[:, s_, k, a:a + n], done, acc_read_act, m["acc_read_act"])
            nv = len(v_chunks)
            for v, chunk in enumerate(v_chunks):
                if v == 0:
                    if kind == "M":
                        pe.wait_ge(vcache_loaded, m["vcache_loaded"] + 32)
                    else:
                        pe.wait_ge(acc_read_act, m["acc_read_act"] + done)
                if v >= 2:
                    pe.wait_ge(turned_lo_made, m["turned_lo_made"] + v - 1)
                for i, (_, col, n) in enumerate(chunk):
                    ins = pe.transpose(t_ps[v % 2][0:n, 128 * i:128 * i + 128], raw[0][:, col:col + n], ident[:, :])
                ins.then_inc(turned_ready, 1)
            pe.wait_ge(opnd_lo_made, m["opnd_lo_made"] + N_SPLITS[kind])
            s = 0

            def scores(g):
                nonlocal s
                for step in g.steps:
                    if s >= 2:
                        pe.wait_ge(scores_biased, m["scores_biased"] + s - 1)
                    if kind == "C":
                        rows = slice(0, 96)
                        q_v, k_v = (qo_sp, ko_v) if step.head else (q_sp, k_sp)
                    else:
                        x = step.which if kind == "B" else step.head
                        rows = slice(64 * x, 64 * x + 64)
                        q_v, k_v = q_sp, k_sp
                    if step.rows == DEC:
                        settle(pe)
                    for key, col, n in step.segs:
                        for i, (qs, ks) in enumerate(PASSES):
                            ins = pe.matmul(s_ps[s % 2][0:step.rows, col:col + n],
                                            q_v[rows, qs, step.q0:step.q0 + step.rows],
                                            k_v[rows, ks, key:key + n], start=i == 0, stop=i == 2)
                    ins.then_inc(scores_ready, 1)
                    s += 1

            a_i = 0
            steps_of = 0
            p_done = 0
            ends, total = [], 0
            for g in groups:
                total += 1 + (g.qn > DEC)
                ends.append(total)

            def turn(g, chunk, a):
                tv = nv + a
                if tv >= 2:
                    pe.wait_ge(turned_lo_made, m["turned_lo_made"] + tv - 1)
                if g.qn == DEC:
                    settle(pe)
                for i, vt, n, cols in chunk:
                    for t, col in enumerate(cols):
                        if col is None:
                            continue
                        step = g.steps[t * (2 if kind == "B" else 1)]
                        at = prob_at(g, step) + col
                        to = DEC * i if g.qn == DEC else 256 * i + 128 * t
                        ins = pe.transpose(t_ps[tv % 2][0:n, to:to + step.rows],
                                           prob[0:step.rows, at:at + n], ident[0:step.rows, 0:step.rows])
                ins.then_inc(turned_ready, 1)

            def times_v(g, h, chunk, a, first, last):
                pe.wait_ge(turned_lo_made, m["turned_lo_made"] + nv + a + 1)
                if first and (h >= 2 or (h and SIDE_PROJ[kind])):
                    pe.wait_ge(acc_read_dve, m["acc_read_dve"] + h - (0 if SIDE_PROJ[kind] else 1))
                width = 128 if kind == "B" else 64
                c0 = 0 if kind == "B" else 64 * g.head
                for x, (i, vt, n, cols) in enumerate(chunk):
                    if g.qn == DEC:
                        src, dst, w_ = DEC * i, 0, DEC
                    else:
                        t0 = 0 if cols[0] is not None else 1
                        w_ = 128 * sum(c is not None for c in cols)
                        src, dst = 256 * i + 128 * t0, 128 * t0
                    for y, (vs, ps) in enumerate(PASSES):
                        ins = pe.matmul(acc[output_bank(kind, h)][0:width, dst:dst + w_], v_sp[0:n, vs, vt, c0:c0 + width],
                                        pt[0:n, a % 2, ps, src:src + w_],
                                        start=first and x == 0 and y == 0,
                                        stop=last and x == len(chunk) - 1 and y == 2)
                ins.then_inc(pv_done, 1)

            scores(groups[0])
            scores(groups[1])
            turned = []
            for h, g in enumerate(groups):
                pe.wait_ge(probs_ready, m["probs_ready"] + ends[h])
                n = len(g.chunks)
                for c in range(n):
                    turn(g, g.chunks[c], a_i + c)
                    turned.append((g, h, g.chunks[c], a_i + c, c == 0, c == n - 1))
                    if c == n - 1 and h + 2 < len(groups):
                        scores(groups[h + 2])
                    if c == n - 1 or len(turned) > 1:
                        for t, sc, number in side_chunks(kind, h):
                            parts = max(n - 1, 1)
                            side_part(wm, kind, r0 + len(proj), done, t, sc, number, max(c - 1, 0), parts)
                    if len(turned) > 1:
                        times_v(*turned.pop(0))
                times_v(*turned.pop(0))
                a_i += n
            if kind == "B":
                sums(m, 0, 1, token_chunks(TOK, CHUNK_TOK), True, True)

        pe.wait_ge(consts_loaded, 16 * 5)
        pe.wait_ge(consts_set, 1)
        for name, m, o in phases():
            if name == "norm":
                tiles, _, chunks, _ = norm_plan(o["what"], o.get("layer", 0))
                banks_free(m)
                for k in range(len(tiles)):
                    sums(m, k, k % 2, chunks, k == 0, k == len(tiles) - 1)
            elif name == "mem":
                banks_free(m)
                pe.wait_ge(normed_lo, m["normed_lo"])
                for n in range(16):
                    layer = n // 4
                    project(m, n, KT, [(0, MEMT)],
                            lambda s_, k, a, w: memh_v[:, s_, (8 * layer + k) * MEMT:(8 * layer + k + 1) * MEMT],
                            n, acc_read_act, m["acc_read_act"])
            elif name == "gate":
                pe.wait_ge(normed_lo, m["normed_lo"])
                banks_free(m)
                done = 0
                for r in range(2):
                    done = project(m, r, KT, token_chunks(TOK, CHUNK_TOK),
                                   lambda s_, k, a, n: h_v[:, s_, k, a:a + n], done, acc_read_act, m["acc_read_act"])
            elif name == "memory_jobs":
                per = job_counts("M")
                for j in range(2):
                    job(at_iteration(m, per, j), "M", 4 * j, m["w"])
            elif name == "latents":
                banks_free(m)
                done = 0
                for t in range(6):
                    done = project(m, t, KT, token_chunks(TOK, CHUNK_TOK),
                                   lambda s_, k, a, n: h_v[:, s_, k, a:a + n], done, acc_read_act, m["acc_read_act"])
            elif name == "jobs":
                per = job_counts(o["kind"])
                n_w = len(JOB_PROJ[o["kind"]])
                pe.wait_ge(normed_lo, m["normed_lo"])
                pe.wait_ge(opnd_lo_made, m["opnd_lo_made"])
                pe.wait_ge(opnd_hi_made, m["opnd_hi_made"])
                with pe.Fori(0, 3) as it:
                    mi = at_iteration(m, o["counts"], it)
                    for u in range(2):
                        job(at_iteration(mi, per, u), o["kind"], n_w * u, mi["w"])
            elif name == "out":
                banks_free(m)
                pe.wait_ge(normed, m["normed"] + KT)
                done = 0
                for f in range(KT):
                    done = project(m, f, KT, token_chunks(TOK, CHUNK_TOK),
                                   lambda s_, k, a, n: h_v[:, s_, k, a:a + n], done, acc_read_dve, m["acc_read_dve"])

    ctx.close()


def _feature_tiles(x):
    t, f = x.shape
    return x.T.reshape(f // 128, 128, t).transpose(1, 0, 2)


def _weight_tile(w, columns):
    k = w.shape[0] // 128
    return w[:, columns].reshape(k, 128, 128).transpose(1, 0, 2).reshape(128, k * 128)


def _constants():
    q = np.arange(128)[:, None]
    j = np.arange(1024)[None, :]
    hidden = (j - 896) // CHUNK > q // CHUNK
    dist = np.where(hidden, NEG, -np.abs(896 + q - j)).astype(np.float32)
    cmask = np.where(hidden, NEG, 0.0).astype(np.float32)
    half = ROPE // 2
    inv = np.exp(np.float32(-math.log(10000.0)) * np.arange(half, dtype=np.float32) * np.float32(2.0)
                 / np.float32(ROPE)).astype(np.float32)
    pos = np.concatenate([np.arange(SEQ), PAST + np.arange(DEC)]).astype(np.float32)
    ang = (inv[:, None] * pos[None, :]).astype(np.float32)
    rope = np.zeros((128, TOK), np.float32)
    rope[64:96] = np.concatenate([np.cos(ang), np.cos(ang)])
    rope[96:128] = np.concatenate([-np.sin(ang), np.sin(ang)])
    slopes = np.exp2(-8.0 * np.arange(1, 7, dtype=np.float32) / 6).astype(np.float32)
    return dict(ident=np.eye(128, dtype=np.float32), dist=dist, cmask=cmask, rope=rope,
                slopes=np.ascontiguousarray(np.broadcast_to(slopes, (128, 6))))


def kernel(**inputs):
    import numpy as np
    import concourse.bacc as bacc
    from concourse.bass_utils import run_bass_kernel_spmd

    a = {k: np.asarray(v) for k, v in inputs.items()}
    sizes = {"A": 768, "B": 768}
    w_in = [a["w_in_a"][0], a["w_in_b"][0], a["w_in_c"][0], a["w_in_a"][1]]
    cols = lambda first: slice(first, first + 128)
    w8 = []
    for layer in range(DEPTH):
        w8 += [_weight_tile(a["w_mem_kv"][layer], cols(128 * t)) for t in range(4)]
    swapped = np.r_[ROPE // 2:ROPE, 0:ROPE // 2]
    for layer, kind in enumerate(KINDS):
        w = w_in[layer]
        n_mix = w.shape[1] - 256 - D
        gate = lambda first, last: [_weight_tile(w, cols(n_mix + 256 + 128 * t)) for t in range(first, last)]
        memory_q = lambda t: [_weight_tile(w, cols(n_mix + 128 * t))]
        w8 += gate(6, 8) + memory_q(0) + gate(0, 3) + memory_q(1) + gate(3, 6)
        if kind == "C":
            w8 += [_weight_tile(w, cols(128 * t)) for t in range(5)]
            kr = w[:, Q_LORA + KV_LORA:n_mix]
            w8.append(_weight_tile(np.concatenate([np.zeros((D, 64), w.dtype), kr, kr[:, swapped]], axis=1), cols(0)))
        else:
            w8 += [_weight_tile(w, cols(768 * part + 128 * t)) for t in range(6) for part in range(3)]
        w8 += [_weight_tile(a["w_out"][layer], cols(128 * t)) for t in range(KT)]
    uq = a["w_uq_c"][0].reshape(Q_LORA, 12, 96)
    uq = np.concatenate([uq, uq[:, :, 64 + swapped]], axis=2)
    ukv = a["w_ukv_c"][0].reshape(KV_LORA, 6, 2, 2, 64)
    col = lambda x: x.reshape(-1, 128).T
    rel = a["rel_bias_a"].transpose(0, 2, 1)
    c = _constants()
    k_cols = lambda x: x.reshape(x.shape[0], 6, 128).transpose(1, 2, 0)
    v_rows = lambda x: x.reshape(4, 128, 6, 128).transpose(2, 1, 0, 3)
    arrays = dict(
        x_in=_feature_tiles(np.concatenate([a["x_prompt"][0], a["x_sample"][0]])),
        mem_in=_feature_tiles(a["mem_prompt"][0]),
        w8=np.stack(w8),
        wc_q=np.stack([_weight_tile(uq[:, h], cols(0)) for h in range(12)]),
        wc_kv=np.stack([_weight_tile(ukv[:, p, :, part].reshape(KV_LORA, 128), cols(0))
                        for p in range(6) for part in range(2)]),
        gains_in=np.concatenate([col(a["norm_g"]), col(a["final_g"]), col(a["mem_norm_g"]), col(a["subln_g_b"]),
                                 col(a["q_norm_g_c"]), col(a["kv_norm_g_c"])], axis=1),
        lambda_in=a["lambda_b"].reshape(256),
        rel_in=rel[:, :, np.minimum(639 - np.arange(768), 128) + 128],
        kcache=np.concatenate([k_cols(a["cache_a_k"][0, 0]), k_cols(a["cache_b_k"][0, 0]), k_cols(a["cache_a_k"][1, 0])]),
        vcache=np.concatenate([v_rows(a["cache_a_v"][0, 0]), v_rows(a["cache_b_v"][0, 0]), v_rows(a["cache_a_v"][1, 0])]),
        lat_cache=_feature_tiles(a["cache_c_lat"][0, 0]),
        rope_cache=a["cache_c_rope"][0, 0].T,
        memk_cache=a["cache_mem_k"].reshape(DEPTH, MEMT, 2, 128).transpose(0, 2, 3, 1),
        memv_cache=a["cache_mem_v"].reshape(DEPTH, MEMT, 2, 128).transpose(0, 2, 3, 1),
        ident_in=c["ident"], dist_in=c["dist"], cmask_in=c["cmask"], rope_in=c["rope"], slope_in=c["slopes"])
    outs = dict(y_out=(D, TOK), k_a=(2, 6, 128, PAST + DEC), v_a=(2, 6, 128, PAST + DEC), k_b=(6, 128, TOK),
                v_b=(6, 128, TOK), lat_out=(KV_LORA, TOK), rope_out=(ROPE, TOK), memkv_out=(128, 16, MEMT))
    nc = bacc.Bacc("TRN2", target_bir_lowering=False, num_devices=1, dynamic_dma_scratch_size=1024)
    aps = {}
    for name in list(arrays):
        arrays[name] = np.ascontiguousarray(arrays[name])
        aps[name] = nc.dram_tensor(name, arrays[name].shape, F32, kind="ExternalInput").ap()
    for name, shape in outs.items():
        aps[name] = nc.dram_tensor(name, shape, F32, kind="ExternalOutput").ap()
    aps["x_scr"] = [nc.dram_tensor(f"x_scr{i}", (128, KT, TOK), F32, kind="Internal").ap() for i in range(DEPTH - 1)]
    aps["rel_scr"] = nc.dram_tensor("rel_scr", (12, 2, 128, BAND), F32, kind="Internal").ap()
    encoder(nc, **aps)
    r = run_bass_kernel_spmd(nc, [arrays], core_ids=[0]).results[0]
    y = r["y_out"].T
    back = lambda x: x.reshape(-1, x.shape[-1]).T
    k_a, v_a = (np.stack([back(r[n][j]) for j in range(2)]) for n in ("k_a", "v_a"))
    k_b, v_b = back(r["k_b"]), back(r["v_b"])
    lat, rope = r["lat_out"].T, r["rope_out"].T
    mem = r["memkv_out"].reshape(128, DEPTH, 2, 2, MEMT).transpose(1, 2, 4, 3, 0).reshape(DEPTH, 2, 1, MEMT, 4, 64)
    heads = lambda x, *shape: x.reshape(x.shape[0], 1, x.shape[1], *shape)
    return (y[None, :SEQ], y[None, SEQ:],
            heads(k_a[:, :PAST], 12, 64), heads(v_a[:, :PAST], 12, 64),
            heads(k_a[:, PAST:], 12, 64), heads(v_a[:, PAST:], 12, 64),
            heads(k_b[None, :SEQ], 6, 2, 64), heads(v_b[None, :SEQ], 6, 128),
            heads(k_b[None, SEQ:], 6, 2, 64), heads(v_b[None, SEQ:], 6, 128),
            lat[None, None, :SEQ], rope[None, None, :SEQ], lat[None, None, SEQ:], rope[None, None, SEQ:],
            mem[:, 0], mem[:, 1])
```

```python
import math
from contextlib import ExitStack

import numpy as np

import concourse.bass as bass
from concourse import mybir

F32 = mybir.dt.float32
F32R = mybir.dt.float32r
ALU = mybir.AluOpType
ACT = mybir.ActivationFunctionType

D = 1024
KT = D // 128
SEQ, DEC, PAST = 1024, 32, 512
TOK = SEQ + DEC
KEYS = TOK + PAST
MEMT = 256
CHUNK_TOK = TOK // 3
CHUNK_KEY = KEYS // 4
DEPTH, CHUNK = 4, 64
BAND = 640
EPS = 1e-6
NEG = -1e30
Q_LORA, KV_LORA, ROPE = 384, 256, 32
SCALE_64 = 64.0 ** -0.5
SCALE_C = 96.0 ** -0.5
KINDS = "ABCA"
LAM_INIT = 0.8 - 0.6 * math.exp(-0.3 * 1)
PASSES = ((0, 0), (0, 1), (1, 0))
G_NORM, G_FINAL, G_MEM, G_SUB, G_Q, G_KV = 0, 32, 40, 72, 73, 76
N_GAINS = 78


class Step:

    def __init__(self, head, tile, which, q0, rows, segs, bias0):
        self.head, self.tile, self.which = head, tile, which
        self.q0, self.rows, self.segs, self.bias0 = q0, rows, segs, bias0
        self.width = segs[-1][1] + segs[-1][2]


class Group:

    def __init__(self, head, parity, steps, chunks, q0, qn):
        self.head, self.parity, self.steps = head, parity, steps
        self.chunks, self.q0, self.qn = chunks, q0, qn


def key_segments(first, count):
    return [(first + a, a, min(512, count - a)) for a in range(0, count, 512)]


def groups_of(kind):
    out = []
    for head in range(1 if kind == "B" else 2):
        for n, g in enumerate([0, 1, 2, 3, 4] if head == 0 else [1, 0, 3, 2, 4]):
            parity = (5 * head + n) % 2
            whiches = (0, 1) if kind == "B" else (0,)
            if g == 4:
                if kind == "M":
                    segs, keys = [(MEMT, 0, MEMT)], [(2, 128), (3, 128)]
                else:
                    segs = [(TOK, 0, PAST), (SEQ, PAST, DEC)]
                    keys = [(8 + i, 128) for i in range(4)] + [(12, DEC)]
                bias0 = {"A": 0, "B": 384, "C": 0, "M": 0}[kind]
                steps = [Step(head, 0, w, SEQ, DEC, segs, bias0) for w in whiches]
                chunks = [[(i, vt, n_k, (i * 128,)) for i, (vt, n_k) in enumerate(keys)]]
                out.append(Group(head, parity, steps, chunks, SEQ, DEC))
                continue
            steps, starts = [], []
            for i in range(2):
                t = 2 * g + i
                if kind == "M":
                    k0, count, bias0 = 0, MEMT, 0
                elif kind == "A":
                    k0 = max(0, t - 4)
                    count, bias0 = (t + 1 - k0) * 128, 128 * (4 - min(t, 4))
                else:
                    k0, count, bias0 = 0, (t + 1) * 128, 128 * (7 - t)
                starts.append((k0, k0 + count // 128))
                steps += [Step(head, i, w, 128 * t, 128, key_segments(128 * k0, count), bias0)
                          for w in whiches]
            tiles = [(vt, tuple((vt - a) * 128 if a <= vt < b else None for a, b in starts))
                     for vt in range(starts[0][0], starts[1][1])]
            chunks = []
            for c in range(0, len(tiles), 2):
                chunk = [(i, vt, 128, cols) for i, (vt, cols) in enumerate(tiles[c:c + 2])]
                chunks.append(sorted(chunk, key=lambda x: None in x[3]))
            out.append(Group(head, parity, steps, chunks, 256 * g, 256))
    return out


GROUPS = {k: groups_of(k) for k in "ABCM"}
V_CHUNKS = {
    "A": [[(4 * c + i, 512 * c + 128 * i, 128) for i in range(4)] for c in range(2)] + [[(12, SEQ, DEC)]],
    "M": [[(i, 128 * i, 128) for i in range(4)]],
}
V_CHUNKS["B"] = V_CHUNKS["A"]
V_CHUNKS["C"] = V_CHUNKS["A"] + [[(8 + i, TOK + 128 * i, 128) for i in range(4)]]


def rectangles(group, chunk):
    if group.qn == DEC:
        full = [x for x in chunk if x[2] == 128]
        rest = [x for x in chunk if x[2] != 128]
        return [(128, 0, DEC * len(full))] + [(n, DEC * i, DEC) for i, _, n, _ in rest]
    found = []
    for i, _, _, cols in sorted(chunk):
        for t in range(2):
            at = 256 * i + 128 * t
            if cols[t] is None:
                continue
            if found and found[-1][1] + found[-1][2] == at:
                found[-1] = (128, found[-1][1], found[-1][2] + 128)
            else:
                found.append((128, at, 128))
    return found


def token_chunks(total, size):
    return [(a, min(size, total - a)) for a in range(0, total, size)]


JOB_PROJ = {
    "A": [],
    "M": [(KT, token_chunks(TOK, CHUNK_TOK))],
    "C": [(3, token_chunks(TOK, CHUNK_TOK))] * 2 + [(2, token_chunks(KEYS, CHUNK_KEY))] * 2,
}
JOB_PROJ["B"] = JOB_PROJ["A"]
QKV = [(KT, token_chunks(TOK, CHUNK_TOK))] * 3
SIDE_PROJ = {"A": QKV, "B": QKV, "C": [], "M": QKV}
N_SPLITS = {"A": 3, "B": 3, "C": 4, "M": 2}


def side_chunks(kind, h, last=False):
    if last:
        return []
    listed = [(t, c) for t, (_, chunks) in enumerate(SIDE_PROJ[kind]) for c in range(len(chunks))]
    n = len(GROUPS[kind])
    first, last = -(-len(listed) * h // n), -(-len(listed) * (h + 1) // n)
    return [(t, c, first + i) for i, (t, c) in enumerate(listed[first:last])]


def side_slots(kind, h, last=False):
    n, listed = len(GROUPS[kind][h].chunks), side_chunks(kind, h, last)
    slots, out = list(range(1, n)) or [0], [[] for _ in range(n)]
    for i, chunk in enumerate(listed):
        own = slots[len(slots) * i // len(listed):len(slots) * (i + 1) // len(listed)]
        own = own or [slots[len(slots) * i // len(listed)]]
        for part, c in enumerate(own):
            out[c].append((*chunk, part, len(own)))
    return out


def output_bank(kind, h):
    return 0 if SIDE_PROJ[kind] else h % 2


def job_counts(kind):
    groups = GROUPS[kind]
    proj = sum(len(c) for _, c in JOB_PROJ[kind])
    att = sum(len(g.chunks) for g in groups)
    v = len(V_CHUNKS[kind])
    steps = sum(len(g.steps) for g in groups)
    proj += sum(len(c) for _, c in SIDE_PROJ[kind])
    c = dict(w=len(JOB_PROJ[kind]) + len(SIDE_PROJ[kind]), acc_ready=proj, acc_read_act=proj,
             acc_read_dve=len(groups), opnd_hi_made=N_SPLITS[kind],
             opnd_lo_made=N_SPLITS[kind], turned_ready=v + att, turned_hi_made=v + att, turned_lo_made=v + att, pv_done=att,
             scores_ready=steps, scores_biased=steps, exps_ready=steps, recips_ready=steps,
             probs_ready=sum(1 + (g.qn > DEC) for g in groups))
    if kind in "AB":
        c.update(kcache_loaded=16, vcache_loaded=16, bias_loaded=16, bias_masked=1, k_stored=16, v_stored=16)
    if kind == "M":
        c.update(kcache_loaded=32, vcache_loaded=32)
    if kind == "B":
        c.update(acc_read_act=proj + 3, acc_read_dve=len(groups) + 1, squares_ready=1, squares_summed=1, rstd_ready=1, recips_ready=steps + 1,
                 lambda_recips_ready=steps // 2)
    if kind == "C":
        c.update(recips_ready=steps + 4)
    return c


def encoder(nc, x_in, mem_in, w8, wc_q, wc_kv, gains_in, lambda_in, rel_in, kcache, vcache, lat_cache,
            rope_cache, memk_cache, memv_cache, ident_in, dist_in, cmask_in, rope_in, slope_in,
            y_out, k_a, v_a, k_b, v_b, lat_out, rope_out, memkv_out, x_scr, rel_scr):
    ctx = ExitStack()
    place = [-(-nc.sbuf_base // 64) * 64]

    def sbuf(name, free, dtype=F32, at=None):
        size = 4 * int(np.prod(free))
        where = place[0] if at is None else at
        if at is None:
            place[0] += -(-size // 32) * 32
        return nc.alloc_sbuf_tensor_at(name, [128, *free], dtype, offset=where)

    h_flat = sbuf("h_split", [2 * KT * TOK], F32R)
    y_sb = sbuf("y_sb", [KT, TOK])
    w_raw = sbuf("w_raw", [2, KT * 128])
    w_hi = sbuf("w_hi", [2, KT * 128], F32R)
    w_lo = sbuf("w_lo", [2, KT * 128], F32R)
    qkv_at = place[0]
    q_sp = sbuf("q_split", [2, TOK], F32R)
    k_sp = sbuf("k_split", [2, KEYS], F32R)
    v_sp = sbuf("v_split", [2, 13, 128], F32R)
    c_tmp = sbuf("c_latents", [6, TOK], F32, at=qkv_at)
    c_cache = sbuf("c_cache", [2, PAST], F32, at=qkv_at + 4 * 6 * TOK)
    raw = [sbuf("raw0", [KEYS]), sbuf("raw1", [KEYS])]
    v_cache = sbuf("v_cache", [4, 128])
    prob = sbuf("prob", [5632])
    qo_at = place[0]
    qo_sp = sbuf("q_odd_split", [2, TOK], F32R)
    q_raw = sbuf("q_raw", [TOK], at=qo_at)
    rope_at = place[0]
    rope_sb = sbuf("rope_sb", [TOK])
    o_tmp = sbuf("o_tmp", [TOK], at=rope_at)
    pt = sbuf("pt_split", [2, 2, 512], F32R)
    bias = sbuf("bias", [2 * BAND])
    ident = sbuf("ident", [128])
    ones = sbuf("ones", [128])
    gains = sbuf("gains", [N_GAINS])
    slopes = sbuf("slopes", [6])
    lam = sbuf("lam", [256])
    stat = sbuf("stat", [32])
    small = sbuf("small", [8])
    assert place[0] <= nc.sbuf_usable_end, place[0]
    neg_lam, eps_sb, sub_gain = small[:, 0:1], small[:, 1:2], small[:, 2:3]

    h_v = h_flat[:, :].rearrange("p (s k t) -> p s k t", s=2, k=KT)
    memh_v = h_flat[:, :].rearrange("p (s f) -> p s f", s=2)
    lat_v = h_flat[:, 0:4 * KEYS].rearrange("p (s k t) -> p s k t", s=2, k=2)
    cq_at = 4 * KEYS
    cq_v = h_flat[:, cq_at:cq_at + 6 * TOK].rearrange("p (s k t) -> p s k t", s=2, k=3)
    ko_at = cq_at + 6 * TOK
    ko_v = h_flat[:, ko_at:ko_at + 2 * KEYS].rearrange("p (s t) -> p s t", s=2)
    y_flat = y_sb[:, :, :].rearrange("p k t -> p (k t)")
    mem_x = y_flat[:, 0:KT * MEMT].rearrange("p (k t) -> p k t", k=KT)
    mem_kv = y_flat[:, KT * MEMT:KT * MEMT + 16 * MEMT].rearrange("p (n t) -> p n t", n=16)
    rstd = prob[:, 0:TOK]
    o_squares = prob[:, TOK:2 * TOK]

    s_ps = [ctx.enter_context(nc.psum_tensor(f"scores{i}", [128, 1024], F32)) for i in range(2)]
    t_ps = [ctx.enter_context(nc.psum_tensor(f"turned{i}", [128, 512], F32)) for i in range(2)]
    acc = [ctx.enter_context(nc.psum_tensor(f"acc{i}", [128, 512], F32)) for i in range(2)]
    sum_banks = [acc[0], acc[1], t_ps[0]]

    def sem(name):
        return ctx.enter_context(nc.semaphore(name))

    consts_loaded = sem("consts_loaded")
    consts_set = sem("consts_set")
    w_loaded = [sem(f"w_loaded{i}") for i in range(2)]
    whi_made, wlo_made = sem("whi_made"), sem("wlo_made")
    acc_ready = sem("acc_ready")
    acc_read_act = sem("acc_read_act")
    acc_read_dve = sem("acc_read_dve")
    opnd_hi_made = sem("opnd_hi_made")
    opnd_lo_made = sem("opnd_lo_made")
    turned_ready = sem("turned_ready")
    turned_hi_made = sem("turned_hi_made")
    turned_lo_made = sem("turned_lo_made")
    pv_done = sem("pv_done")
    gates_ready = sem("gates_ready")
    scores_ready = sem("scores_ready")
    scores_biased = sem("scores_biased")
    exps_ready = sem("exps_ready")
    probs_ready = sem("probs_ready")
    recips_ready = sem("recips_ready")
    lambda_recips_ready = sem("lambda_recips_ready")
    kcache_loaded = sem("kcache_loaded")
    vcache_loaded = sem("vcache_loaded")
    bias_loaded = sem("bias_loaded")
    bias_masked = sem("bias_masked")
    k_stored, v_stored = sem("k_stored"), sem("v_stored")
    squares_ready = sem("squares_ready")
    squares_summed = sem("squares_summed")
    rstd_ready = sem("rstd_ready")
    normed = sem("normed")
    normed_hi, normed_lo = sem("normed_hi"), sem("normed_lo")
    normed_stored = [sem(f"normed_stored{i}") for i in range(2)]
    x_loaded = sem("x_loaded")
    x_stored = sem("x_stored")
    memkv_stored = sem("memkv_stored")
    rel_stored = sem("rel_stored")
    settled = sem("settled")
    xt_in = [sem(f"xt_in{f}") for f in range(KT)]
    block = ctx.enter_context(nc.Block())

    def settle(eng):
        eng.sem_inc(settled, 1)

    def advance(m, counts, times=1):
        for k, v in counts.items():
            m[k] = m[k] + v * times

    def at_iteration(m, counts, it):
        return {k: (v + it * counts[k] if counts.get(k) else v) for k, v in m.items()}

    def norm_counts(tiles, chunks, steps, split=True, store=False):
        c = dict(squares_ready=tiles, squares_summed=tiles, acc_read_act=chunks, rstd_ready=1, normed=steps)
        if split:
            c.update(normed_hi=steps, normed_lo=steps)
        if store:
            c.update(normed_stored0=8 * steps, normed_stored1=8 * steps)
        return c

    MEM_PROJ = dict(w=16, acc_ready=16, acc_read_act=16, memkv_stored=16)
    GATE = dict(w=2, acc_ready=6, acc_read_act=6)
    LATENTS = dict(w=6, acc_ready=18, acc_read_act=18, kcache_loaded=48, bias_loaded=16, opnd_hi_made=1, opnd_lo_made=1)
    KEY_ROPE = dict(recips_ready=2, k_stored=16, opnd_hi_made=4)
    QKV_FIRST = dict(w=3, acc_ready=9, acc_read_act=9, opnd_hi_made=2, opnd_lo_made=2, kcache_loaded=16,
                     vcache_loaded=16)
    OUT = dict(w=8, acc_ready=24, acc_read_dve=24, normed_hi=8, normed=8, x_stored=16 * 8)

    def job_start(m, kind, pair):
        m = dict(m)
        advance(m, QKV_FIRST)
        return at_iteration(m, job_counts(kind), pair)

    def double(c):
        return {k: 2 * v for k, v in c.items()}

    COUNTED = (
        "w", "acc_ready", "acc_read_act", "acc_read_dve", "opnd_hi_made", "opnd_lo_made", "turned_ready",
        "turned_hi_made", "turned_lo_made", "pv_done", "scores_ready", "scores_biased", "exps_ready",
        "probs_ready", "recips_ready", "lambda_recips_ready", "kcache_loaded", "vcache_loaded",
        "bias_loaded", "bias_masked", "k_stored", "v_stored", "squares_ready", "squares_summed",
        "rstd_ready", "normed", "normed_hi", "normed_lo", "normed_stored0", "normed_stored1",
        "x_loaded", "x_stored", "memkv_stored", "gates_ready")

    def fresh():
        m = {k: 0 for k in COUNTED}
        m["x_loaded"] = 16
        return m

    def course(m):
        w8_at = 0

        def give(name, counts, times=1, **more):
            start = dict(m)
            advance(m, counts, times)
            return name, start, dict(counts=counts, **more)

        yield give("norm", norm_counts(KT, 1, 4 * KT), what="mem")
        yield give("mem", MEM_PROJ, w8=w8_at)
        w8_at += 16
        yield give("load_x", dict(x_loaded=16))
        yield give("norm", norm_counts(KT, 3, KT), what="h", layer=0)
        for layer, kind in enumerate(KINDS):
            yield give("gate", GATE, w8=w8_at, layer=layer)
            yield give("memory_jobs", {**double(job_counts("M")), "bias_loaded": 16, "gates_ready": 6},
                       w8=w8_at + 2, layer=layer, last=kind)
            w8_at += 10
            if kind == "C":
                yield give("latents", LATENTS, w8=w8_at)
                w8_at += 6
                yield give("norm", norm_counts(3, 3, 3), what="cq")
                yield give("norm", norm_counts(2, 3, 2, store=True), what="lat")
                yield give("key_rope", KEY_ROPE)
            yield give("jobs", double(job_counts(kind)), 3, kind=kind, w8=w8_at, layer=layer)
            w8_at += 0 if kind == "C" else 18
            counts = dict(OUT)
            if layer == DEPTH - 1:
                counts.pop("x_stored")
            yield give("out", counts, w8=w8_at, layer=layer)
            w8_at += 8
            if layer < DEPTH - 1:
                yield give("norm", norm_counts(KT, 3, KT), what="h", layer=layer + 1)
        yield give("norm", norm_counts(KT, 3, KT, split=False, store=True), what="final")

    final_counts = fresh()
    COURSE = list(course(final_counts))
    LAST_W8 = w8.shape[0]

    def phases():
        return COURSE

    def norm_plan(what, layer=0):
        if what == "mem":
            steps = [(mem_x[:, k, :], G_MEM + 8 * i + k,
                      memh_v[:, 0, (8 * i + k) * MEMT:(8 * i + k + 1) * MEMT],
                      memh_v[:, 1, (8 * i + k) * MEMT:(8 * i + k + 1) * MEMT], None)
                     for i in range(DEPTH) for k in range(KT)]
            return [mem_x[:, k, :] for k in range(KT)], D, [(0, MEMT)], steps
        tok = token_chunks(TOK, CHUNK_TOK)
        if what == "h":
            return ([y_sb[:, k, :] for k in range(KT)], D, tok,
                    [(y_sb[:, k, :], G_NORM + 8 * layer + k, h_v[:, 0, k, :], h_v[:, 1, k, :], None)
                     for k in range(KT)])
        if what == "final":
            return ([y_sb[:, k, :] for k in range(KT)], D, tok,
                    [(y_sb[:, k, :], G_FINAL + k, None, None, y_out[k * 128:(k + 1) * 128, :])
                     for k in range(KT)])
        if what == "cq":
            return ([c_tmp[:, k, :] for k in range(3)], Q_LORA, tok,
                    [(c_tmp[:, k, :], G_Q + k, cq_v[:, 0, k, :], cq_v[:, 1, k, :], None) for k in range(3)])
        return ([c_tmp[:, 3 + k, :] for k in range(2)], KV_LORA, tok,
                [(c_tmp[:, 3 + k, :], G_KV + k, lat_v[:, 0, k, 0:TOK], lat_v[:, 1, k, 0:TOK],
                  lat_out[k * 128:(k + 1) * 128, :]) for k in range(2)])

    def prob_at(group, step):
        if step.which:
            at = 3584 + 1024 * step.tile
        else:
            at = (768 if group.parity == 0 else 1024) * step.tile + 1536 * group.parity
        return at

    @block.sync
    def _(sp):
        for dst, src in ((ident[:, :], ident_in), (gains[:, :], gains_in), (slopes[:, :], slope_in),
                         (lam[:, :], lambda_in.partition_broadcast(128))):
            sp.dma_start(dst, src).then_inc(consts_loaded, 16)
        sp.dma_start(mem_x, mem_in).then_inc(x_loaded, 16)
        toeplitz = bass.AP(rel_in.tensor, 127, [[768, 24], [-1, 128], [1, BAND]])
        sp.dma_start(rel_scr.rearrange("g h p k -> (g h) p k"), toeplitz).then_inc(rel_stored, 16)

        def weight(n, r, src, width, slot=None):
            slot = r % 2 if slot is None else slot
            sp.wait_ge(wlo_made, n + r - 1)
            sp.dma_start(w_raw[:, slot, 0:width], src).then_inc(w_loaded[slot], 16)

        def w8_tile(index):
            return w8[index].rearrange("(o p) f -> (o p) f", o=1)

        def first_gates(w, index):
            for r in range(2):
                weight(w, r, w8[index + r], KT * 128)

        for name, m, o in phases():
            if name == "norm" and o["what"] in ("lat", "final"):
                _, _, _, steps = norm_plan(o["what"])
                for n, step in enumerate(steps):
                    sp.wait_ge(normed, m["normed"] + n + 1)
                    sp.dma_start(step[4], raw[n % 2][:, 0:TOK]).then_inc(normed_stored[n % 2], 16)
            elif name == "mem":
                def body(it):
                    for r in range(2):
                        weight(m["w"] + 2 * it, r, w8[o["w8"] + 2 * it + r], KT * 128)
                for n in range(2):
                    sp.dma_start(w_raw[:, n, :], w8[o["w8"] + n]).then_inc(w_loaded[n], 16)
                with sp.Fori(1, 8) as it:
                    body(it)
                first_gates(m["w"] + 16, o["w8"] + 16)
                sp.wait_ge(acc_read_act, m["acc_read_act"] + 16)
                sp.dma_start(memkv_out, mem_kv).then_inc(memkv_stored, 16)
            elif name == "load_x":
                sp.wait_ge(normed_lo, m["normed_lo"])
                sp.wait_ge(memkv_stored, m["memkv_stored"])
                sp.dma_start(y_sb[:, :, :], x_in).then_inc(x_loaded, 16)
            elif name == "memory_jobs":
                for r in range(2):
                    weight(m["w"], r, w8[o["w8"] + r], KT * 128)
                sp.wait_ge(acc_read_dve, m["acc_read_dve"])
                sp.dma_start(bias[:, 0:MEMT], cmask_in[:, 0:MEMT]).then_inc(bias_loaded, 16)
                sp.wait_ge(normed_lo, m["normed_lo"])
                layer = o["layer"]
                per = job_counts("M")
                for j in range(2):
                    mj = at_iteration(m, per, j)
                    sp.wait_ge(opnd_lo_made, mj["opnd_lo_made"])
                    sp.dma_start(raw[1][:, 0:MEMT], memkv_out[:, 4 * layer + j, :]).then_inc(kcache_loaded, 16)
                    sp.dma_start(raw[1][:, MEMT:2 * MEMT], memk_cache[layer, j]).then_inc(kcache_loaded, 16)
                    sp.wait_ge(opnd_lo_made, mj["opnd_lo_made"] + 1)
                    sp.dma_start(raw[0][:, 0:MEMT], memkv_out[:, 4 * layer + 2 + j, :]).then_inc(vcache_loaded, 16)
                    sp.dma_start(raw[0][:, MEMT:2 * MEMT], memv_cache[layer, j]).then_inc(vcache_loaded, 16)
                    for r in range(4 * j + 2, min(4 * j + 6, 8)):
                        weight(m["w"], r, w8[o["w8"] + r], KT * 128)
            elif name == "latents":
                for r in range(2):
                    weight(m["w"], r, w8[o["w8"] + r], KT * 128)
                sp.wait_ge(opnd_lo_made, m["opnd_lo_made"])
                sp.wait_ge(acc_read_dve, m["acc_read_dve"])
                sp.dma_start(c_cache[:, :, :], lat_cache).then_inc(kcache_loaded, 16)
                sp.dma_start(rope_sb[:, :], rope_in).then_inc(kcache_loaded, 16)
                sp.dma_start(raw[1][64:96, TOK:KEYS], rope_cache).then_inc(kcache_loaded, 16)
                sp.dma_start(bias[:, 0:1024], cmask_in).then_inc(bias_loaded, 16)
                for r in range(2, 6):
                    weight(m["w"], r, w8[o["w8"] + r], KT * 128)
            elif name == "key_rope":
                sp.wait_ge(recips_ready, m["recips_ready"] + 2)
                sp.dma_start(rope_out, raw[1][64:96, 0:TOK]).then_inc(k_stored, 16)
            elif name == "jobs":
                kind, layer = o["kind"], o["layer"]
                per = job_counts(kind)
                sp.wait_ge(rel_stored, 16)
                if kind == "C":
                    with sp.Fori(0, 3) as it:
                        for u in range(2):
                            pair = 2 * it + u
                            for i, (src, width) in enumerate(((wc_q[2 * pair], 384), (wc_q[2 * pair + 1], 384),
                                                              (wc_kv[2 * pair], 256), (wc_kv[2 * pair + 1], 256))):
                                weight(m["w"] + 8 * it, 4 * u + i, src, width)
                    continue
                slot = {0: 0, 1: 1, 3: 2}[layer]

                def job_transfers(pair, u, last=False):
                    mj = job_start(m, kind, pair)
                    if not last:
                        for r in (1, 2):
                            weight(mj["w"], r, w8[o["w8"] + 3 * pair + 3 + r], KT * 128, (1 + u + r) % 2)
                    sp.wait_ge(scores_biased, mj["scores_biased"])
                    if kind == "A":
                        sp.dma_start(bias[:, :].rearrange("p (h k) -> p h k", h=2),
                                     rel_scr[6 * (layer // 3) + pair].rearrange("h p k -> p h k")).then_inc(bias_loaded, 16)
                        k_dst, v_dst = k_a[layer // 3, pair], v_a[layer // 3, pair]
                        first = PAST
                    else:
                        sp.dma_start(bias[:, 0:1024], dist_in).then_inc(bias_loaded, 16)
                        k_dst, v_dst, first = k_b[pair], v_b[pair], 0
                    sp.wait_ge(acc_read_act, mj["acc_read_act"])
                    sp.dma_start(k_dst, raw[1][:, first:TOK]).then_inc(k_stored, 16)
                    sp.dma_start(v_dst, raw[0][:, first:TOK]).then_inc(v_stored, 16)
                    if last:
                        return
                    sp.wait_ge(opnd_lo_made, mj["opnd_lo_made"])
                    sp.dma_start(raw[1][:, TOK:KEYS], kcache[6 * slot + pair + 1]).then_inc(kcache_loaded, 16)
                    sp.wait_ge(opnd_lo_made, mj["opnd_lo_made"] + 1)
                    sp.dma_start(v_cache[:, :, :], vcache[6 * slot + pair + 1]).then_inc(vcache_loaded, 16)
                    weight(mj["w"], 3, w8[o["w8"] + 3 * pair + 6], KT * 128, u % 2)

                for r in range(4):
                    weight(m["w"], r, w8[o["w8"] + r], KT * 128)
                sp.wait_ge(opnd_lo_made, m["opnd_lo_made"])
                sp.dma_start(raw[1][:, TOK:KEYS], kcache[6 * slot]).then_inc(kcache_loaded, 16)
                sp.dma_start(v_cache[:, :, :], vcache[6 * slot]).then_inc(vcache_loaded, 16)
                with sp.Fori(0, 2) as it:
                    for u in range(2):
                        job_transfers(2 * it + u, u)
                job_transfers(4, 0)
                job_transfers(5, 1, last=True)
            elif name == "out":
                layer = o["layer"]
                for r in range(2):
                    if r or KINDS[layer] == "C":
                        weight(m["w"], r, w8[o["w8"] + r], KT * 128)
                src = x_in if layer == 0 else x_scr[layer - 1]
                sp.wait_ge(x_stored, m["x_stored"])
                for f in range(KT):
                    sp.wait_ge(normed, m["normed"] + f + 1)
                    sp.dma_start(y_sb[:, f, :], src[:, f, :]).then_inc(xt_in[f], 16)

                def store(f):
                    if layer < DEPTH - 1:
                        sp.wait_ge(acc_read_dve, m["acc_read_dve"] + 3 * (f + 1))
                        sp.dma_start(x_scr[layer][:, f, :], y_sb[:, f, :]).then_inc(x_stored, 16)
                for f in range(KT):
                    if f + 2 < KT:
                        weight(m["w"], f + 2, w8[o["w8"] + f + 2], KT * 128)
                    if f + 2 == KT and layer < DEPTH - 1:
                        first_gates(m["w"] + KT, o["w8"] + KT)
                    store(f)
        sp.wait_ge(normed_stored[0], final_counts["normed_stored0"])
        sp.wait_ge(normed_stored[1], final_counts["normed_stored1"])
        sp.wait_ge(k_stored, final_counts["k_stored"])
        sp.wait_ge(v_stored, final_counts["v_stored"])
        sp.wait_ge(memkv_stored, final_counts["memkv_stored"])
        sp.wait_ge(x_stored, final_counts["x_stored"])

    @block.scalar
    def _(act):
        def split_weight(m, r, wide, end):
            w = m["w"]
            act.wait_ge(w_loaded[r % 2], 8 * w + 16 * (r // 2 + 1))
            act.wait_ge(acc_ready, m["acc_ready"] + end)
            act.activation(w_hi[:, r % 2, 0:wide], w_raw[:, r % 2, 0:wide], ACT.Copy).then_inc(whi_made, 1)

        def norm(m, what, layer=0):
            tiles, width, chunks, steps = norm_plan(what, layer)
            act.wait_ge(x_loaded, m["x_loaded"])
            act.wait_ge(acc_read_dve, m["acc_read_dve"])
            act.wait_ge(acc_read_act, m["acc_read_act"])
            act.wait_ge(k_stored, m["k_stored"])
            act.wait_ge(v_stored, m["v_stored"])
            act.wait_ge(normed_lo, m["normed_lo"])
            act.wait_ge(normed_stored[0], m["normed_stored0"])
            act.wait_ge(normed_stored[1], m["normed_stored1"])
            for k, tile in enumerate(tiles):
                if k >= 2:
                    act.wait_ge(squares_summed, m["squares_summed"] + k - 1)
                n = sum(c for _, c in chunks)
                act.activation(raw[k % 2][:, 0:n], tile, ACT.Square).then_inc(squares_ready, 1)
            act.wait_ge(squares_summed, m["squares_summed"] + len(tiles))
            root(m, chunks, width, len(tiles))
            for n, step in enumerate(steps):
                if step[2] is not None:
                    act.wait_ge(normed, m["normed"] + n + 1)
                    act.activation(step[2], raw[n % 2][:, 0:step[0].shape[-1]], ACT.Copy).then_inc(normed_hi, 1)

        def root(m, chunks, width, used, first=0):
            for c, (a, n) in enumerate(chunks):
                act.activation(rstd[:, a:a + n], sum_banks[c][:, 0:n], ACT.Ln, scale=1.0 / width,
                               bias=eps_sb).then_inc(acc_read_act, 1)
            n = sum(c for _, c in chunks)
            act.wait_ge(acc_read_act, m["acc_read_act"] + first + len(chunks))
            act.activation(rstd[:, 0:n], rstd[:, 0:n], ACT.Exp, scale=-0.5).then_inc(rstd_ready, 1)

        def transposed_v(m, kind):
            for v, chunk in enumerate(V_CHUNKS[kind]):
                act.wait_ge(turned_ready, m["turned_ready"] + v + 1)
                act.wait_ge(pv_done, m["pv_done"])
                rows, n = chunk[0][2], len(chunk)
                act.activation(v_sp[0:rows, 0, chunk[0][0]:chunk[0][0] + n, :],
                               t_ps[v % 2][0:rows, 0:128 * n].rearrange("p (n d) -> p n d", d=128),
                               ACT.Copy).then_inc(turned_hi_made, 1)

        def qkv_out(t, a, n):
            return (q_raw, raw[1], raw[0])[t][:, a:a + n]

        def qkv_scale(kind, t):
            return SCALE_64 if kind in "AB" and t == 0 else 1.0

        def job(m, kind, r0, it, next_wide, side_out=None, last=False):
            groups, proj, side = GROUPS[kind], JOB_PROJ[kind], [] if last else SIDE_PROJ[kind]
            if proj:
                act.wait_ge(acc_read_dve, m["acc_read_dve"])
                act.wait_ge(k_stored, m["k_stored"])
                act.wait_ge(v_stored, m["v_stored"])
            wm = dict(m, w=it["w"])
            ends = [0]
            for _, chunks in proj:
                ends.append(ends[-1] + len(chunks))
            if kind == "C":
                split_weight(wm, r0, 384, 0)
            done = 0
            for j, (kt, chunks) in enumerate(proj):
                if j + 1 < len(proj):
                    split_weight(wm, r0 + j + 1, 128 * proj[j + 1][0], ends[j])
                elif side:
                    split_weight(wm, r0 + j + 1, 128 * side[0][0], ends[j])
                for c, (a, n) in enumerate(chunks):
                    act.wait_ge(acc_ready, m["acc_ready"] + done + 1)
                    src = acc[done % 2]
                    if kind == "C" and c == 0 and j == 1:
                        act.wait_ge(opnd_lo_made, m["opnd_lo_made"] + 1)
                    if kind == "C" and c == 0 and j == 2:
                        act.wait_ge(opnd_lo_made, m["opnd_lo_made"] + 2)
                    if kind == "C" and c == 0 and j == 3:
                        act.wait_ge(opnd_lo_made, m["opnd_lo_made"] + 4)
                    done += 1
                    q_scale = SCALE_C if kind == "C" else SCALE_64
                    if j == 0 or (kind == "C" and j == 1):
                        act.activation(raw[0][:, a:a + n], src[:, 0:n], ACT.Copy, scale=q_scale).then_inc(acc_read_act, 1)
                    elif kind == "C" and j == 2:
                        act.activation(raw[1][0:64, a:a + n], src[0:64, 0:n], ACT.Copy)
                        act.activation(raw[0][0:64, a:a + n], src[64:128, 0:n], ACT.Copy).then_inc(acc_read_act, 1)
                    else:
                        dst = raw[1] if j == 1 else raw[0]
                        act.activation(dst[:, a:a + n], src[:, 0:n], ACT.Copy).then_inc(acc_read_act, 1)
            if proj:
                transposed_v(m, kind)
            nv = len(V_CHUNKS[kind])
            s = 0
            a_i = 0

            def exponentials(steps, g):
                nonlocal s
                for step in steps:
                    act.wait_ge(scores_biased, m["scores_biased"] + s + 1)
                    at = prob_at(g, step)
                    p = prob[0:step.rows, at:at + step.width]
                    act.activation(p, p, ACT.Exp, scale=-1.0, bias=stat[0:step.rows, s % 8:s % 8 + 1],
                                   accum_out=stat[0:step.rows, 8 + s % 8:9 + s % 8]).then_inc(exps_ready, 1)
                    s += 1

            exponentials(groups[0].steps, groups[0])
            if not proj:
                transposed_v(m, kind)
            if side:
                split_weight(wm, r0 + len(proj) + 1, 128 * side[1][0], done)
            for h, g in enumerate(groups):
                for c, chunk in enumerate(g.chunks):
                    act.wait_ge(turned_ready, m["turned_ready"] + nv + a_i + 1)
                    act.wait_ge(pv_done, m["pv_done"] + max(a_i - 1, 0))
                    rects = rectangles(g, chunk)
                    for i, (rows, c0, n) in enumerate(rects):
                        ins = act.activation(pt[0:rows, a_i % 2, 0, c0:c0 + n],
                                             t_ps[(nv + a_i) % 2][0:rows, c0:c0 + n], ACT.Copy)
                    ins.then_inc(turned_hi_made, 1)
                    a_i += 1
                    if h + 1 < len(groups):
                        half = len(groups[h + 1].steps) // 2
                        if c == 0:
                            exponentials(groups[h + 1].steps[:half], groups[h + 1])
                        if c == min(1, len(g.chunks) - 1):
                            exponentials(groups[h + 1].steps[half:], groups[h + 1])
                    for t, sc, i, part, parts in side_slots(kind, h, last)[c]:
                        if part < parts - 1:
                            continue
                        act.wait_ge(acc_ready, m["acc_ready"] + done + i + 1)
                        a, n = side[t][1][sc]
                        if kind in "AB" and sc == 0:
                            if t == 0:
                                act.wait_ge(opnd_lo_made, m["opnd_lo_made"])
                            elif t == 1:
                                act.wait_ge(k_stored, m["k_stored"] + 16)
                            else:
                                act.wait_ge(v_stored, m["v_stored"] + 16)
                        act.activation(side_out(t, a, n), acc[1][:, 0:n], ACT.Copy,
                                       scale=qkv_scale(kind, t)).then_inc(acc_read_act, 1)
                        if sc == len(side[t][1]) - 1 and t + 1 < len(side):
                            wide = 128 * side[t + 2][0] if t + 2 < len(side) else next_wide
                            split_weight(wm, r0 + len(proj) + t + 2, wide, done + i + 1)
                if h == 1 and next_wide and proj and not side:
                    split_weight(wm, r0 + len(proj), next_wide, ends[-2])
            if kind == "B":
                act.wait_ge(acc_read_dve, m["acc_read_dve"] + len(groups))
                act.activation(o_squares, o_tmp[:, 0:TOK], ACT.Square).then_inc(squares_ready, 1)
                act.wait_ge(squares_summed, m["squares_summed"] + 1)
                root(m, token_chunks(TOK, CHUNK_TOK), 128, 1,
                     first=sum(len(chunks) for _, chunks in proj + side))

        act.wait_ge(consts_set, 3)
        act.activation(small[:, 5:7], small[:, 3:5], ACT.Exp).then_inc(consts_set, 1)
        split_weight(fresh(), 0, KT * 128, 0)
        for name, m, o in phases():
            if name == "norm":
                norm(m, o["what"], o.get("layer", 0))
            elif name == "mem":
                def pair_of(mi, first=0):
                    for r in range(2):
                        split_weight(dict(mi), r + 1, KT * 128, r)
                        act.wait_ge(acc_ready, mi["acc_ready"] + r + 1)
                        yield r
                per = dict(w=2, acc_ready=2, acc_read_act=2)
                with act.Fori(0, 8) as it:
                    mi = at_iteration(m, per, it)
                    for r in pair_of(mi):
                        act.activation(mem_kv[:, 2 * it + r, :], acc[r][:, 0:MEMT], ACT.Copy).then_inc(acc_read_act, 1)
            elif name == "gate":
                act.wait_ge(x_stored, m["x_stored"])
                for r in range(2):
                    split_weight(m, r + 1, KT * 128, 3 * r)
                    for c, (a, n) in enumerate(token_chunks(TOK, CHUNK_TOK)):
                        act.wait_ge(acc_ready, m["acc_ready"] + 3 * r + c + 1)
                        act.activation(y_sb[:, 6 + r, a:a + n], acc[(3 * r + c) % 2][:, 0:n],
                                       ACT.Silu).then_inc(acc_read_act, 1)
            elif name == "memory_jobs":
                per = job_counts("M")
                for j in range(2):
                    job(at_iteration(m, per, j), "M", 4 * j, dict(w=m["w"]), KT * 128,
                        lambda t, a, n: y_sb[:, 3 * j + t, a:a + n])
                act.wait_ge(acc_read_act, m["acc_read_act"] + 2 * per["acc_read_act"])
                for t in range(6):
                    act.activation(y_sb[:, t, :], y_sb[:, t, :], ACT.Silu).then_inc(gates_ready, 1)
            elif name == "latents":
                act.wait_ge(acc_read_dve, m["acc_read_dve"])
                for t in range(6):
                    if t < 5:
                        split_weight(m, t + 1, KT * 128, 3 * t)
                    for c, (a, n) in enumerate(token_chunks(TOK, CHUNK_TOK)):
                        act.wait_ge(acc_ready, m["acc_ready"] + 3 * t + c + 1)
                        act.activation(c_tmp[:, t, a:a + n], acc[(3 * t + c) % 2][:, 0:n],
                                       ACT.Copy).then_inc(acc_read_act, 1)
            elif name == "jobs":
                kind = o["kind"]
                per = job_counts(kind)
                if kind == "C":
                    with act.Fori(0, 3) as it:
                        mi = at_iteration(m, o["counts"], it)
                        for u in range(2):
                            job(at_iteration(mi, per, u), kind, 4 * u, dict(w=mi["w"]), 0)
                else:
                    act.wait_ge(acc_read_dve, m["acc_read_dve"])
                    for t in range(3):
                        split_weight(m, t + 1, KT * 128, 3 * t)
                        for c, (a, n) in enumerate(token_chunks(TOK, CHUNK_TOK)):
                            act.wait_ge(acc_ready, m["acc_ready"] + 3 * t + c + 1)
                            act.activation(qkv_out(t, a, n), acc[(3 * t + c) % 2][:, 0:n], ACT.Copy,
                                           scale=qkv_scale(kind, t)).then_inc(acc_read_act, 1)
                    with act.Fori(0, 2) as it:
                        for u in range(2):
                            job(job_start(m, kind, 2 * it + u), kind, 3 * u + 3, dict(w=m["w"] + 6 * it),
                                KT * 128, qkv_out)
                    job(job_start(m, kind, 4), kind, 3, dict(w=m["w"] + 12), KT * 128, qkv_out)
                    job(job_start(m, kind, 5), kind, 0, dict(w=m["w"] + 18), 0, last=True)
                if o["kind"] == "C":
                    after = {k: v + 3 * o["counts"].get(k, 0) for k, v in m.items()}
                    split_weight(after, 0, KT * 128, 0)
            elif name == "out":
                act.wait_ge(acc_read_dve, m["acc_read_dve"])
                for k in range(KT):
                    act.activation(h_v[:, 0, k, :], y_sb[:, k, :], ACT.Copy).then_inc(normed_hi, 1)
                for f in range(KT):
                    if o["w8"] + f + 1 < LAST_W8:
                        split_weight(m, f + 1, KT * 128, 3 * f)

    @block.vector
    def _(dve):
        def normalise(m, what, layer=0):
            _, _, _, steps = norm_plan(what, layer)
            dve.wait_ge(rstd_ready, m["rstd_ready"] + 1)
            for n, (tile, g, hi, _, store) in enumerate(steps):
                w = tile.shape[-1]
                if n >= 2 and hi is not None:
                    dve.wait_ge(normed_lo, m["normed_lo"] + n - 1)
                if n >= 2 and store is not None:
                    dve.wait_ge(normed_stored[n % 2], m[f"normed_stored{n % 2}"] + 16 * (n // 2))
                dve.scalar_tensor_tensor(out=raw[n % 2][:, 0:w], in0=tile, scalar=gains[:, g:g + 1],
                                         in1=rstd[:, 0:w], op0=ALU.mult, op1=ALU.mult).then_inc(normed, 1)

        def rotate(m, own, src, dst, tmp, src_rows=64):
            dve.tensor_tensor(tmp[64:96, 0:TOK], src[96:128, 0:TOK], rope_sb[96:128, :], ALU.mult)
            dve.tensor_tensor(dst[64:96, 0:TOK], src[64:96, 0:TOK], rope_sb[64:96, :], ALU.mult).then_inc(recips_ready, 1)
            dve.wait_ge(recips_ready, own + 1)
            dve.tensor_tensor(dst[64:96, 0:TOK], dst[64:96, 0:TOK], tmp[64:96, 0:TOK], ALU.add).then_inc(recips_ready, 1)
            dve.wait_ge(recips_ready, own + 2)

        def transposed_v(m, kind):
            for v, chunk in enumerate(V_CHUNKS[kind]):
                dve.wait_ge(turned_hi_made, m["turned_hi_made"] + v + 1)
                rows, n, vt = chunk[0][2], len(chunk), chunk[0][0]
                dve.tensor_tensor(v_sp[0:rows, 1, vt:vt + n, :],
                                  t_ps[v % 2][0:rows, 0:128 * n].rearrange("p (n d) -> p n d", d=128),
                                  v_sp[0:rows, 0, vt:vt + n, :].bitcast(F32), ALU.subtract).then_inc(turned_lo_made, 1)

        def q_and_k(cached_k):
            dve.tensor_copy(q_sp[:, 0, :], q_raw[:, 0:TOK]).then_inc(opnd_hi_made, 1)
            dve.wait_ge(kcache_loaded, cached_k)
            dve.tensor_copy(k_sp[:, 0, :], raw[1][:, 0:KEYS]).then_inc(opnd_hi_made, 1)

        def job(m, kind, tile, last=False):
            groups = GROUPS[kind]
            nv = len(V_CHUNKS[kind])
            r_own = m["recips_ready"]
            if kind in "CM":
                dve.wait_ge(acc_read_act, m["acc_read_act"] + 3)
            if kind == "C":
                rotate(m, r_own, raw[0], raw[0], raw[1])
                dve.tensor_copy(q_sp[0:96, 0, :], raw[0][0:96, 0:TOK]).then_inc(opnd_hi_made, 1)
                dve.wait_ge(acc_read_act, m["acc_read_act"] + 6)
                rotate(m, r_own + 2, raw[0], raw[0], raw[1])
                dve.tensor_copy(qo_sp[0:96, 0, :], raw[0][0:96, 0:TOK]).then_inc(opnd_hi_made, 1)
                r_own = r_own + 4
                dve.wait_ge(acc_read_act, m["acc_read_act"] + 10)
                dve.tensor_copy(k_sp[0:64, 0, :], raw[1][0:64, :]).then_inc(opnd_hi_made, 1)
                dve.tensor_copy(ko_v[0:64, 0, :], raw[0][0:64, :]).then_inc(opnd_hi_made, 1)
            elif kind == "M":
                dve.tensor_copy(q_sp[:, 0, :], raw[0][:, 0:TOK]).then_inc(opnd_hi_made, 1)
                dve.wait_ge(kcache_loaded, m["kcache_loaded"] + 32)
                dve.tensor_copy(k_sp[:, 0, 0:2 * MEMT], raw[1][:, 0:2 * MEMT]).then_inc(opnd_hi_made, 1)
            else:
                dve.wait_ge(vcache_loaded, m["vcache_loaded"])
                dve.tensor_copy(v_sp[:, 0, 8:12, :], v_cache[:, :, :]).then_inc(opnd_hi_made, 1)
            if kind in "CM":
                transposed_v(m, kind)
            if kind == "A":
                dve.wait_ge(bias_loaded, m["bias_loaded"] + 16)
                both = bias[:, :].rearrange("p (h k) -> p h k", h=2)
                dve.memset(both[64:128, :, 0:CHUNK], NEG)
                dve.memset(both[0:64, :, BAND - CHUNK:BAND], NEG).then_inc(bias_masked, 1)
            if kind == "B":
                dve.wait_ge(bias_loaded, m["bias_loaded"] + 16)
                dve.tensor_scalar(bias[:, 0:1024], bias[:, 0:1024], slopes[:, bass.ds(tile, 1)], None,
                                  ALU.mult).then_inc(bias_masked, 1)
            if kind in "AB":
                dve.wait_ge(bias_masked, m["bias_masked"] + 1)
            else:
                dve.wait_ge(bias_loaded, m["bias_loaded"])
            ends, total = [], 0
            for g in groups:
                total += len(g.chunks)
                ends.append(total)
            s = 0
            normed = 0
            p_done = 0

            def minima(h, g, steps):
                nonlocal s
                for step in steps:
                    dve.wait_ge(scores_ready, m["scores_ready"] + s + 1)
                    if h >= 2:
                        dve.wait_ge(turned_ready, m["turned_ready"] + nv + ends[h - 2])
                    if step.which and h >= 1:
                        dve.wait_ge(probs_ready, m["probs_ready"] + p_done)
                    settle(dve)
                    at = prob_at(g, step)
                    b0 = step.bias0 + (BAND * step.head if kind == "A" else 0)
                    dve.tensor_tensor_reduce(
                        out=prob[0:step.rows, at:at + step.width],
                        in0=s_ps[s % 2][0:step.rows, 0:step.width],
                        in1=bias[0:step.rows, b0:b0 + step.width] if kind != "M" else bias[0:step.rows, 0:MEMT],
                        scale=-1.0, scalar=3e38, op0=ALU.add, op1=ALU.min,
                        accum_out=stat[0:step.rows, s % 8:s % 8 + 1]).then_inc(scores_biased, 1)
                    s += 1

            def probabilities(g):
                nonlocal normed, p_done
                count = 2 if kind == "B" else 1
                for first in range(0, len(g.steps), count):
                    steps = g.steps[first:first + count]
                    rows, width = steps[0].rows, steps[0].width
                    cols = []
                    for i, step in enumerate(steps):
                        n = normed + i
                        dve.wait_ge(exps_ready, m["exps_ready"] + n + 1)
                        cols.append(stat[0:rows, 16 + n % 8:17 + n % 8])
                        dve.reciprocal(cols[i], stat[0:rows, 8 + n % 8:9 + n % 8]).then_inc(recips_ready, 1)
                    at = prob_at(g, steps[0])
                    p = prob[0:rows, at:at + width]
                    if kind == "B":
                        dve.wait_ge(recips_ready, r_own + normed + count)
                        dve.tensor_scalar(p, p, cols[0], None, ALU.mult)
                        lamr = stat[0:rows, 24 + first // 2:25 + first // 2]
                        dve.tensor_scalar(lamr, cols[1], neg_lam[0:rows, :], None, ALU.mult).then_inc(lambda_recips_ready, 1)
                        b_count[0] = b_count[0] + 1
                        dve.wait_ge(lambda_recips_ready, m["lambda_recips_ready"] + b_count[0])
                        at1 = prob_at(g, steps[1])
                        dve.scalar_tensor_tensor(out=p, in0=prob[0:rows, at1:at1 + width], scalar=lamr, in1=p,
                                                 op0=ALU.mult, op1=ALU.add).then_inc(probs_ready, 1)
                    else:
                        dve.wait_ge(recips_ready, r_own + normed + 1)
                        dve.tensor_scalar(p, p, cols[0], None, ALU.mult).then_inc(probs_ready, 1)
                    normed += count
                    p_done += 1

            b_count = [0]
            half = [len(g.steps) // 2 for g in groups]
            minima(0, groups[0], groups[0].steps)
            if kind == "A":
                minima(1, groups[1], groups[1].steps[:half[1]])
            if kind in "AB":
                transposed_v(m, kind)
            probabilities(groups[0])
            if kind != "A":
                minima(1, groups[1], groups[1].steps[:half[1]])
            a_i = 0
            for h, g in enumerate(groups):
                for i, chunk in enumerate(g.chunks):
                    dve.wait_ge(turned_hi_made, m["turned_hi_made"] + nv + a_i + 1)
                    for rows, c, n in rectangles(g, chunk):
                        ins = dve.tensor_tensor(pt[0:rows, a_i % 2, 1, c:c + n],
                                                t_ps[(nv + a_i) % 2][0:rows, c:c + n],
                                                pt[0:rows, a_i % 2, 0, c:c + n].bitcast(F32), ALU.subtract)
                    ins.then_inc(turned_lo_made, 1)
                    a_i += 1
                    if i == 0 and h + 1 < len(groups):
                        minima(h + 1, groups[h + 1], groups[h + 1].steps[half[h + 1]:])
                if h + 1 < len(groups):
                    probabilities(groups[h + 1])
                if h + 2 < len(groups):
                    minima(h + 2, groups[h + 2], groups[h + 2].steps[:half[h + 2]])
                if kind in "AB" and h + 2 == len(groups) and not last:
                    dve.wait_ge(scores_ready, m["scores_ready"] + s)
                    dve.wait_ge(acc_read_act, m["acc_read_act"] + 6)
                    q_and_k(m["kcache_loaded"] + 16)
                dve.wait_ge(pv_done, m["pv_done"] + ends[h])
                o_ps = acc[output_bank(kind, h)]
                if kind == "B":
                    dve.tensor_copy(o_tmp[:, g.q0:g.q0 + g.qn], o_ps[:, 0:g.qn]).then_inc(acc_read_dve, 1)
                else:
                    r0 = 64 * g.head
                    gate = y_sb[r0:r0 + 64, tile, g.q0:g.q0 + g.qn]
                    dve.tensor_tensor(gate, o_ps[0:64, 0:g.qn], gate, ALU.mult).then_inc(acc_read_dve, 1)
            if kind == "B":
                dve.wait_ge(rstd_ready, m["rstd_ready"] + 1)
                dve.scalar_tensor_tensor(out=o_tmp[:, 0:TOK], in0=o_tmp[:, 0:TOK], scalar=sub_gain,
                                         in1=rstd, op0=ALU.mult, op1=ALU.mult).then_inc(recips_ready, 1)
                dve.wait_ge(recips_ready, m["recips_ready"] + s + 1)
                gate = y_sb[:, tile, :]
                dve.tensor_tensor(gate, o_tmp[:, 0:TOK], gate, ALU.mult).then_inc(acc_read_dve, 1)

        dve.wait_ge(consts_loaded, 16 * 4)
        dve.wait_ge(consts_set, 1)
        for i in range(2):
            dve.tensor_tensor_reduce(out=prob[:, 64 * i:64 * i + 64],
                                     in0=lam[:, 128 * i:128 * i + 64], in1=lam[:, 128 * i + 64:128 * i + 128],
                                     scale=1.0, scalar=0.0, op0=ALU.mult, op1=ALU.add,
                                     accum_out=small[:, 3 + i:4 + i]).then_inc(consts_set, 1)
        dve.wait_ge(consts_set, 4)
        dve.scalar_tensor_tensor(out=neg_lam, in0=small[:, 6:7], scalar=-LAM_INIT, in1=small[:, 5:6],
                                 op0=ALU.add, op1=ALU.subtract).then_inc(consts_set, 1)
        dve.tensor_scalar(sub_gain, gains[:, G_SUB:G_SUB + 1], 1.0 - LAM_INIT, None, ALU.mult).then_inc(consts_set, 1)
        dve.wait_ge(consts_set, 6)
        for name, m, o in phases():
            if name == "norm":
                normalise(m, o["what"], o.get("layer", 0))
            elif name == "memory_jobs":
                per = job_counts("M")
                mb = dict(m, bias_loaded=m["bias_loaded"] + 16)
                for j in range(2):
                    job(at_iteration(mb, per, j), "M", 6 + j)
            elif name == "latents":
                dve.wait_ge(acc_read_act, m["acc_read_act"] + 18)
                dve.wait_ge(kcache_loaded, m["kcache_loaded"] + 48)
                dve.tensor_copy(lat_v[:, 0, :, TOK:KEYS], c_cache[:, :, :]).then_inc(opnd_hi_made, 1)
            elif name == "key_rope":
                dve.wait_ge(normed_stored[0], m["normed_stored0"])
                dve.wait_ge(normed_stored[1], m["normed_stored1"])
                dve.wait_ge(normed_lo, m["normed_lo"])
                rotate(m, m["recips_ready"], c_tmp[:, 5, :], raw[1], raw[0])
                dve.tensor_copy(k_sp[64:96, 0, :], raw[1][64:96, :]).then_inc(opnd_hi_made, 1)
                dve.tensor_copy(ko_v[64:96, 0, :], raw[1][64:96, :]).then_inc(opnd_hi_made, 1)
                dve.wait_ge(opnd_hi_made, m["opnd_hi_made"] + 2)
                for keys in (k_sp, ko_v):
                    dve.tensor_tensor(keys[64:96, 1, :], raw[1][64:96, :], keys[64:96, 0, :].bitcast(F32),
                                      ALU.subtract).then_inc(opnd_hi_made, 1)
            elif name == "jobs":
                per = job_counts(o["kind"])
                dve.wait_ge(gates_ready, m["gates_ready"])
                if o["kind"] == "C":
                    with dve.Fori(0, 3) as it:
                        mi = at_iteration(m, o["counts"], it)
                        for u in range(2):
                            job(at_iteration(mi, per, u), "C", 2 * it + u)
                else:
                    kind = o["kind"]
                    dve.wait_ge(acc_read_act, m["acc_read_act"] + 6)
                    q_and_k(m["kcache_loaded"] + 16)
                    with dve.Fori(0, 2) as it:
                        for u in range(2):
                            job(job_start(m, kind, 2 * it + u), kind, 2 * it + u)
                    job(job_start(m, kind, 4), kind, 4)
                    job(job_start(m, kind, 5), kind, 5, last=True)
            elif name == "out":
                for k in range(KT):
                    dve.wait_ge(normed_hi, m["normed_hi"] + k + 1)
                    dve.tensor_tensor(h_v[:, 1, k, :], y_sb[:, k, :], h_v[:, 0, k, :].bitcast(F32),
                                      ALU.subtract).then_inc(normed, 1)
                for f in range(KT):
                    dve.wait_ge(xt_in[f], 16 * (o["layer"] + 1))
                    for c, (a, n) in enumerate(token_chunks(TOK, CHUNK_TOK)):
                        dve.wait_ge(acc_ready, m["acc_ready"] + 3 * f + c + 1)
                        x = y_sb[:, f, a:a + n]
                        dve.tensor_tensor(x, acc[(3 * f + c) % 2][:, 0:n], x, ALU.add).then_inc(acc_read_dve, 1)

    @block.gpsimd
    def _(pool):
        def split_weight(m, r, wide):
            pool.wait_ge(whi_made, m["w"] + r + 1)
            pool.tensor_tensor(w_lo[:, r % 2, 0:wide], w_raw[:, r % 2, 0:wide],
                               w_hi[:, r % 2, 0:wide].bitcast(F32), ALU.subtract).then_inc(wlo_made, 1)

        def low(m, i, out, x, hi):
            pool.wait_ge(opnd_hi_made, m["opnd_hi_made"] + i + 1)
            pool.tensor_tensor(out, x, hi.bitcast(F32), ALU.subtract).then_inc(opnd_lo_made, 1)

        def q_and_k(m, i):
            low(m, i, q_sp[:, 1, :], q_raw[:, 0:TOK], q_sp[:, 0, :])
            low(m, i + 1, k_sp[:, 1, :], raw[1][:, :], k_sp[:, 0, :])

        def job(m, kind, r0, w, next_wide, last=False):
            proj = JOB_PROJ[kind]
            wm = dict(m, w=w)
            if kind in "AB":
                low(m, 0, v_sp[:, 1, 8:12, :], v_cache[:, :, :], v_sp[:, 0, 8:12, :])
                if not last:
                    for t in (1, 2, 3):
                        split_weight(wm, r0 + t, KT * 128)
                    q_and_k(m, 1)
                return
            if kind == "C":
                split_weight(wm, r0, 384)
            for j in range(len(proj)):
                if j + 1 < len(proj):
                    split_weight(wm, r0 + j + 1, 128 * proj[j + 1][0])
                if kind == "C":
                    if j == 0:
                        low(m, 0, q_sp[0:96, 1, :], raw[0][0:96, 0:TOK], q_sp[0:96, 0, :])
                    elif j == 1:
                        low(m, 1, qo_sp[0:96, 1, :], raw[0][0:96, 0:TOK], qo_sp[0:96, 0, :])
                    elif j == 2:
                        low(m, 2, k_sp[0:64, 1, :], raw[1][0:64, :], k_sp[0:64, 0, :])
                        low(m, 3, ko_v[0:64, 1, :], raw[0][0:64, :], ko_v[0:64, 0, :])
                elif j == 0:
                    low(m, 0, q_sp[:, 1, :], raw[0][:, 0:TOK], q_sp[:, 0, :])
            if kind == "M":
                low(m, 1, k_sp[:, 1, 0:2 * MEMT], raw[1][:, 0:2 * MEMT], k_sp[:, 0, 0:2 * MEMT])
            for t, (kt, _) in enumerate(SIDE_PROJ[kind]):
                split_weight(wm, r0 + len(proj) + t, 128 * kt)
            if next_wide:
                split_weight(wm, r0 + len(proj) + len(SIDE_PROJ[kind]), next_wide)

        pool.memset(ones[:, :], 1.0)
        pool.memset(eps_sb, EPS).then_inc(consts_set, 1)
        pool.wait_ge(consts_loaded, 16 * 4)
        split_weight(fresh(), 0, KT * 128)
        for name, m, o in phases():
            if name == "norm":
                _, _, _, steps = norm_plan(o["what"], o.get("layer", 0))
                for n, (tile, _, hi, lo, _) in enumerate(steps):
                    if hi is not None:
                        pool.wait_ge(normed_hi, m["normed_hi"] + n + 1)
                        pool.tensor_tensor(lo, raw[n % 2][:, 0:tile.shape[-1]], hi.bitcast(F32),
                                           ALU.subtract).then_inc(normed_lo, 1)
            elif name in ("mem", "gate"):
                with pool.Fori(0, 8 if name == "mem" else 1) as it:
                    mi = dict(m, w=m["w"] + 2 * it)
                    for r in range(2):
                        split_weight(mi, r + 1, KT * 128)
            elif name == "memory_jobs":
                per = job_counts("M")
                for j in range(2):
                    job(at_iteration(m, per, j), "M", 4 * j, m["w"], KT * 128)
            elif name == "latents":
                for t in range(5):
                    split_weight(m, t + 1, KT * 128)
                low(m, 0, lat_v[:, 1, :, TOK:KEYS], c_cache[:, :, :], lat_v[:, 0, :, TOK:KEYS])
            elif name == "jobs":
                kind = o["kind"]
                per = job_counts(kind)
                if kind == "C":
                    with pool.Fori(0, 3) as it:
                        mi = at_iteration(m, o["counts"], it)
                        for u in range(2):
                            job(at_iteration(mi, per, u), kind, 4 * u, mi["w"], 0)
                else:
                    for t in (1, 2, 3):
                        split_weight(m, t, KT * 128)
                    q_and_k(m, 0)
                    with pool.Fori(0, 2) as it:
                        for u in range(2):
                            job(job_start(m, kind, 2 * it + u), kind, 3 * u + 3, m["w"] + 6 * it, KT * 128)
                    job(job_start(m, kind, 4), kind, 3, m["w"] + 12, KT * 128)
                    job(job_start(m, kind, 5), kind, 0, 0, 0, last=True)
                if o["kind"] == "C":
                    split_weight(dict(m, w=m["w"] + 3 * o["counts"]["w"]), 0, KT * 128)
            elif name == "out":
                for f in range(KT):
                    if o["w8"] + f + 1 < LAST_W8:
                        split_weight(m, f + 1, KT * 128)

    @block.tensor
    def _(pe):
        def project(m, r, kt, chunks, moving, done, freed, freed_before):
            pe.wait_ge(wlo_made, m["w"] + r + 1)
            for a, n in chunks:
                if done >= 2:
                    pe.wait_ge(freed, freed_before + done - 1)
                out = acc[done % 2][:, 0:n]
                for k in range(kt):
                    for i, (ws, xs) in enumerate(PASSES):
                        w = (w_hi, w_lo)[ws][:, r % 2, 128 * k:128 * k + 128]
                        ins = pe.matmul(out, w, moving(xs, k, a, n), start=k == 0 and i == 0,
                                        stop=k == kt - 1 and i == 2)
                ins.then_inc(acc_ready, 1)
                done += 1
            return done

        def banks_free(m):
            pe.wait_ge(acc_read_act, m["acc_read_act"])
            pe.wait_ge(acc_read_dve, m["acc_read_dve"])
            pe.wait_ge(turned_lo_made, m["turned_lo_made"])

        def sums(m, k, squares, chunks, first, last):
            pe.wait_ge(squares_ready, m["squares_ready"] + k + 1)
            for c, (a, n) in enumerate(chunks):
                ins = pe.matmul(sum_banks[c][:, 0:n], ones[:, :], squares[:, a:a + n], start=first, stop=last)
            ins.then_inc(squares_summed, 1)

        def side_part(m, kind, r, done, t, c, number, part, parts):
            kt, chunks = SIDE_PROJ[kind][t]
            a, n = chunks[c]
            passes = [(k, i) for k in range(kt) for i in range(3)]
            if part == 0:
                pe.wait_ge(wlo_made, m["w"] + r + t + 1)
                pe.wait_ge(acc_read_act, m["acc_read_act"] + done + number)
            for k, i in passes[len(passes) * part // parts:len(passes) * (part + 1) // parts]:
                ws, xs = PASSES[i]
                w = (w_hi, w_lo)[ws][:, (r + t) % 2, 128 * k:128 * k + 128]
                ins = pe.matmul(acc[1][:, 0:n], w, h_v[:, xs, k, a:a + n], start=k == 0 and i == 0,
                                stop=k == kt - 1 and i == 2)
            if part == parts - 1:
                ins.then_inc(acc_ready, 1)

        def job(m, kind, r0, w, last=False):
            groups, proj, v_chunks = GROUPS[kind], JOB_PROJ[kind], V_CHUNKS[kind]
            wm = dict(m, w=w)
            if proj:
                banks_free(m)
            done = 0
            for j, (kt, chunks) in enumerate(proj):
                if kind == "C":
                    src = cq_v if j < 2 else lat_v
                else:
                    src = h_v
                done = project(wm, r0 + j, kt, chunks, lambda s_, k, a, n: src[:, s_, k, a:a + n], done, acc_read_act, m["acc_read_act"])
            nv = len(v_chunks)

            def transposed_v():
                for v, chunk in enumerate(v_chunks):
                    if v == 0:
                        if kind == "M":
                            pe.wait_ge(vcache_loaded, m["vcache_loaded"] + 32)
                        pe.wait_ge(acc_read_act, m["acc_read_act"] + done)
                        pe.wait_ge(acc_read_dve, m["acc_read_dve"] - (kind == "B"))
                        pe.wait_ge(turned_lo_made, m["turned_lo_made"])
                    if v >= 2:
                        pe.wait_ge(turned_lo_made, m["turned_lo_made"] + v - 1)
                    for i, (_, col, n) in enumerate(chunk):
                        ins = pe.transpose(t_ps[v % 2][0:n, 128 * i:128 * i + 128], raw[0][:, col:col + n], ident[:, :])
                    ins.then_inc(turned_ready, 1)

            if proj:
                transposed_v()
                pe.wait_ge(opnd_lo_made, m["opnd_lo_made"] + N_SPLITS[kind])
            else:
                pe.wait_ge(opnd_lo_made, m["opnd_lo_made"])
                pe.wait_ge(scores_biased, m["scores_biased"])
            s = 0

            def scores(g):
                nonlocal s
                for step in g.steps:
                    if s >= 2:
                        pe.wait_ge(scores_biased, m["scores_biased"] + s - 1)
                    if kind == "C":
                        rows = slice(0, 96)
                        q_v, k_v = (qo_sp, ko_v) if step.head else (q_sp, k_sp)
                    else:
                        x = step.which if kind == "B" else step.head
                        rows = slice(64 * x, 64 * x + 64)
                        q_v, k_v = q_sp, k_sp
                    if step.rows == DEC:
                        settle(pe)
                    for key, col, n in step.segs:
                        for i, (qs, ks) in enumerate(PASSES):
                            ins = pe.matmul(s_ps[s % 2][0:step.rows, col:col + n],
                                            q_v[rows, qs, step.q0:step.q0 + step.rows],
                                            k_v[rows, ks, key:key + n], start=i == 0, stop=i == 2)
                    ins.then_inc(scores_ready, 1)
                    s += 1

            a_i = 0
            steps_of = 0
            p_done = 0
            ends, total = [], 0
            for g in groups:
                total += 1 + (g.qn > DEC)
                ends.append(total)

            def turn(g, chunk, a):
                tv = nv + a
                if tv >= 2:
                    pe.wait_ge(turned_lo_made, m["turned_lo_made"] + tv - 1)
                if g.qn == DEC:
                    settle(pe)
                for i, vt, n, cols in chunk:
                    for t, col in enumerate(cols):
                        if col is None:
                            continue
                        step = g.steps[t * (2 if kind == "B" else 1)]
                        at = prob_at(g, step) + col
                        to = DEC * i if g.qn == DEC else 256 * i + 128 * t
                        ins = pe.transpose(t_ps[tv % 2][0:n, to:to + step.rows],
                                           prob[0:step.rows, at:at + n], ident[0:step.rows, 0:step.rows])
                ins.then_inc(turned_ready, 1)

            def times_v(g, h, chunk, a, first, last):
                pe.wait_ge(turned_lo_made, m["turned_lo_made"] + nv + a + 1)
                if first and kind in "AB" and g.qn == DEC:
                    pe.wait_ge(opnd_lo_made, m["opnd_lo_made"] + 1)
                if first and (h >= 2 or (h and SIDE_PROJ[kind])):
                    pe.wait_ge(acc_read_dve, m["acc_read_dve"] + h - (0 if SIDE_PROJ[kind] else 1))
                width = 128 if kind == "B" else 64
                c0 = 0 if kind == "B" else 64 * g.head
                for x, (i, vt, n, cols) in enumerate(chunk):
                    if g.qn == DEC:
                        src, dst, w_ = DEC * i, 0, DEC
                    else:
                        t0 = 0 if cols[0] is not None else 1
                        w_ = 128 * sum(c is not None for c in cols)
                        src, dst = 256 * i + 128 * t0, 128 * t0
                    for y, (vs, ps) in enumerate(PASSES):
                        ins = pe.matmul(acc[output_bank(kind, h)][0:width, dst:dst + w_], v_sp[0:n, vs, vt, c0:c0 + width],
                                        pt[0:n, a % 2, ps, src:src + w_],
                                        start=first and x == 0 and y == 0,
                                        stop=last and x == len(chunk) - 1 and y == 2)
                ins.then_inc(pv_done, 1)

            scores(groups[0])
            if kind != "B":
                scores(groups[1])
            if not proj:
                transposed_v()
            if kind == "B":
                scores(groups[1])
            turned = []
            for h, g in enumerate(groups):
                pe.wait_ge(probs_ready, m["probs_ready"] + ends[h])
                n = len(g.chunks)
                for c in range(n):
                    turn(g, g.chunks[c], a_i + c)
                    turned.append((g, h, g.chunks[c], a_i + c, c == 0, c == n - 1))
                    if c == n - 1 and h + 2 < len(groups):
                        scores(groups[h + 2])
                    for t, sc, number, part, parts in side_slots(kind, h, last)[c]:
                        side_part(wm, kind, r0 + len(proj), done, t, sc, number, part, parts)
                    if len(turned) > 1:
                        times_v(*turned.pop(0))
                times_v(*turned.pop(0))
                a_i += n
            if kind == "B":
                sums(m, 0, o_squares, token_chunks(TOK, CHUNK_TOK), True, True)

        pe.wait_ge(consts_loaded, 16 * 4)
        pe.wait_ge(consts_set, 1)
        for name, m, o in phases():
            if name == "norm":
                tiles, _, chunks, _ = norm_plan(o["what"], o.get("layer", 0))
                banks_free(m)
                for k in range(len(tiles)):
                    sums(m, k, raw[k % 2], chunks, k == 0, k == len(tiles) - 1)
            elif name == "mem":
                banks_free(m)
                pe.wait_ge(normed_lo, m["normed_lo"])
                for n in range(16):
                    layer = n // 4
                    project(m, n, KT, [(0, MEMT)],
                            lambda s_, k, a, w: memh_v[:, s_, (8 * layer + k) * MEMT:(8 * layer + k + 1) * MEMT],
                            n, acc_read_act, m["acc_read_act"])
            elif name == "gate":
                pe.wait_ge(normed_lo, m["normed_lo"])
                banks_free(m)
                done = 0
                for r in range(2):
                    done = project(m, r, KT, token_chunks(TOK, CHUNK_TOK),
                                   lambda s_, k, a, n: h_v[:, s_, k, a:a + n], done, acc_read_act, m["acc_read_act"])
            elif name == "memory_jobs":
                per = job_counts("M")
                for j in range(2):
                    job(at_iteration(m, per, j), "M", 4 * j, m["w"])
            elif name == "latents":
                banks_free(m)
                done = 0
                for t in range(6):
                    done = project(m, t, KT, token_chunks(TOK, CHUNK_TOK),
                                   lambda s_, k, a, n: h_v[:, s_, k, a:a + n], done, acc_read_act, m["acc_read_act"])
            elif name == "jobs":
                kind = o["kind"]
                per = job_counts(kind)
                if kind == "C":
                    pe.wait_ge(normed_lo, m["normed_lo"])
                    pe.wait_ge(opnd_lo_made, m["opnd_lo_made"])
                    pe.wait_ge(opnd_hi_made, m["opnd_hi_made"])
                    with pe.Fori(0, 3) as it:
                        mi = at_iteration(m, o["counts"], it)
                        for u in range(2):
                            job(at_iteration(mi, per, u), kind, 4 * u, mi["w"])
                else:
                    banks_free(m)
                    done = 0
                    for t in range(3):
                        done = project(m, t, KT, token_chunks(TOK, CHUNK_TOK),
                                       lambda s_, k, a, n: h_v[:, s_, k, a:a + n], done, acc_read_act, m["acc_read_act"])
                    with pe.Fori(0, 2) as it:
                        for u in range(2):
                            job(job_start(m, kind, 2 * it + u), kind, 3 * u + 3, m["w"] + 6 * it)
                    job(job_start(m, kind, 4), kind, 3, m["w"] + 12)
                    job(job_start(m, kind, 5), kind, 0, 0, last=True)
            elif name == "out":
                banks_free(m)
                pe.wait_ge(normed, m["normed"] + KT)
                done = 0
                for f in range(KT):
                    done = project(m, f, KT, token_chunks(TOK, CHUNK_TOK),
                                   lambda s_, k, a, n: h_v[:, s_, k, a:a + n], done, acc_read_dve, m["acc_read_dve"])

    ctx.close()


def _feature_tiles(x):
    t, f = x.shape
    return x.T.reshape(f // 128, 128, t).transpose(1, 0, 2)


def _weight_tile(w, columns):
    k = w.shape[0] // 128
    return w[:, columns].reshape(k, 128, 128).transpose(1, 0, 2).reshape(128, k * 128)


def _constants():
    q = np.arange(128)[:, None]
    j = np.arange(1024)[None, :]
    hidden = (j - 896) // CHUNK > q // CHUNK
    dist = np.where(hidden, NEG, -np.abs(896 + q - j)).astype(np.float32)
    cmask = np.where(hidden, NEG, 0.0).astype(np.float32)
    half = ROPE // 2
    inv = np.exp(np.float32(-math.log(10000.0)) * np.arange(half, dtype=np.float32) * np.float32(2.0)
                 / np.float32(ROPE)).astype(np.float32)
    pos = np.concatenate([np.arange(SEQ), PAST + np.arange(DEC)]).astype(np.float32)
    ang = (inv[:, None] * pos[None, :]).astype(np.float32)
    rope = np.zeros((128, TOK), np.float32)
    rope[64:96] = np.concatenate([np.cos(ang), np.cos(ang)])
    rope[96:128] = np.concatenate([-np.sin(ang), np.sin(ang)])
    slopes = np.exp2(-8.0 * np.arange(1, 7, dtype=np.float32) / 6).astype(np.float32)
    return dict(ident=np.eye(128, dtype=np.float32), dist=dist, cmask=cmask, rope=rope,
                slopes=np.ascontiguousarray(np.broadcast_to(slopes, (128, 6))))


def kernel(**inputs):
    import numpy as np
    import concourse.bacc as bacc
    from concourse.bass_utils import run_bass_kernel_spmd

    a = {k: np.asarray(v) for k, v in inputs.items()}
    sizes = {"A": 768, "B": 768}
    w_in = [a["w_in_a"][0], a["w_in_b"][0], a["w_in_c"][0], a["w_in_a"][1]]
    cols = lambda first: slice(first, first + 128)
    w8 = []
    for layer in range(DEPTH):
        w8 += [_weight_tile(a["w_mem_kv"][layer], cols(128 * t)) for t in range(4)]
    swapped = np.r_[ROPE // 2:ROPE, 0:ROPE // 2]
    for layer, kind in enumerate(KINDS):
        w = w_in[layer]
        n_mix = w.shape[1] - 256 - D
        gate = lambda first, last: [_weight_tile(w, cols(n_mix + 256 + 128 * t)) for t in range(first, last)]
        memory_q = lambda t: [_weight_tile(w, cols(n_mix + 128 * t))]
        w8 += gate(6, 8) + memory_q(0) + gate(0, 3) + memory_q(1) + gate(3, 6)
        if kind == "C":
            w8 += [_weight_tile(w, cols(128 * t)) for t in range(5)]
            kr = w[:, Q_LORA + KV_LORA:n_mix]
            w8.append(_weight_tile(np.concatenate([np.zeros((D, 64), w.dtype), kr, kr[:, swapped]], axis=1), cols(0)))
        else:
            w8 += [_weight_tile(w, cols(768 * part + 128 * t)) for t in range(6) for part in range(3)]
        w8 += [_weight_tile(a["w_out"][layer], cols(128 * t)) for t in range(KT)]
    uq = a["w_uq_c"][0].reshape(Q_LORA, 12, 96)
    uq = np.concatenate([uq, uq[:, :, 64 + swapped]], axis=2)
    ukv = a["w_ukv_c"][0].reshape(KV_LORA, 6, 2, 2, 64)
    col = lambda x: x.reshape(-1, 128).T
    rel = a["rel_bias_a"].transpose(0, 2, 1)
    c = _constants()
    k_cols = lambda x: x.reshape(x.shape[0], 6, 128).transpose(1, 2, 0)
    v_rows = lambda x: x.reshape(4, 128, 6, 128).transpose(2, 1, 0, 3)
    arrays = dict(
        x_in=_feature_tiles(np.concatenate([a["x_prompt"][0], a["x_sample"][0]])),
        mem_in=_feature_tiles(a["mem_prompt"][0]),
        w8=np.stack(w8),
        wc_q=np.stack([_weight_tile(uq[:, h], cols(0)) for h in range(12)]),
        wc_kv=np.stack([_weight_tile(ukv[:, p, :, part].reshape(KV_LORA, 128), cols(0))
                        for p in range(6) for part in range(2)]),
        gains_in=np.concatenate([col(a["norm_g"]), col(a["final_g"]), col(a["mem_norm_g"]), col(a["subln_g_b"]),
                                 col(a["q_norm_g_c"]), col(a["kv_norm_g_c"])], axis=1),
        lambda_in=a["lambda_b"].reshape(256),
        rel_in=rel[:, :, np.minimum(639 - np.arange(768), 128) + 128],
        kcache=np.concatenate([k_cols(a["cache_a_k"][0, 0]), k_cols(a["cache_b_k"][0, 0]), k_cols(a["cache_a_k"][1, 0])]),
        vcache=np.concatenate([v_rows(a["cache_a_v"][0, 0]), v_rows(a["cache_b_v"][0, 0]), v_rows(a["cache_a_v"][1, 0])]),
        lat_cache=_feature_tiles(a["cache_c_lat"][0, 0]),
        rope_cache=a["cache_c_rope"][0, 0].T,
        memk_cache=a["cache_mem_k"].reshape(DEPTH, MEMT, 2, 128).transpose(0, 2, 3, 1),
        memv_cache=a["cache_mem_v"].reshape(DEPTH, MEMT, 2, 128).transpose(0, 2, 3, 1),
        ident_in=c["ident"], dist_in=c["dist"], cmask_in=c["cmask"], rope_in=c["rope"], slope_in=c["slopes"])
    outs = dict(y_out=(D, TOK), k_a=(2, 6, 128, PAST + DEC), v_a=(2, 6, 128, PAST + DEC), k_b=(6, 128, TOK),
                v_b=(6, 128, TOK), lat_out=(KV_LORA, TOK), rope_out=(ROPE, TOK), memkv_out=(128, 16, MEMT))
    nc = bacc.Bacc("TRN2", target_bir_lowering=False, num_devices=1, dynamic_dma_scratch_size=1024)
    aps = {}
    for name in list(arrays):
        arrays[name] = np.ascontiguousarray(arrays[name])
        aps[name] = nc.dram_tensor(name, arrays[name].shape, F32, kind="ExternalInput").ap()
    for name, shape in outs.items():
        aps[name] = nc.dram_tensor(name, shape, F32, kind="ExternalOutput").ap()
    aps["x_scr"] = [nc.dram_tensor(f"x_scr{i}", (128, KT, TOK), F32, kind="Internal").ap() for i in range(DEPTH - 1)]
    aps["rel_scr"] = nc.dram_tensor("rel_scr", (12, 2, 128, BAND), F32, kind="Internal").ap()
    encoder(nc, **aps)
    r = run_bass_kernel_spmd(nc, [arrays], core_ids=[0]).results[0]
    y = r["y_out"].T
    back = lambda x: x.reshape(-1, x.shape[-1]).T
    k_a, v_a = (np.stack([back(r[n][j]) for j in range(2)]) for n in ("k_a", "v_a"))
    k_b, v_b = back(r["k_b"]), back(r["v_b"])
    lat, rope = r["lat_out"].T, r["rope_out"].T
    mem = r["memkv_out"].reshape(128, DEPTH, 2, 2, MEMT).transpose(1, 2, 4, 3, 0).reshape(DEPTH, 2, 1, MEMT, 4, 64)
    heads = lambda x, *shape: x.reshape(x.shape[0], 1, x.shape[1], *shape)
    return (y[None, :SEQ], y[None, SEQ:],
            heads(k_a[:, :PAST], 12, 64), heads(v_a[:, :PAST], 12, 64),
            heads(k_a[:, PAST:], 12, 64), heads(v_a[:, PAST:], 12, 64),
            heads(k_b[None, :SEQ], 6, 2, 64), heads(v_b[None, :SEQ], 6, 128),
            heads(k_b[None, SEQ:], 6, 2, 64), heads(v_b[None, SEQ:], 6, 128),
            lat[None, None, :SEQ], rope[None, None, :SEQ], lat[None, None, SEQ:], rope[None, None, SEQ:],
            mem[:, 0], mem[:, 1])
```

```python
import math
from contextlib import ExitStack

import numpy as np

import concourse.bass as bass
from concourse import mybir

F32 = mybir.dt.float32
F32R = mybir.dt.float32r
ALU = mybir.AluOpType
ACT = mybir.ActivationFunctionType

D = 1024
KT = D // 128
SEQ, DEC, PAST = 1024, 32, 512
TOK = SEQ + DEC
KEYS = TOK + PAST
MEMT = 256
CHUNK_TOK = TOK // 3
CHUNK_KEY = KEYS // 4
DEPTH, CHUNK = 4, 64
BAND = 640
EPS = 1e-6
NEG = -1e30
Q_LORA, KV_LORA, ROPE = 384, 256, 32
SCALE_64 = 64.0 ** -0.5
SCALE_C = 96.0 ** -0.5
KINDS = "ABCA"
LAM_INIT = 0.8 - 0.6 * math.exp(-0.3 * 1)
PASSES = ((0, 0), (0, 1), (1, 0))
G_NORM, G_FINAL, G_MEM, G_SUB, G_Q, G_KV = 0, 32, 40, 72, 73, 76
N_GAINS = 78


class Step:

    def __init__(self, head, tile, which, q0, rows, segs, bias0):
        self.head, self.tile, self.which = head, tile, which
        self.q0, self.rows, self.segs, self.bias0 = q0, rows, segs, bias0
        self.width = segs[-1][1] + segs[-1][2]


class Group:

    def __init__(self, head, parity, steps, chunks, q0, qn):
        self.head, self.parity, self.steps = head, parity, steps
        self.chunks, self.q0, self.qn = chunks, q0, qn


def key_segments(first, count):
    return [(first + a, a, min(512, count - a)) for a in range(0, count, 512)]


def groups_of(kind):
    out = []
    for head in range(1 if kind == "B" else 2):
        for n, g in enumerate([0, 1, 2, 3, 4] if head == 0 else [1, 0, 3, 2, 4]):
            parity = (5 * head + n) % 2
            whiches = (0, 1) if kind == "B" else (0,)
            if g == 4:
                if kind == "M":
                    segs, keys = [(MEMT, 0, MEMT)], [(2, 128), (3, 128)]
                else:
                    segs = [(TOK, 0, PAST), (SEQ, PAST, DEC)]
                    keys = [(8 + i, 128) for i in range(4)] + [(12, DEC)]
                bias0 = {"A": 0, "B": 384, "C": 0, "M": 0}[kind]
                steps = [Step(head, 0, w, SEQ, DEC, segs, bias0) for w in whiches]
                chunks = [[(i, vt, n_k, (i * 128,)) for i, (vt, n_k) in enumerate(keys)]]
                out.append(Group(head, parity, steps, chunks, SEQ, DEC))
                continue
            steps, starts = [], []
            for i in range(2):
                t = 2 * g + i
                if kind == "M":
                    k0, count, bias0 = 0, MEMT, 0
                elif kind == "A":
                    k0 = max(0, t - 4)
                    count, bias0 = (t + 1 - k0) * 128, 128 * (4 - min(t, 4))
                else:
                    k0, count, bias0 = 0, (t + 1) * 128, 128 * (7 - t)
                starts.append((k0, k0 + count // 128))
                steps += [Step(head, i, w, 128 * t, 128, key_segments(128 * k0, count), bias0)
                          for w in whiches]
            tiles = [(vt, tuple((vt - a) * 128 if a <= vt < b else None for a, b in starts))
                     for vt in range(starts[0][0], starts[1][1])]
            chunks = []
            for c in range(0, len(tiles), 2):
                chunk = [(i, vt, 128, cols) for i, (vt, cols) in enumerate(tiles[c:c + 2])]
                chunks.append(sorted(chunk, key=lambda x: None in x[3]))
            out.append(Group(head, parity, steps, chunks, 256 * g, 256))
    return out


GROUPS = {k: groups_of(k) for k in "ABCM"}
V_CHUNKS = {
    "A": [[(4 * c + i, 512 * c + 128 * i, 128) for i in range(4)] for c in range(2)] + [[(12, SEQ, DEC)]],
    "M": [[(i, 128 * i, 128) for i in range(4)]],
}
V_CHUNKS["B"] = V_CHUNKS["A"]
V_CHUNKS["C"] = V_CHUNKS["A"] + [[(8 + i, TOK + 128 * i, 128) for i in range(4)]]


def rectangles(group, chunk):
    if group.qn == DEC:
        full = [x for x in chunk if x[2] == 128]
        rest = [x for x in chunk if x[2] != 128]
        return [(128, 0, DEC * len(full))] + [(n, DEC * i, DEC) for i, _, n, _ in rest]
    found = []
    for i, _, _, cols in sorted(chunk):
        for t in range(2):
            at = 256 * i + 128 * t
            if cols[t] is None:
                continue
            if found and found[-1][1] + found[-1][2] == at:
                found[-1] = (128, found[-1][1], found[-1][2] + 128)
            else:
                found.append((128, at, 128))
    return found


def token_chunks(total, size):
    return [(a, min(size, total - a)) for a in range(0, total, size)]


JOB_PROJ = {
    "A": [],
    "M": [(KT, token_chunks(TOK, CHUNK_TOK))],
    "C": [],
}
JOB_PROJ["B"] = JOB_PROJ["A"]
QKV = [(KT, token_chunks(TOK, CHUNK_TOK))] * 3
SIDE_PROJ = {"A": QKV, "B": QKV, "M": QKV,
             "C": [(3, token_chunks(TOK, CHUNK_TOK)), (3, token_chunks(TOK, TOK // 4))]
             + [(2, token_chunks(KEYS, CHUNK_KEY))] * 2}
N_SPLITS = {"A": 3, "B": 3, "C": 4, "M": 2}


EARLY = {"A": 0, "B": 0, "C": 0, "M": 2}


def side_chunks(kind, h, last=False):
    if last:
        return []
    listed = [(t, c) for t, (_, chunks) in enumerate(SIDE_PROJ[kind]) for c in range(len(chunks))]
    n, early = len(GROUPS[kind]), EARLY[kind]
    listed = listed[early:]
    first, last = -(-len(listed) * h // n), -(-len(listed) * (h + 1) // n)
    return [(t, c, early + first + i) for i, (t, c) in enumerate(listed[first:last])]


def side_slots(kind, h, last=False):
    n, listed = len(GROUPS[kind][h].chunks), side_chunks(kind, h, last)
    slots, out = list(range(n)), [[] for _ in range(n)]
    for i, chunk in enumerate(listed):
        own = slots[len(slots) * i // len(listed):len(slots) * (i + 1) // len(listed)]
        own = own or [slots[len(slots) * i // len(listed)]]
        for part, c in enumerate(own):
            out[c].append((*chunk, part, len(own)))
    return out


def output_bank(kind, h):
    return 0 if SIDE_PROJ[kind] else h % 2


def job_counts(kind):
    groups = GROUPS[kind]
    proj = sum(len(c) for _, c in JOB_PROJ[kind])
    att = sum(len(g.chunks) for g in groups)
    v = len(V_CHUNKS[kind])
    steps = sum(len(g.steps) for g in groups)
    proj += sum(len(c) for _, c in SIDE_PROJ[kind])
    c = dict(w=len(JOB_PROJ[kind]) + len(SIDE_PROJ[kind]), acc_ready=proj, acc_read_act=proj,
             acc_read_dve=len(groups), opnd_hi_made=N_SPLITS[kind],
             opnd_lo_made=N_SPLITS[kind], turned_ready=v + att, turned_hi_made=v + att, turned_lo_made=v + att, pv_done=att,
             scores_ready=steps, scores_biased=steps, exps_ready=steps, recips_ready=steps,
             probs_ready=sum(1 + (g.qn > DEC) for g in groups))
    if kind in "AB":
        c.update(kcache_loaded=16, vcache_loaded=16, bias_loaded=16, bias_masked=1, k_stored=16, v_stored=16)
    if kind == "M":
        c.update(kcache_loaded=32, vcache_loaded=32)
    if kind == "B":
        c.update(acc_read_act=proj + 3, acc_read_dve=len(groups) + 1, squares_ready=1, squares_summed=1, rstd_ready=1, recips_ready=steps + 1,
                 lambda_recips_ready=steps // 2)
    if kind == "C":
        c.update(rotated=4)
    return c


def encoder(nc, x_in, mem_in, w8, wc_q, wc_kv, gains_in, lambda_in, rel_in, kcache, vcache, lat_cache,
            rope_cache, memk_cache, memv_cache, ident_in, dist_in, cmask_in, rope_in, slope_in,
            y_out, k_a, v_a, k_b, v_b, lat_out, rope_out, memkv_out, x_scr, rel_scr):
    ctx = ExitStack()
    place = [-(-nc.sbuf_base // 64) * 64]

    def sbuf(name, free, dtype=F32, at=None):
        size = 4 * int(np.prod(free))
        where = place[0] if at is None else at
        if at is None:
            place[0] += -(-size // 32) * 32
        return nc.alloc_sbuf_tensor_at(name, [128, *free], dtype, offset=where)

    h_at = place[0]
    h_flat = sbuf("h_split", [2 * KT * TOK], F32R)
    y_sb = sbuf("y_sb", [KT, TOK])
    w_at = place[0]
    w_raw = sbuf("w_raw", [2, KT * 128])
    w_hi = sbuf("w_hi", [2, KT * 128], F32R)
    w_lo = sbuf("w_lo", [2, KT * 128], F32R)
    qkv_at = place[0]
    q_sp = sbuf("q_split", [2, TOK], F32R)
    k_sp = sbuf("k_split", [2, KEYS], F32R)
    v_sp = sbuf("v_split", [2, 13, 128], F32R)
    c_tmp = sbuf("c_latents", [6, TOK], F32, at=qkv_at)
    c_cache = sbuf("c_cache", [2, PAST], F32, at=qkv_at + 4 * 6 * TOK)
    raw = [sbuf("raw0", [KEYS]), sbuf("raw1", [KEYS])]
    v_cache = sbuf("v_cache", [4, 128])
    prob = sbuf("prob", [5632])
    qo_at = place[0]
    qo_sp = sbuf("q_odd_split", [2, TOK], F32R)
    q_raw = sbuf("q_raw", [TOK], at=qo_at)
    rope_at = place[0]
    rope_sb = sbuf("rope_sb", [TOK])
    o_tmp = sbuf("o_tmp", [TOK], at=rope_at)
    pt = sbuf("pt_split", [2, 2, 512], F32R)
    bias = sbuf("bias", [2 * BAND])
    ident = sbuf("ident", [128])
    ones = sbuf("ones", [128])
    gains = sbuf("gains", [N_GAINS])
    slopes = sbuf("slopes", [6])
    lam = sbuf("lam", [256])
    stat = sbuf("stat", [32])
    small = sbuf("small", [8])
    w_rest = sbuf("w_rest", [6, KT * 128], F32, at=w_at)
    assert place[0] <= nc.sbuf_usable_end, place[0]
    neg_lam, eps_sb, sub_gain = small[:, 0:1], small[:, 1:2], small[:, 2:3]

    h_v = h_flat[:, :].rearrange("p (s k t) -> p s k t", s=2, k=KT)
    memh_v = h_flat[:, :].rearrange("p (s f) -> p s f", s=2)
    lat_v = h_flat[:, 0:4 * KEYS].rearrange("p (s k t) -> p s k t", s=2, k=2)
    cq_at = 4 * KEYS
    cq_v = h_flat[:, cq_at:cq_at + 6 * TOK].rearrange("p (s k t) -> p s k t", s=2, k=3)
    ko_at = cq_at + 6 * TOK
    ko_v = h_flat[:, ko_at:ko_at + 2 * KEYS].rearrange("p (s t) -> p s t", s=2)
    qe_raw = sbuf("q_even_raw", [TOK], F32, at=h_at + 4 * (ko_at + 2 * KEYS))
    pairs = lambda x: x.rearrange("p (a b) -> p a b", a=2)
    qe_v, rope_v = pairs(qe_raw[:, :]), pairs(rope_sb[:, :])
    qo_v = w_rest[:, 4:6, Q_LORA:Q_LORA + TOK // 2]
    rot_v = w_rest[:, 0:2, Q_LORA:Q_LORA + TOK // 2]
    ko_raw = w_rest[:, 0:4, Q_LORA:Q_LORA + CHUNK_KEY]
    y_flat = y_sb[:, :, :].rearrange("p k t -> p (k t)")
    mem_x = y_flat[:, 0:KT * MEMT].rearrange("p (k t) -> p k t", k=KT)
    mem_kv = prob[:, TOK:TOK + 16 * MEMT].rearrange("p (n t) -> p n t", n=16)
    rstd = prob[:, 0:TOK]
    o_squares = q_raw[:, 0:TOK]

    s_ps = [ctx.enter_context(nc.psum_tensor(f"scores{i}", [128, 1024], F32)) for i in range(2)]
    t_ps = [ctx.enter_context(nc.psum_tensor(f"turned{i}", [128, 512], F32)) for i in range(2)]
    acc = [ctx.enter_context(nc.psum_tensor(f"acc{i}", [128, 512], F32)) for i in range(2)]
    head_banks = [acc[0], acc[1], t_ps[0]]
    pair_banks = [s_ps[i // 2][:, 512 * (i % 2):512 * (i % 2) + 512] for i in range(4)] + [t[:, :] for t in t_ps]

    def sem(name):
        return ctx.enter_context(nc.semaphore(name))

    consts_loaded = sem("consts_loaded")
    consts_set = sem("consts_set")
    w_loaded = [sem(f"w_loaded{i}") for i in range(2)]
    whi_made, wlo_made = sem("whi_made"), sem("wlo_made")
    acc_ready = sem("acc_ready")
    acc_read_act = sem("acc_read_act")
    acc_read_dve = sem("acc_read_dve")
    opnd_hi_made = sem("opnd_hi_made")
    opnd_lo_made = sem("opnd_lo_made")
    turned_ready = sem("turned_ready")
    turned_hi_made = sem("turned_hi_made")
    turned_lo_made = sem("turned_lo_made")
    pv_done = sem("pv_done")
    gates_ready = sem("gates_ready")
    scores_ready = sem("scores_ready")
    scores_biased = sem("scores_biased")
    exps_ready = sem("exps_ready")
    probs_ready = sem("probs_ready")
    recips_ready = sem("recips_ready")
    lambda_recips_ready = sem("lambda_recips_ready")
    kcache_loaded = sem("kcache_loaded")
    vcache_loaded = sem("vcache_loaded")
    bias_loaded = sem("bias_loaded")
    bias_masked = sem("bias_masked")
    k_stored, v_stored = sem("k_stored"), sem("v_stored")
    squares_ready = sem("squares_ready")
    squares_added = sem("squares_added")
    squares_summed = sem("squares_summed")
    rstd_ready = sem("rstd_ready")
    normed = sem("normed")
    normed_hi, normed_lo = sem("normed_hi"), sem("normed_lo")
    normed_stored = [sem(f"normed_stored{i}") for i in range(2)]
    x_loaded = sem("x_loaded")
    x_head_loaded, x_tail_loaded = sem("x_head_loaded"), sem("x_tail_loaded")
    x_stored = sem("x_stored")
    memkv_stored = sem("memkv_stored")
    rel_stored = sem("rel_stored")
    rotated = sem("rotated")
    settled = sem("settled")
    xt_in = [sem(f"xt_in{f}") for f in range(KT)]
    block = ctx.enter_context(nc.Block())

    def settle(eng):
        eng.sem_inc(settled, 1)

    def advance(m, counts, times=1):
        for k, v in counts.items():
            m[k] = m[k] + v * times

    def at_iteration(m, counts, it):
        return {k: (v + it * counts[k] if counts.get(k) else v) for k, v in m.items()}

    def norm_counts(tiles, chunks, steps, split=True, store=False):
        c = dict(squares_ready=tiles, squares_summed=tiles, acc_read_act=chunks, rstd_ready=1, normed=steps)
        if split:
            c.update(normed_hi=steps, normed_lo=steps)
        if store:
            c.update(normed_stored0=8 * steps, normed_stored1=8 * steps)
        return c

    MEM_PROJ = dict(w=16, acc_ready=16, acc_read_act=16, memkv_stored=16, squares_ready=8, squares_added=7,
                    squares_summed=1)
    GATE = dict(w=2, acc_ready=6, acc_read_act=6)
    LATENTS = dict(w=6, acc_ready=18, acc_read_act=18, kcache_loaded=48, bias_loaded=16, opnd_hi_made=1, opnd_lo_made=1)
    KEY_ROPE = dict(rotated=2, k_stored=16, opnd_hi_made=4)
    QKV_FIRST = dict(w=3, acc_ready=9, acc_read_act=9, opnd_hi_made=2, opnd_lo_made=2, kcache_loaded=16,
                     vcache_loaded=16)
    QKV_FIRST_C = dict(w=4, acc_ready=15, acc_read_act=15, opnd_hi_made=4, opnd_lo_made=4, rotated=4)
    OUT = dict(squares_ready=8, squares_added=6, squares_summed=2, w=8, acc_ready=24, acc_read_dve=24, normed_hi=8, normed=8, x_stored=16 * 8)

    def job_start(m, kind, pair):
        m = dict(m)
        advance(m, QKV_FIRST_C if kind == "C" else QKV_FIRST)
        return at_iteration(m, job_counts(kind), pair)

    def double(c):
        return {k: 2 * v for k, v in c.items()}

    COUNTED = (
        "w", "acc_ready", "acc_read_act", "acc_read_dve", "opnd_hi_made", "opnd_lo_made", "turned_ready",
        "turned_hi_made", "turned_lo_made", "pv_done", "scores_ready", "scores_biased", "exps_ready",
        "probs_ready", "recips_ready", "lambda_recips_ready", "kcache_loaded", "vcache_loaded",
        "bias_loaded", "bias_masked", "k_stored", "v_stored", "squares_ready", "squares_summed",
        "rstd_ready", "normed", "normed_hi", "normed_lo", "normed_stored0", "normed_stored1",
        "x_loaded", "x_stored", "memkv_stored", "gates_ready", "rotated", "squares_added")

    def fresh():
        m = {k: 0 for k in COUNTED}
        m["x_loaded"] = 16
        return m

    def course(m):
        w8_at = 0

        def give(name, counts, times=1, **more):
            start = dict(m)
            advance(m, counts, times)
            return name, start, dict(counts=counts, **more)

        yield give("norm", norm_counts(KT, 1, 4 * KT), what="mem")
        yield give("mem", MEM_PROJ, w8=w8_at)
        w8_at += 16
        yield give("norm", norm_counts(0, 3, KT), what="h", layer=0, summed=True)
        for layer, kind in enumerate(KINDS):
            yield give("gate", GATE, w8=w8_at, layer=layer)
            yield give("memory_jobs", {**double(job_counts("M")), "bias_loaded": 16, "gates_ready": 6},
                       w8=w8_at + 2, layer=layer, last=kind)
            w8_at += 10
            if kind == "C":
                yield give("latents", LATENTS, w8=w8_at)
                w8_at += 6
                yield give("norm", norm_counts(3, 3, 3), what="cq")
                yield give("norm", norm_counts(2, 3, 2, store=True), what="lat")
                yield give("key_rope", KEY_ROPE)
            yield give("jobs", double(job_counts(kind)), 3, kind=kind, w8=w8_at, layer=layer)
            w8_at += 0 if kind == "C" else 18
            counts = dict(OUT)
            if layer == DEPTH - 1:
                counts.pop("x_stored")
            yield give("out", counts, w8=w8_at, layer=layer)
            w8_at += 8
            if layer < DEPTH - 1:
                yield give("norm", norm_counts(0, 3, KT), what="h", layer=layer + 1, summed=True)
        yield give("norm", norm_counts(0, 3, KT, split=False, store=True), what="final", summed=True)

    final_counts = fresh()
    COURSE = list(course(final_counts))
    LAST_W8 = w8.shape[0]

    def phases():
        return COURSE

    def norm_plan(what, layer=0):
        if what == "mem":
            steps = [(mem_x[:, k, :], G_MEM + 8 * i + k,
                      memh_v[:, 0, (8 * i + k) * MEMT:(8 * i + k + 1) * MEMT],
                      memh_v[:, 1, (8 * i + k) * MEMT:(8 * i + k + 1) * MEMT], None)
                     for i in range(DEPTH) for k in range(KT)]
            return [mem_x[:, k, :] for k in range(KT)], D, [(0, MEMT)], steps
        tok = token_chunks(TOK, CHUNK_TOK)
        if what == "h":
            return ([y_sb[:, k, :] for k in range(KT)], D, tok,
                    [(y_sb[:, k, :], G_NORM + 8 * layer + k, h_v[:, 0, k, :], h_v[:, 1, k, :], None)
                     for k in range(KT)])
        if what == "final":
            return ([y_sb[:, k, :] for k in range(KT)], D, tok,
                    [(y_sb[:, k, :], G_FINAL + k, None, None, y_out[k * 128:(k + 1) * 128, :])
                     for k in range(KT)])
        if what == "cq":
            return ([c_tmp[:, k, :] for k in range(3)], Q_LORA, tok,
                    [(c_tmp[:, k, :], G_Q + k, cq_v[:, 0, k, :], cq_v[:, 1, k, :], None) for k in range(3)])
        return ([c_tmp[:, 3 + k, :] for k in range(2)], KV_LORA, tok,
                [(c_tmp[:, 3 + k, :], G_KV + k, lat_v[:, 0, k, 0:TOK], lat_v[:, 1, k, 0:TOK],
                  lat_out[k * 128:(k + 1) * 128, :]) for k in range(2)])

    def norm_slot(what, n):
        if what == "mem":
            return raw[n % 2][:, MEMT * (n // 2 % 4):MEMT * (n // 2 % 4) + MEMT], 8
        return raw[n % 2][:, 0:TOK], 2

    def prob_at(group, step):
        if step.which:
            at = 3584 + 1024 * step.tile
        else:
            at = (768 if group.parity == 0 else 1024) * step.tile + 1536 * group.parity
        return at

    @block.sync
    def _(sp):
        for dst, src in ((ident[:, :], ident_in), (gains[:, :], gains_in), (slopes[:, :], slope_in),
                         (lam[:, :], lambda_in.partition_broadcast(128))):
            sp.dma_start(dst, src).then_inc(consts_loaded, 16)
        sp.dma_start(mem_x, mem_in).then_inc(x_loaded, 16)
        for r in range(2):
            sp.dma_start(w_raw[:, r, :], w8[r]).then_inc(w_loaded[r], 16)
        sp.dma_start(y_sb[:, 2:KT, :], x_in[:, 2:KT, :]).then_inc(x_tail_loaded, 16)
        def weight(n, r, src, width, slot=None):
            slot = r % 2 if slot is None else slot
            sp.wait_ge(wlo_made, n + r - 1)
            sp.dma_start(w_raw[:, slot, 0:width], src).then_inc(w_loaded[slot], 16)

        def w8_tile(index):
            return w8[index].rearrange("(o p) f -> (o p) f", o=1)

        def first_gates(w, index):
            for r in range(2):
                weight(w, r, w8[index + r], KT * 128)

        for name, m, o in phases():
            if name == "norm" and o["what"] in ("lat", "final"):
                _, _, _, steps = norm_plan(o["what"])
                for n, step in enumerate(steps):
                    sp.wait_ge(normed, m["normed"] + n + 1)
                    sp.dma_start(step[4], raw[n % 2][:, 0:TOK]).then_inc(normed_stored[n % 2], 16)
            elif name == "mem":
                sp.wait_ge(normed_lo, m["normed_lo"])
                sp.dma_start(y_sb[:, 0:2, :], x_in[:, 0:2, :]).then_inc(x_head_loaded, 16)
                for r in range(2, 16):
                    weight(m["w"], r, w8[o["w8"] + r], KT * 128)
                    if r < 14:
                        toeplitz = bass.AP(rel_in.tensor, 127 + 2 * 768 * (r - 2), [[768, 2], [-1, 128], [1, BAND]])
                        sp.dma_start(rel_scr[r - 2], toeplitz).then_inc(rel_stored, 16)
                first_gates(m["w"] + 16, o["w8"] + 16)
                sp.wait_ge(acc_read_act, m["acc_read_act"] + 16)
                sp.dma_start(memkv_out, mem_kv).then_inc(memkv_stored, 16)
            elif name == "memory_jobs":
                for r in range(2):
                    weight(m["w"], r, w8[o["w8"] + r], KT * 128)
                sp.wait_ge(acc_read_dve, m["acc_read_dve"])
                sp.dma_start(bias[:, 0:MEMT], cmask_in[:, 0:MEMT]).then_inc(bias_loaded, 16)
                sp.wait_ge(normed_lo, m["normed_lo"])
                sp.wait_ge(memkv_stored, 16)
                layer = o["layer"]
                per = job_counts("M")
                for j in range(2):
                    mj = at_iteration(m, per, j)
                    sp.wait_ge(opnd_lo_made, mj["opnd_lo_made"])
                    sp.dma_start(raw[1][:, 0:MEMT], memkv_out[:, 4 * layer + j, :]).then_inc(kcache_loaded, 16)
                    sp.dma_start(raw[1][:, MEMT:2 * MEMT], memk_cache[layer, j]).then_inc(kcache_loaded, 16)
                    sp.wait_ge(opnd_lo_made, mj["opnd_lo_made"] + 1)
                    sp.dma_start(raw[0][:, 0:MEMT], memkv_out[:, 4 * layer + 2 + j, :]).then_inc(vcache_loaded, 16)
                    sp.dma_start(raw[0][:, MEMT:2 * MEMT], memv_cache[layer, j]).then_inc(vcache_loaded, 16)
                    for r in range(4 * j + 2, min(4 * j + 6, 8)):
                        weight(m["w"], r, w8[o["w8"] + r], KT * 128)
            elif name == "latents":
                for r in range(2):
                    weight(m["w"], r, w8[o["w8"] + r], KT * 128)
                sp.wait_ge(opnd_lo_made, m["opnd_lo_made"])
                sp.wait_ge(acc_read_dve, m["acc_read_dve"])
                sp.dma_start(c_cache[:, :, :], lat_cache).then_inc(kcache_loaded, 16)
                sp.dma_start(rope_sb[:, :], rope_in).then_inc(kcache_loaded, 16)
                sp.dma_start(raw[1][64:96, TOK:KEYS], rope_cache).then_inc(kcache_loaded, 16)
                sp.dma_start(bias[:, 0:1024], cmask_in).then_inc(bias_loaded, 16)
                for r in range(2, 6):
                    weight(m["w"], r, w8[o["w8"] + r], KT * 128)
            elif name == "key_rope":
                sp.wait_ge(rotated, m["rotated"] + 2)
                sp.dma_start(rope_out, raw[1][64:96, 0:TOK]).then_inc(k_stored, 16)
            elif name == "jobs":
                kind, layer = o["kind"], o["layer"]
                per = job_counts(kind)
                sp.wait_ge(rel_stored, 16 * 12)
                if kind == "C":
                    with sp.Fori(0, 3) as it:
                        for u in range(2):
                            pair = 2 * it + u
                            for i, (src, width) in enumerate(((wc_q[2 * pair], 384), (wc_q[2 * pair + 1], 384),
                                                              (wc_kv[2 * pair], 256), (wc_kv[2 * pair + 1], 256))):
                                weight(m["w"] + 8 * it, 4 * u + i, src, width)
                    continue
                slot = {0: 0, 1: 1, 3: 2}[layer]

                def job_transfers(pair, u, last=False):
                    mj = job_start(m, kind, pair)
                    if not last:
                        for r in (1, 2):
                            weight(mj["w"], r, w8[o["w8"] + 3 * pair + 3 + r], KT * 128, (1 + u + r) % 2)
                    sp.wait_ge(scores_biased, mj["scores_biased"])
                    if kind == "A":
                        sp.dma_start(bias[:, :].rearrange("p (h k) -> p h k", h=2),
                                     rel_scr[6 * (layer // 3) + pair].rearrange("h p k -> p h k")).then_inc(bias_loaded, 16)
                        k_dst, v_dst = k_a[layer // 3, pair], v_a[layer // 3, pair]
                        first = PAST
                    else:
                        sp.dma_start(bias[:, 0:1024], dist_in).then_inc(bias_loaded, 16)
                        k_dst, v_dst, first = k_b[pair], v_b[pair], 0
                    sp.wait_ge(acc_read_act, mj["acc_read_act"])
                    sp.dma_start(k_dst, raw[1][:, first:TOK]).then_inc(k_stored, 16)
                    sp.dma_start(v_dst, raw[0][:, first:TOK]).then_inc(v_stored, 16)
                    if last:
                        return
                    sp.wait_ge(opnd_lo_made, mj["opnd_lo_made"])
                    sp.dma_start(raw[1][:, TOK:KEYS], kcache[6 * slot + pair + 1]).then_inc(kcache_loaded, 16)
                    sp.wait_ge(opnd_lo_made, mj["opnd_lo_made"] + 1)
                    sp.dma_start(v_cache[:, :, :], vcache[6 * slot + pair + 1]).then_inc(vcache_loaded, 16)
                    weight(mj["w"], 3, w8[o["w8"] + 3 * pair + 6], KT * 128, u % 2)

                for r in range(4):
                    weight(m["w"], r, w8[o["w8"] + r], KT * 128)
                sp.wait_ge(opnd_lo_made, m["opnd_lo_made"])
                sp.dma_start(raw[1][:, TOK:KEYS], kcache[6 * slot]).then_inc(kcache_loaded, 16)
                sp.dma_start(v_cache[:, :, :], vcache[6 * slot]).then_inc(vcache_loaded, 16)
                with sp.Fori(0, 2) as it:
                    for u in range(2):
                        job_transfers(2 * it + u, u)
                job_transfers(4, 0)
                job_transfers(5, 1, last=True)
            elif name == "out":
                layer = o["layer"]
                for r in range(2):
                    if r == 0 and KINDS[layer] == "C":
                        sp.wait_ge(opnd_lo_made, m["opnd_lo_made"])
                    if r or KINDS[layer] == "C":
                        weight(m["w"], r, w8[o["w8"] + r], KT * 128)
                src = x_in if layer == 0 else x_scr[layer - 1]
                sp.wait_ge(x_stored, m["x_stored"])
                for f in range(KT):
                    sp.wait_ge(normed, m["normed"] + f + 1)
                    sp.dma_start(y_sb[:, f, :], src[:, f, :]).then_inc(xt_in[f], 16)

                def store(f):
                    if layer < DEPTH - 1:
                        sp.wait_ge(acc_read_dve, m["acc_read_dve"] + 3 * (f + 1))
                        sp.dma_start(x_scr[layer][:, f, :], y_sb[:, f, :]).then_inc(x_stored, 16)
                for f in range(KT):
                    if f + 2 < KT:
                        weight(m["w"], f + 2, w8[o["w8"] + f + 2], KT * 128)
                    if f + 2 == KT and layer < DEPTH - 1:
                        first_gates(m["w"] + KT, o["w8"] + KT)
                    store(f)
        sp.wait_ge(normed_stored[0], final_counts["normed_stored0"])
        sp.wait_ge(normed_stored[1], final_counts["normed_stored1"])
        sp.wait_ge(k_stored, final_counts["k_stored"])
        sp.wait_ge(v_stored, final_counts["v_stored"])
        sp.wait_ge(memkv_stored, final_counts["memkv_stored"])
        sp.wait_ge(x_stored, final_counts["x_stored"])

    @block.scalar
    def _(act):
        def split_weight(m, r, wide, end):
            w = m["w"]
            act.wait_ge(w_loaded[r % 2], 8 * w + 16 * (r // 2 + 1))
            act.wait_ge(acc_ready, m["acc_ready"] + end)
            act.activation(w_hi[:, r % 2, 0:wide], w_raw[:, r % 2, 0:wide], ACT.Copy).then_inc(whi_made, 1)

        def norm(m, what, layer=0, summed=False):
            tiles, width, chunks, steps = norm_plan(what, layer)
            if summed:
                tiles = []
            act.wait_ge(x_loaded, m["x_loaded"])
            act.wait_ge(acc_read_dve, m["acc_read_dve"])
            act.wait_ge(acc_read_act, m["acc_read_act"])
            act.wait_ge(k_stored, m["k_stored"])
            act.wait_ge(v_stored, m["v_stored"])
            act.wait_ge(normed_lo, m["normed_lo"])
            act.wait_ge(normed_stored[0], m["normed_stored0"])
            act.wait_ge(normed_stored[1], m["normed_stored1"])
            for k, tile in enumerate(tiles):
                if k >= 2:
                    act.wait_ge(squares_summed, m["squares_summed"] + k - 1)
                n = sum(c for _, c in chunks)
                act.activation(raw[k % 2][:, 0:n], tile, ACT.Square).then_inc(squares_ready, 1)
            act.wait_ge(squares_summed, m["squares_summed"] + len(tiles))
            root(m, chunks, width, pair_banks)
            for n, step in enumerate(steps):
                if step[2] is not None:
                    act.wait_ge(normed, m["normed"] + n + 1)
                    act.activation(step[2], norm_slot(what, n)[0], ACT.Copy).then_inc(normed_hi, 1)

        def root(m, chunks, width, banks, first=0):
            for c, (a, n) in enumerate(chunks):
                act.activation(rstd[:, a:a + n], banks[c][:, 0:n], ACT.Ln, scale=1.0 / width,
                               bias=eps_sb).then_inc(acc_read_act, 1)
            n = sum(c for _, c in chunks)
            act.wait_ge(acc_read_act, m["acc_read_act"] + first + len(chunks))
            act.activation(rstd[:, 0:n], rstd[:, 0:n], ACT.Exp, scale=-0.5).then_inc(rstd_ready, 1)

        def transposed_v(m, kind):
            for v, chunk in enumerate(V_CHUNKS[kind]):
                act.wait_ge(turned_ready, m["turned_ready"] + v + 1)
                act.wait_ge(pv_done, m["pv_done"])
                rows, n = chunk[0][2], len(chunk)
                act.activation(v_sp[0:rows, 0, chunk[0][0]:chunk[0][0] + n, :],
                               t_ps[v % 2][0:rows, 0:128 * n].rearrange("p (n d) -> p n d", d=128),
                               ACT.Copy).then_inc(turned_hi_made, 1)

        def q_k_v_out(kind, t, a, n, src):
            if kind == "C" and t == 2:
                act.activation(raw[1][0:64, a:a + n], src[0:64, 0:n], ACT.Copy)
                act.activation(ko_raw[0:64, a // CHUNK_KEY, :], src[64:128, 0:n], ACT.Copy).then_inc(acc_read_act, 1)
            elif kind == "C":
                half = TOK // 2
                if t == 0:
                    dst = qe_raw[:, a:a + n]
                elif t == 1:
                    dst = qo_v[:, a // half, a % half:a % half + n]
                else:
                    dst = raw[0][:, a:a + n]
                act.activation(dst, src[:, 0:n], ACT.Copy, scale=SCALE_C if t < 2 else 1.0).then_inc(acc_read_act, 1)
            else:
                act.activation((q_raw, raw[1], raw[0])[t][:, a:a + n], src[:, 0:n], ACT.Copy,
                               scale=1.0 if t else SCALE_64).then_inc(acc_read_act, 1)

        def job(m, kind, r0, it, next_wide, side_out=None, last=False):
            groups, proj, side = GROUPS[kind], JOB_PROJ[kind], [] if last else SIDE_PROJ[kind]
            if proj:
                act.wait_ge(acc_read_dve, m["acc_read_dve"])
                act.wait_ge(k_stored, m["k_stored"])
                act.wait_ge(v_stored, m["v_stored"])
            wm = dict(m, w=it["w"])
            ends = [0]
            for _, chunks in proj:
                ends.append(ends[-1] + len(chunks))
            done = 0
            for j, (kt, chunks) in enumerate(proj):
                if j + 1 < len(proj):
                    split_weight(wm, r0 + j + 1, 128 * proj[j + 1][0], ends[j])
                elif side:
                    split_weight(wm, r0 + j + 1, 128 * side[0][0], ends[j])
                for c, (a, n) in enumerate(chunks):
                    act.wait_ge(acc_ready, m["acc_ready"] + done + 1)
                    src = acc[done % 2]
                    done += 1
                    act.activation(raw[0][:, a:a + n], src[:, 0:n], ACT.Copy, scale=SCALE_64).then_inc(acc_read_act, 1)
            if proj:
                for i in range(EARLY[kind]):
                    a, n = side[0][1][i]
                    act.wait_ge(acc_ready, m["acc_ready"] + done + i + 1)
                    act.activation(side_out(0, a, n), acc[(done + i) % 2][:, 0:n], ACT.Copy).then_inc(acc_read_act, 1)
                transposed_v(m, kind)
            nv = len(V_CHUNKS[kind])
            s = 0
            a_i = 0

            def exponentials(steps, g):
                nonlocal s
                for step in steps:
                    act.wait_ge(scores_biased, m["scores_biased"] + s + 1)
                    at = prob_at(g, step)
                    p = prob[0:step.rows, at:at + step.width]
                    act.activation(p, p, ACT.Exp, scale=-1.0, bias=stat[0:step.rows, s % 8:s % 8 + 1],
                                   accum_out=stat[0:step.rows, 8 + s % 8:9 + s % 8]).then_inc(exps_ready, 1)
                    s += 1

            exponentials(groups[0].steps, groups[0])
            if not proj:
                transposed_v(m, kind)
            if side:
                split_weight(wm, r0 + len(proj) + 1, 128 * side[1][0], done)
            for h, g in enumerate(groups):
                for c, chunk in enumerate(g.chunks):
                    act.wait_ge(turned_ready, m["turned_ready"] + nv + a_i + 1)
                    act.wait_ge(pv_done, m["pv_done"] + max(a_i - 1, 0))
                    rects = rectangles(g, chunk)
                    for i, (rows, c0, n) in enumerate(rects):
                        ins = act.activation(pt[0:rows, a_i % 2, 0, c0:c0 + n],
                                             t_ps[(nv + a_i) % 2][0:rows, c0:c0 + n], ACT.Copy)
                    ins.then_inc(turned_hi_made, 1)
                    a_i += 1
                    if h + 1 < len(groups):
                        half = len(groups[h + 1].steps) // 2
                        if c == 0:
                            exponentials(groups[h + 1].steps[:half], groups[h + 1])
                        if c == min(1, len(g.chunks) - 1):
                            exponentials(groups[h + 1].steps[half:], groups[h + 1])
                    for t, sc, i, part, parts in side_slots(kind, h, last)[c]:
                        if part < parts - 1:
                            continue
                        act.wait_ge(acc_ready, m["acc_ready"] + done + i + 1)
                        a, n = side[t][1][sc]
                        if kind == "C" and t != 1 and sc == 0:
                            act.wait_ge(opnd_lo_made, m["opnd_lo_made"])
                        if kind in "AB" and sc == 0:
                            if t == 0:
                                act.wait_ge(opnd_lo_made, m["opnd_lo_made"])
                            elif t == 1:
                                act.wait_ge(k_stored, m["k_stored"] + 16)
                            else:
                                act.wait_ge(v_stored, m["v_stored"] + 16)
                        if kind == "M":
                            act.activation(side_out(t, a, n), acc[1][:, 0:n], ACT.Copy).then_inc(acc_read_act, 1)
                        else:
                            q_k_v_out(kind, t, a, n, acc[1])
                        if sc == len(side[t][1]) - 1 and t + 1 < len(side):
                            wide = 128 * side[t + 2][0] if t + 2 < len(side) else next_wide
                            if wide:
                                split_weight(wm, r0 + len(proj) + t + 2, wide, done + i + 1)
            if kind == "B":
                if not last:
                    act.wait_ge(opnd_lo_made, m["opnd_lo_made"] + 2)
                act.wait_ge(acc_read_dve, m["acc_read_dve"] + len(groups) - 1)
                act.activation(o_squares[:, 0:SEQ], o_tmp[:, 0:SEQ], ACT.Square)
                act.wait_ge(acc_read_dve, m["acc_read_dve"] + len(groups))
                act.activation(o_squares[:, SEQ:TOK], o_tmp[:, SEQ:TOK], ACT.Square).then_inc(squares_ready, 1)
                act.wait_ge(squares_summed, m["squares_summed"] + 1)
                root(m, token_chunks(TOK, CHUNK_TOK), 128, head_banks,
                     first=sum(len(chunks) for _, chunks in proj + side))

        act.wait_ge(consts_set, 3)
        act.activation(small[:, 5:7], small[:, 3:5], ACT.Exp).then_inc(consts_set, 1)
        split_weight(fresh(), 0, KT * 128, 0)
        for name, m, o in phases():
            if name == "norm":
                norm(m, o["what"], o.get("layer", 0), o.get("summed", False))
            elif name == "mem":
                def pair_of(mi, first=0):
                    for r in range(2):
                        split_weight(dict(mi), r + 1, KT * 128, r)
                        act.wait_ge(acc_ready, mi["acc_ready"] + r + 1)
                        yield r
                per = dict(w=2, acc_ready=2, acc_read_act=2)
                with act.Fori(0, 8) as it:
                    mi = at_iteration(m, per, it)
                    for r in pair_of(mi):
                        act.activation(mem_kv[:, 2 * it + r, :], acc[r][:, 0:MEMT], ACT.Copy).then_inc(acc_read_act, 1)
                split_weight(m, 17, KT * 128, 16)
            elif name == "gate":
                act.wait_ge(x_stored, m["x_stored"])
                split_weight(m, 2, KT * 128, 3)
                for i in range(6):
                    a, n = token_chunks(TOK, CHUNK_TOK)[i % 3]
                    act.wait_ge(acc_ready, m["acc_ready"] + i + 1)
                    act.activation(y_sb[:, 6 + i // 3, a:a + n], pair_banks[i][:, 0:n], ACT.Silu).then_inc(acc_read_act, 1)
            elif name == "memory_jobs":
                per = job_counts("M")
                for j in range(2):
                    job(at_iteration(m, per, j), "M", 4 * j, dict(w=m["w"]), KT * 128,
                        lambda t, a, n: y_sb[:, 3 * j + t, a:a + n])
                act.wait_ge(acc_read_act, m["acc_read_act"] + 2 * per["acc_read_act"])
                for t in range(6):
                    act.activation(y_sb[:, t, :], y_sb[:, t, :], ACT.Silu).then_inc(gates_ready, 1)
            elif name == "latents":
                act.wait_ge(acc_read_dve, m["acc_read_dve"])
                for t in range(6):
                    if t < 5:
                        split_weight(m, t + 1, KT * 128, 3 * t)
                    for c, (a, n) in enumerate(token_chunks(TOK, CHUNK_TOK)):
                        act.wait_ge(acc_ready, m["acc_ready"] + 3 * t + c + 1)
                        act.activation(c_tmp[:, t, a:a + n], acc[(3 * t + c) % 2][:, 0:n],
                                       ACT.Copy).then_inc(acc_read_act, 1)
            elif name == "jobs":
                kind = o["kind"]
                per = job_counts(kind)
                act.wait_ge(acc_read_dve, m["acc_read_dve"])
                act.wait_ge(k_stored, m["k_stored"])
                side = SIDE_PROJ[kind]
                if kind == "C":
                    split_weight(m, 0, 128 * side[0][0], 0)
                done = 0
                for t, (_, chunks) in enumerate(side):
                    split_weight(m, t + 1, 128 * side[(t + 1) % len(side)][0], done)
                    for a, n in chunks:
                        act.wait_ge(acc_ready, m["acc_ready"] + done + 1)
                        q_k_v_out(kind, t, a, n, acc[done % 2])
                        done += 1
                n_w, next_wide = len(side), 128 * side[0][0]
                with act.Fori(0, 2) as it:
                    for u in range(2):
                        job(job_start(m, kind, 2 * it + u), kind, n_w * u + n_w, dict(w=m["w"] + 2 * n_w * it),
                            next_wide)
                job(job_start(m, kind, 4), kind, n_w, dict(w=m["w"] + 4 * n_w), 0 if kind == "C" else next_wide)
                job(job_start(m, kind, 5), kind, 0, dict(w=m["w"] + 6 * n_w), 0, last=True)
                if o["kind"] == "C":
                    after = {k: v + 3 * o["counts"].get(k, 0) for k, v in m.items()}
                    split_weight(after, 0, KT * 128, 0)
            elif name == "out":
                act.wait_ge(acc_read_dve, m["acc_read_dve"])
                split_weight(m, 1, KT * 128, 0)
                for k in range(KT):
                    act.activation(h_v[:, 0, k, :], y_sb[:, k, :], ACT.Copy).then_inc(normed_hi, 1)
                act.wait_ge(k_stored, m["k_stored"])
                act.wait_ge(v_stored, m["v_stored"])
                act.wait_ge(normed_stored[0], m["normed_stored0"])
                act.wait_ge(normed_stored[1], m["normed_stored1"])

                def square(f):
                    act.wait_ge(acc_read_dve, m["acc_read_dve"] + 3 * (f + 1))
                    if f >= 2:
                        act.wait_ge(squares_added, m["squares_added"] + f - 1)
                    act.activation(raw[min(f, 1)][:, 0:TOK], y_sb[:, f, :], ACT.Square).then_inc(squares_ready, 1)

                for f in range(1, KT):
                    if o["w8"] + f + 1 < LAST_W8:
                        split_weight(m, f + 1, KT * 128, 3 * f)
                    square(f - 1)
                if o["w8"] + KT + 1 < LAST_W8:
                    split_weight(m, KT + 1, KT * 128, 3 * KT)
                square(KT - 1)

    @block.vector
    def _(dve):
        def normalise(m, what, layer=0):
            _, _, _, steps = norm_plan(what, layer)
            dve.wait_ge(rstd_ready, m["rstd_ready"] + 1)
            for n, (tile, g, hi, _, store) in enumerate(steps):
                w = tile.shape[-1]
                slot, slots = norm_slot(what, n)
                if n >= slots and hi is not None:
                    dve.wait_ge(normed_lo, m["normed_lo"] + n - slots + 1)
                if n >= 2 and store is not None:
                    dve.wait_ge(normed_stored[n % 2], m[f"normed_stored{n % 2}"] + 16 * (n // 2))
                dve.scalar_tensor_tensor(out=slot, in0=tile, scalar=gains[:, g:g + 1],
                                         in1=rstd[:, 0:w], op0=ALU.mult, op1=ALU.mult).then_inc(normed, 1)

        def rotate(own, src, dst, tmp):
            dve.tensor_tensor(tmp[64:96], src[96:128], rope_v[96:128], ALU.mult)
            dve.tensor_tensor(dst[64:96], src[64:96], rope_v[64:96], ALU.mult).then_inc(rotated, 1)
            dve.wait_ge(rotated, own + 1)
            dve.tensor_tensor(dst[64:96], dst[64:96], tmp[64:96], ALU.add).then_inc(rotated, 1)
            dve.wait_ge(rotated, own + 2)

        def q_of_c(head, own, steps=(0, 1, 2, 3)):
            x, split = (qo_v, qo_sp) if head else (qe_v, q_sp)
            if 0 in steps:
                dve.tensor_tensor(rot_v[64:96], x[96:128], rope_v[96:128], ALU.mult)
            if 1 in steps:
                dve.tensor_tensor(x[64:96], x[64:96], rope_v[64:96], ALU.mult).then_inc(rotated, 1)
            if 2 in steps:
                dve.wait_ge(rotated, own + 1)
                dve.tensor_tensor(x[64:96], x[64:96], rot_v[64:96], ALU.add).then_inc(rotated, 1)
            if 3 in steps:
                dve.wait_ge(rotated, own + 2)
                dve.tensor_copy(pairs(split[0:96, 0, :]), x[0:96]).then_inc(opnd_hi_made, 1)

        def keys_of_c(head):
            if head:
                dve.tensor_copy(ko_v[0:64, 0, :].rearrange("p (c n) -> p c n", c=4), ko_raw[0:64]).then_inc(opnd_hi_made, 1)
            else:
                dve.tensor_copy(k_sp[0:64, 0, :], raw[1][0:64, :]).then_inc(opnd_hi_made, 1)

        def transposed_v(m, kind):
            for v, chunk in enumerate(V_CHUNKS[kind]):
                dve.wait_ge(turned_hi_made, m["turned_hi_made"] + v + 1)
                rows, n, vt = chunk[0][2], len(chunk), chunk[0][0]
                dve.tensor_tensor(v_sp[0:rows, 1, vt:vt + n, :],
                                  t_ps[v % 2][0:rows, 0:128 * n].rearrange("p (n d) -> p n d", d=128),
                                  v_sp[0:rows, 0, vt:vt + n, :].bitcast(F32), ALU.subtract).then_inc(turned_lo_made, 1)

        def q_of_ab():
            dve.tensor_copy(q_sp[:, 0, :], q_raw[:, 0:TOK]).then_inc(opnd_hi_made, 1)

        def k_of_ab(cached_k):
            dve.wait_ge(kcache_loaded, cached_k)
            dve.tensor_copy(k_sp[:, 0, :], raw[1][:, 0:KEYS]).then_inc(opnd_hi_made, 1)

        def cached_v(m):
            dve.wait_ge(vcache_loaded, m["vcache_loaded"])
            dve.tensor_copy(v_sp[:, 0, 8:12, :], v_cache[:, :, :]).then_inc(opnd_hi_made, 1)

        def head_of_b(m, tile):
            cached_v(m)
            dve.wait_ge(bias_loaded, m["bias_loaded"] + 16)
            dve.tensor_scalar(bias[:, 0:1024], bias[:, 0:1024], slopes[:, bass.ds(tile, 1)], None,
                              ALU.mult).then_inc(bias_masked, 1)

        def job_after(m):
            return at_iteration(m, job_counts("B"), 1)

        def job(m, kind, tile, last=False):
            groups = GROUPS[kind]
            nv = len(V_CHUNKS[kind])
            r_own = m["recips_ready"]
            if kind == "M":
                dve.wait_ge(acc_read_act, m["acc_read_act"] + 3)
                dve.tensor_copy(q_sp[:, 0, :], raw[0][:, 0:TOK]).then_inc(opnd_hi_made, 1)
                dve.wait_ge(kcache_loaded, m["kcache_loaded"] + 32)
                dve.tensor_copy(k_sp[:, 0, 0:2 * MEMT], raw[1][:, 0:2 * MEMT]).then_inc(opnd_hi_made, 1)
            elif kind == "A":
                cached_v(m)
            if kind == "M":
                transposed_v(m, kind)
            if kind == "A":
                dve.wait_ge(bias_loaded, m["bias_loaded"] + 16)
                both = bias[:, :].rearrange("p (h k) -> p h k", h=2)
                dve.memset(both[64:128, :, 0:CHUNK], NEG)
                dve.memset(both[0:64, :, BAND - CHUNK:BAND], NEG).then_inc(bias_masked, 1)
            if kind in "AB":
                dve.wait_ge(bias_masked, m["bias_masked"] + 1)
            else:
                dve.wait_ge(bias_loaded, m["bias_loaded"])
            ends, total = [], 0
            for g in groups:
                total += len(g.chunks)
                ends.append(total)
            s = 0
            normed = 0
            p_done = 0

            def minima(h, g, steps):
                nonlocal s
                for step in steps:
                    dve.wait_ge(scores_ready, m["scores_ready"] + s + 1)
                    if h >= 2:
                        dve.wait_ge(turned_ready, m["turned_ready"] + nv + ends[h - 2])
                    if step.which and h >= 1:
                        dve.wait_ge(probs_ready, m["probs_ready"] + p_done)
                    settle(dve)
                    at = prob_at(g, step)
                    b0 = step.bias0 + (BAND * step.head if kind == "A" else 0)
                    dve.tensor_tensor_reduce(
                        out=prob[0:step.rows, at:at + step.width],
                        in0=s_ps[s % 2][0:step.rows, 0:step.width],
                        in1=bias[0:step.rows, b0:b0 + step.width] if kind != "M" else bias[0:step.rows, 0:MEMT],
                        scale=-1.0, scalar=3e38, op0=ALU.add, op1=ALU.min,
                        accum_out=stat[0:step.rows, s % 8:s % 8 + 1]).then_inc(scores_biased, 1)
                    s += 1

            def probabilities(g, tiles=(0, 1)):
                nonlocal normed, p_done
                count = 2 if kind == "B" else 1
                for first in [count * t for t in tiles if count * t < len(g.steps)]:
                    steps = g.steps[first:first + count]
                    rows, width = steps[0].rows, steps[0].width
                    cols = []
                    for i, step in enumerate(steps):
                        n = normed + i
                        dve.wait_ge(exps_ready, m["exps_ready"] + n + 1)
                        cols.append(stat[0:rows, 16 + n % 8:17 + n % 8])
                        dve.reciprocal(cols[i], stat[0:rows, 8 + n % 8:9 + n % 8]).then_inc(recips_ready, 1)
                    at = prob_at(g, steps[0])
                    p = prob[0:rows, at:at + width]
                    if kind == "B":
                        dve.wait_ge(recips_ready, r_own + normed + count)
                        dve.tensor_scalar(p, p, cols[0], None, ALU.mult)
                        lamr = stat[0:rows, 24 + first // 2:25 + first // 2]
                        dve.tensor_scalar(lamr, cols[1], neg_lam[0:rows, :], None, ALU.mult).then_inc(lambda_recips_ready, 1)
                        b_count[0] = b_count[0] + 1
                        dve.wait_ge(lambda_recips_ready, m["lambda_recips_ready"] + b_count[0])
                        at1 = prob_at(g, steps[1])
                        dve.scalar_tensor_tensor(out=p, in0=prob[0:rows, at1:at1 + width], scalar=lamr, in1=p,
                                                 op0=ALU.mult, op1=ALU.add).then_inc(probs_ready, 1)
                    else:
                        dve.wait_ge(recips_ready, r_own + normed + 1)
                        dve.tensor_scalar(p, p, cols[0], None, ALU.mult).then_inc(probs_ready, 1)
                    normed += count
                    p_done += 1

            def next_operands(h, i):
                if kind == "C":
                    if (h, i) == (2, 1):
                        dve.wait_ge(acc_read_act, m["acc_read_act"] + 3)
                        q_of_c(0, m["rotated"], (0,))
                    elif (h, i) in ((2, 2), (3, 1)):
                        q_of_c(0, m["rotated"], (h - 1,))
                    elif (h, i) == (4, 0):
                        dve.wait_ge(scores_ready, m["scores_ready"] + 10)
                        q_of_c(0, m["rotated"], (3,))
                    elif (h, i) == (5, 1):
                        dve.wait_ge(acc_read_act, m["acc_read_act"] + 7)
                        q_of_c(1, m["rotated"] + 2, (0,))
                    elif (h, i) in ((7, 0), (7, 1)):
                        q_of_c(1, m["rotated"] + 2, (i + 1,))
                    elif (h, i) == (7, 3):
                        dve.wait_ge(acc_read_act, m["acc_read_act"] + 11)
                        keys_of_c(0)
                    elif (h, i) == (8, 1):
                        dve.wait_ge(scores_ready, m["scores_ready"] + s)
                        q_of_c(1, m["rotated"] + 2, (3,))
                    elif (h, i) == (8, 2):
                        keys_of_c(1)
                elif kind in "AB" and h + 2 == len(groups):
                    if i == 0:
                        dve.wait_ge(scores_ready, m["scores_ready"] + s)
                        dve.wait_ge(acc_read_act, m["acc_read_act"] + 6)
                        q_of_ab()
                    elif i == 1:
                        k_of_ab(m["kcache_loaded"] + 16)

            b_count = [0]
            half = [len(g.steps) // 2 for g in groups]
            minima(0, groups[0], groups[0].steps)
            if kind in "AC":
                minima(1, groups[1], groups[1].steps[:half[1]])
            if kind != "M":
                transposed_v(m, kind)
            probabilities(groups[0])
            if kind in "BM":
                minima(1, groups[1], groups[1].steps[:half[1]])
            a_i = 0
            for h, g in enumerate(groups):
                for i, chunk in enumerate(g.chunks):
                    dve.wait_ge(turned_hi_made, m["turned_hi_made"] + nv + a_i + 1)
                    for rows, c, n in rectangles(g, chunk):
                        ins = dve.tensor_tensor(pt[0:rows, a_i % 2, 1, c:c + n],
                                                t_ps[(nv + a_i) % 2][0:rows, c:c + n],
                                                pt[0:rows, a_i % 2, 0, c:c + n].bitcast(F32), ALU.subtract)
                    ins.then_inc(turned_lo_made, 1)
                    a_i += 1
                    if i == 0 and h + 1 < len(groups):
                        minima(h + 1, groups[h + 1], groups[h + 1].steps[half[h + 1]:])
                    if i == 1 and h + 1 < len(groups):
                        probabilities(groups[h + 1], (0,))
                    if not last:
                        next_operands(h, i)
                if h + 1 < len(groups):
                    probabilities(groups[h + 1], (1,) if len(g.chunks) > 1 else (0, 1))
                if h + 2 < len(groups):
                    minima(h + 2, groups[h + 2], groups[h + 2].steps[:half[h + 2]])
                dve.wait_ge(pv_done, m["pv_done"] + ends[h])
                o_ps = acc[output_bank(kind, h)]
                if kind == "B":
                    dve.tensor_copy(o_tmp[:, g.q0:g.q0 + g.qn], o_ps[:, 0:g.qn]).then_inc(acc_read_dve, 1)
                else:
                    r0 = 64 * g.head
                    gate = y_sb[r0:r0 + 64, tile, g.q0:g.q0 + g.qn]
                    dve.tensor_tensor(gate, o_ps[0:64, 0:g.qn], gate, ALU.mult).then_inc(acc_read_dve, 1)
            if kind == "B":
                gate = y_sb[:, tile, :]
                dve.wait_ge(acc_read_dve, m["acc_read_dve"] + len(groups))
                dve.scalar_tensor_tensor(out=gate, in0=o_tmp[:, 0:TOK], scalar=sub_gain, in1=gate,
                                         op0=ALU.mult, op1=ALU.mult).then_inc(recips_ready, 1)
                if not last:
                    head_of_b(job_after(m), tile + 1)
                dve.wait_ge(recips_ready, m["recips_ready"] + s + 1)
                dve.wait_ge(rstd_ready, m["rstd_ready"] + 1)
                dve.tensor_tensor(gate, gate, rstd, ALU.mult).then_inc(acc_read_dve, 1)
                dve.wait_ge(acc_read_dve, m["acc_read_dve"] + len(groups) + 1)

        dve.wait_ge(consts_loaded, 16 * 4)
        dve.wait_ge(consts_set, 1)
        for i in range(2):
            dve.tensor_tensor_reduce(out=prob[:, 64 * i:64 * i + 64],
                                     in0=lam[:, 128 * i:128 * i + 64], in1=lam[:, 128 * i + 64:128 * i + 128],
                                     scale=1.0, scalar=0.0, op0=ALU.mult, op1=ALU.add,
                                     accum_out=small[:, 3 + i:4 + i]).then_inc(consts_set, 1)
        dve.wait_ge(consts_set, 4)
        dve.scalar_tensor_tensor(out=neg_lam, in0=small[:, 6:7], scalar=-LAM_INIT, in1=small[:, 5:6],
                                 op0=ALU.add, op1=ALU.subtract).then_inc(consts_set, 1)
        dve.tensor_scalar(sub_gain, gains[:, G_SUB:G_SUB + 1], 1.0 - LAM_INIT, None, ALU.mult).then_inc(consts_set, 1)
        dve.wait_ge(consts_set, 6)
        def squares_of_x(m):
            dve.wait_ge(normed_lo, m["normed_lo"])
            for n, f in enumerate([2, 3, 4, 5, 6, 7, 0, 1]):
                if n == 0:
                    dve.wait_ge(x_tail_loaded, 16)
                if n == 6:
                    dve.wait_ge(x_head_loaded, 16)
                if n >= 2:
                    dve.wait_ge(squares_added, m["squares_added"] + n - 1)
                dve.tensor_tensor(raw[min(n, 1)][:, 0:TOK], y_sb[:, f, :], y_sb[:, f, :], ALU.mult).then_inc(squares_ready, 1)
                if n:
                    dve.wait_ge(squares_ready, m["squares_ready"] + n + 1)
                    dve.tensor_tensor(raw[0][:, 0:TOK], raw[0][:, 0:TOK], raw[1][:, 0:TOK], ALU.add).then_inc(squares_added, 1)

        for name, m, o in phases():
            if name == "mem":
                squares_of_x(m)
            if name == "norm":
                normalise(m, o["what"], o.get("layer", 0))
            elif name == "memory_jobs":
                per = job_counts("M")
                mb = dict(m, bias_loaded=m["bias_loaded"] + 16)
                for j in range(2):
                    job(at_iteration(mb, per, j), "M", 6 + j)
            elif name == "latents":
                dve.wait_ge(acc_read_act, m["acc_read_act"] + 18)
                dve.wait_ge(kcache_loaded, m["kcache_loaded"] + 48)
                dve.tensor_copy(lat_v[:, 0, :, TOK:KEYS], c_cache[:, :, :]).then_inc(opnd_hi_made, 1)
            elif name == "key_rope":
                dve.wait_ge(normed_stored[0], m["normed_stored0"])
                dve.wait_ge(normed_stored[1], m["normed_stored1"])
                dve.wait_ge(normed_lo, m["normed_lo"])
                rotate(m["rotated"], pairs(c_tmp[:, 5, :]), pairs(raw[1][:, 0:TOK]), pairs(raw[0][:, 0:TOK]))
                dve.tensor_copy(k_sp[64:96, 0, :], raw[1][64:96, :]).then_inc(opnd_hi_made, 1)
                dve.tensor_copy(ko_v[64:96, 0, :], raw[1][64:96, :]).then_inc(opnd_hi_made, 1)
                dve.wait_ge(opnd_hi_made, m["opnd_hi_made"] + 2)
                for keys in (k_sp, ko_v):
                    dve.tensor_tensor(keys[64:96, 1, :], raw[1][64:96, :], keys[64:96, 0, :].bitcast(F32),
                                      ALU.subtract).then_inc(opnd_hi_made, 1)
            elif name == "jobs":
                per = job_counts(o["kind"])
                dve.wait_ge(gates_ready, m["gates_ready"])
                kind = o["kind"]
                if kind == "C":
                    for head in range(2):
                        dve.wait_ge(acc_read_act, m["acc_read_act"] + (7 if head else 3))
                        q_of_c(head, m["rotated"] + 2 * head)
                        if head == 0:
                            dve.wait_ge(acc_read_act, m["acc_read_act"] + 11)
                            keys_of_c(0)
                    keys_of_c(1)
                else:
                    dve.wait_ge(acc_read_act, m["acc_read_act"] + 6)
                    q_of_ab()
                    k_of_ab(m["kcache_loaded"] + 16)
                if kind == "B":
                    head_of_b(job_start(m, kind, 0), 0)
                with dve.Fori(0, 2) as it:
                    for u in range(2):
                        job(job_start(m, kind, 2 * it + u), kind, 2 * it + u)
                job(job_start(m, kind, 4), kind, 4)
                job(job_start(m, kind, 5), kind, 5, last=True)
            elif name == "out":
                for k in range(KT):
                    dve.wait_ge(normed_hi, m["normed_hi"] + k + 1)
                    dve.tensor_tensor(h_v[:, 1, k, :], y_sb[:, k, :], h_v[:, 0, k, :].bitcast(F32),
                                      ALU.subtract).then_inc(normed, 1)
                for f in range(KT):
                    dve.wait_ge(xt_in[f], 16 * (o["layer"] + 1))
                    for c, (a, n) in enumerate(token_chunks(TOK, CHUNK_TOK)):
                        dve.wait_ge(acc_ready, m["acc_ready"] + 3 * f + c + 1)
                        x = y_sb[:, f, a:a + n]
                        i = 3 * f + c
                        bank = pair_banks[i] if i < 6 else acc[i % 2]
                        dve.tensor_tensor(x, bank[:, 0:n], x, ALU.add).then_inc(acc_read_dve, 1)

    @block.gpsimd
    def _(pool):
        def split_weight(m, r, wide):
            pool.wait_ge(whi_made, m["w"] + r + 1)
            pool.tensor_tensor(w_lo[:, r % 2, 0:wide], w_raw[:, r % 2, 0:wide],
                               w_hi[:, r % 2, 0:wide].bitcast(F32), ALU.subtract).then_inc(wlo_made, 1)

        def low(m, i, out, x, hi):
            pool.wait_ge(opnd_hi_made, m["opnd_hi_made"] + i + 1)
            pool.tensor_tensor(out, x, hi.bitcast(F32), ALU.subtract).then_inc(opnd_lo_made, 1)

        def q_and_k(m, i):
            low(m, i, q_sp[:, 1, :], q_raw[:, 0:TOK], q_sp[:, 0, :])
            low(m, i + 1, k_sp[:, 1, :], raw[1][:, :], k_sp[:, 0, :])

        def q_and_k_of_c(m, head):
            if head:
                low(m, 2, pairs(qo_sp[0:96, 1, :]), qo_v[0:96], pairs(qo_sp[0:96, 0, :]))
                ko_halves = ko_v[0:64].rearrange("p s (c n) -> p s c n", c=4)
                low(m, 3, ko_halves[:, 1], ko_raw[0:64], ko_halves[:, 0])
            else:
                low(m, 1, k_sp[0:64, 1, :], raw[1][0:64, :], k_sp[0:64, 0, :])

        def job(m, kind, r0, w, next_wide, last=False):
            proj = JOB_PROJ[kind]
            wm = dict(m, w=w)
            if kind == "C":
                if not last:
                    for t in (1, 2, 3):
                        split_weight(wm, r0 + t, 128 * SIDE_PROJ["C"][t][0])
                    low(m, 0, q_sp[0:96, 1, :], qe_raw[0:96, :], q_sp[0:96, 0, :])
                    if next_wide:
                        split_weight(wm, r0 + 4, next_wide)
                    q_and_k_of_c(m, 0)
                    q_and_k_of_c(m, 1)
                return
            if kind in "AB":
                low(m, 0, v_sp[:, 1, 8:12, :], v_cache[:, :, :], v_sp[:, 0, 8:12, :])
                if not last:
                    for t in (1, 2, 3):
                        split_weight(wm, r0 + t, KT * 128)
                    q_and_k(m, 1)
                return
            for j in range(len(proj)):
                if j + 1 < len(proj):
                    split_weight(wm, r0 + j + 1, 128 * proj[j + 1][0])
                split_weight(wm, r0 + len(proj), 128 * SIDE_PROJ[kind][0][0])
                low(m, 0, q_sp[:, 1, :], raw[0][:, 0:TOK], q_sp[:, 0, :])
            if kind == "M":
                low(m, 1, k_sp[:, 1, 0:2 * MEMT], raw[1][:, 0:2 * MEMT], k_sp[:, 0, 0:2 * MEMT])
            for t, (kt, _) in enumerate(SIDE_PROJ[kind]):
                if t:
                    split_weight(wm, r0 + len(proj) + t, 128 * kt)
            if next_wide:
                split_weight(wm, r0 + len(proj) + len(SIDE_PROJ[kind]), next_wide)

        pool.memset(ones[:, :], 1.0)
        pool.memset(eps_sb, EPS).then_inc(consts_set, 1)
        pool.wait_ge(consts_loaded, 16 * 4)
        split_weight(fresh(), 0, KT * 128)
        for name, m, o in phases():
            if name == "norm":
                _, _, _, steps = norm_plan(o["what"], o.get("layer", 0))
                for n, (tile, _, hi, lo, _) in enumerate(steps):
                    if hi is not None:
                        pool.wait_ge(normed_hi, m["normed_hi"] + n + 1)
                        pool.tensor_tensor(lo, norm_slot(o["what"], n)[0], hi.bitcast(F32),
                                           ALU.subtract).then_inc(normed_lo, 1)
            elif name == "mem":
                with pool.Fori(0, 8) as it:
                    mi = dict(m, w=m["w"] + 2 * it)
                    for r in range(2):
                        split_weight(mi, r + 1, KT * 128)
                split_weight(m, 17, KT * 128)
            elif name == "gate":
                split_weight(m, 2, KT * 128)
            elif name == "memory_jobs":
                per = job_counts("M")
                for j in range(2):
                    job(at_iteration(m, per, j), "M", 4 * j, m["w"], KT * 128)
            elif name == "latents":
                for t in range(5):
                    split_weight(m, t + 1, KT * 128)
                low(m, 0, lat_v[:, 1, :, TOK:KEYS], c_cache[:, :, :], lat_v[:, 0, :, TOK:KEYS])
            elif name == "jobs":
                kind = o["kind"]
                per = job_counts(kind)
                side = SIDE_PROJ[kind]
                n_w, next_wide = len(side), 128 * side[0][0]
                if kind == "C":
                    split_weight(m, 0, next_wide)
                for t in range(1, n_w + 1):
                    split_weight(m, t, 128 * side[t % n_w][0])
                if kind == "C":
                    low(m, 0, q_sp[0:96, 1, :], qe_raw[0:96, :], q_sp[0:96, 0, :])
                    q_and_k_of_c(m, 0)
                    q_and_k_of_c(m, 1)
                else:
                    q_and_k(m, 0)
                with pool.Fori(0, 2) as it:
                    for u in range(2):
                        job(job_start(m, kind, 2 * it + u), kind, n_w * u + n_w, m["w"] + 2 * n_w * it, next_wide)
                job(job_start(m, kind, 4), kind, n_w, m["w"] + 4 * n_w, 0 if kind == "C" else next_wide)
                job(job_start(m, kind, 5), kind, 0, 0, 0, last=True)
                if o["kind"] == "C":
                    split_weight(dict(m, w=m["w"] + 3 * o["counts"]["w"]), 0, KT * 128)
            elif name == "out":
                for f in range(KT):
                    if o["w8"] + f + 1 < LAST_W8:
                        split_weight(m, f + 1, KT * 128)
                    if f >= 2:
                        pool.wait_ge(squares_ready, m["squares_ready"] + f)
                        pool.tensor_tensor(raw[0][:, 0:TOK], raw[0][:, 0:TOK], raw[1][:, 0:TOK],
                                           ALU.add).then_inc(squares_added, 1)
                if o["w8"] + KT + 1 < LAST_W8:
                    split_weight(m, KT + 1, KT * 128)

    @block.tensor
    def _(pe):
        def project(m, r, kt, chunks, moving, done, freed, freed_before):
            pe.wait_ge(wlo_made, m["w"] + r + 1)
            for a, n in chunks:
                if done >= 2:
                    pe.wait_ge(freed, freed_before + done - 1)
                out = acc[done % 2][:, 0:n]
                for k in range(kt):
                    for i, (ws, xs) in enumerate(PASSES):
                        w = (w_hi, w_lo)[ws][:, r % 2, 128 * k:128 * k + 128]
                        ins = pe.matmul(out, w, moving(xs, k, a, n), start=k == 0 and i == 0,
                                        stop=k == kt - 1 and i == 2)
                ins.then_inc(acc_ready, 1)
                done += 1
            return done

        def banks_free(m):
            pe.wait_ge(acc_read_act, m["acc_read_act"])
            pe.wait_ge(acc_read_dve, m["acc_read_dve"])
            pe.wait_ge(turned_lo_made, m["turned_lo_made"])

        def project_pair(m, moving, operand_ready, before):
            pe.wait_ge(acc_read_act, m["acc_read_act"])
            pe.wait_ge(scores_biased, m["scores_biased"])
            pe.wait_ge(turned_lo_made, m["turned_lo_made"])
            pe.wait_ge(wlo_made, m["w"] + 2)
            for k in range(KT):
                pe.wait_ge(operand_ready, before + k + 1)
                for r in range(2):
                    for c, (a, n) in enumerate(token_chunks(TOK, CHUNK_TOK)):
                        for i, (ws, xs) in enumerate(PASSES):
                            w = (w_hi, w_lo)[ws][:, r, 128 * k:128 * k + 128]
                            ins = pe.matmul(pair_banks[3 * r + c][:, 0:n], w, moving[:, xs, k, a:a + n],
                                            start=k == 0 and i == 0, stop=k == KT - 1 and i == 2)
                        if k == KT - 1:
                            ins.then_inc(acc_ready, 1)

        def sums(m, k, squares, chunks, first, last, banks=None):
            pe.wait_ge(squares_ready, m["squares_ready"] + k + 1)
            for c, (a, n) in enumerate(chunks):
                ins = pe.matmul((banks or pair_banks)[c][:, 0:n], ones[:, :], squares[:, a:a + n], start=first, stop=last)
            ins.then_inc(squares_summed, 1)

        def moving_of(kind, t):
            if kind == "C":
                return cq_v if t < 2 else lat_v
            return h_v

        def side_part(m, kind, r, done, t, c, number, part, parts):
            kt, chunks = SIDE_PROJ[kind][t]
            a, n = chunks[c]
            moving = moving_of(kind, t)
            passes = [(k, i) for k in range(kt) for i in range(3)]
            if part == 0:
                pe.wait_ge(wlo_made, m["w"] + r + t + 1)
                pe.wait_ge(acc_read_act, m["acc_read_act"] + done + number)
            for k, i in passes[len(passes) * part // parts:len(passes) * (part + 1) // parts]:
                ws, xs = PASSES[i]
                w = (w_hi, w_lo)[ws][:, (r + t) % 2, 128 * k:128 * k + 128]
                ins = pe.matmul(acc[1][:, 0:n], w, moving[:, xs, k, a:a + n], start=k == 0 and i == 0,
                                stop=k == kt - 1 and i == 2)
            if part == parts - 1:
                ins.then_inc(acc_ready, 1)

        def job(m, kind, r0, w, last=False):
            groups, proj, v_chunks = GROUPS[kind], JOB_PROJ[kind], V_CHUNKS[kind]
            wm = dict(m, w=w)
            if proj:
                banks_free(m)
            done = 0
            for j, (kt, chunks) in enumerate(proj):
                done = project(wm, r0 + j, kt, chunks, lambda s_, k, a, n: h_v[:, s_, k, a:a + n], done, acc_read_act, m["acc_read_act"])
            if EARLY[kind]:
                project(wm, r0 + len(proj), KT, SIDE_PROJ[kind][0][1][:EARLY[kind]],
                        lambda s_, k, a, n: h_v[:, s_, k, a:a + n], done, acc_read_act, m["acc_read_act"])
            nv = len(v_chunks)

            def transposed_v():
                for v, chunk in enumerate(v_chunks):
                    if v == 0:
                        if kind == "M":
                            pe.wait_ge(vcache_loaded, m["vcache_loaded"] + 32)
                        pe.wait_ge(acc_read_act, m["acc_read_act"] + done + EARLY[kind])
                        pe.wait_ge(acc_read_dve, m["acc_read_dve"] - (kind == "B"))
                        pe.wait_ge(turned_lo_made, m["turned_lo_made"])
                    if v >= 2:
                        pe.wait_ge(turned_lo_made, m["turned_lo_made"] + v - 1)
                    for i, (_, col, n) in enumerate(chunk):
                        ins = pe.transpose(t_ps[v % 2][0:n, 128 * i:128 * i + 128], raw[0][:, col:col + n], ident[:, :])
                    ins.then_inc(turned_ready, 1)

            if proj:
                transposed_v()
                pe.wait_ge(opnd_lo_made, m["opnd_lo_made"] + N_SPLITS[kind])
            else:
                pe.wait_ge(opnd_lo_made, m["opnd_lo_made"])
                pe.wait_ge(scores_biased, m["scores_biased"])
            s = 0

            def scores(g):
                nonlocal s
                for step in g.steps:
                    if s >= 2:
                        pe.wait_ge(scores_biased, m["scores_biased"] + s - 1)
                    if kind == "C":
                        rows = slice(0, 96)
                        q_v, k_v = (qo_sp, ko_v) if step.head else (q_sp, k_sp)
                    else:
                        x = step.which if kind == "B" else step.head
                        rows = slice(64 * x, 64 * x + 64)
                        q_v, k_v = q_sp, k_sp
                    if step.rows == DEC:
                        settle(pe)
                    for key, col, n in step.segs:
                        for i, (qs, ks) in enumerate(PASSES):
                            ins = pe.matmul(s_ps[s % 2][0:step.rows, col:col + n],
                                            q_v[rows, qs, step.q0:step.q0 + step.rows],
                                            k_v[rows, ks, key:key + n], start=i == 0, stop=i == 2)
                    ins.then_inc(scores_ready, 1)
                    s += 1

            a_i = 0
            steps_of = 0
            p_done = 0
            ends, total = [], 0
            for g in groups:
                total += 1 + (g.qn > DEC)
                ends.append(total)

            def turn(g, chunk, a):
                tv = nv + a
                if tv >= 2:
                    pe.wait_ge(turned_lo_made, m["turned_lo_made"] + tv - 1)
                if g.qn == DEC:
                    settle(pe)
                for i, vt, n, cols in chunk:
                    for t, col in enumerate(cols):
                        if col is None:
                            continue
                        step = g.steps[t * (2 if kind == "B" else 1)]
                        at = prob_at(g, step) + col
                        to = DEC * i if g.qn == DEC else 256 * i + 128 * t
                        ins = pe.transpose(t_ps[tv % 2][0:n, to:to + step.rows],
                                           prob[0:step.rows, at:at + n], ident[0:step.rows, 0:step.rows])
                ins.then_inc(turned_ready, 1)

            def times_v(g, h, chunk, a, first, last):
                pe.wait_ge(turned_lo_made, m["turned_lo_made"] + nv + a + 1)
                if first and kind in "AB" and g.qn == DEC:
                    pe.wait_ge(opnd_lo_made, m["opnd_lo_made"] + 1)
                if first and (h >= 2 or (h and SIDE_PROJ[kind])):
                    pe.wait_ge(acc_read_dve, m["acc_read_dve"] + h - (0 if SIDE_PROJ[kind] else 1))
                width = 128 if kind == "B" else 64
                c0 = 0 if kind == "B" else 64 * g.head
                for x, (i, vt, n, cols) in enumerate(chunk):
                    if g.qn == DEC:
                        src, dst, w_ = DEC * i, 0, DEC
                    else:
                        t0 = 0 if cols[0] is not None else 1
                        w_ = 128 * sum(c is not None for c in cols)
                        src, dst = 256 * i + 128 * t0, 128 * t0
                    for y, (vs, ps) in enumerate(PASSES):
                        ins = pe.matmul(acc[output_bank(kind, h)][0:width, dst:dst + w_], v_sp[0:n, vs, vt, c0:c0 + width],
                                        pt[0:n, a % 2, ps, src:src + w_],
                                        start=first and x == 0 and y == 0,
                                        stop=last and x == len(chunk) - 1 and y == 2)
                ins.then_inc(pv_done, 1)

            scores(groups[0])
            if kind != "B":
                scores(groups[1])
            if not proj:
                transposed_v()
            if kind == "B":
                scores(groups[1])
            turned = []
            for h, g in enumerate(groups):
                pe.wait_ge(probs_ready, m["probs_ready"] + ends[h])
                n = len(g.chunks)
                for c in range(n):
                    turn(g, g.chunks[c], a_i + c)
                    turned.append((g, h, g.chunks[c], a_i + c, c == 0, c == n - 1))
                    if c == n - 1 and h + 2 < len(groups):
                        scores(groups[h + 2])
                    for t, sc, number, part, parts in side_slots(kind, h, last)[c]:
                        side_part(wm, kind, r0 + len(proj), done, t, sc, number, part, parts)
                    if len(turned) > 1:
                        times_v(*turned.pop(0))
                times_v(*turned.pop(0))
                a_i += n
            if kind == "B":
                sums(m, 0, o_squares, token_chunks(TOK, CHUNK_TOK), True, True, head_banks)

        pe.wait_ge(consts_loaded, 16 * 4)
        pe.wait_ge(consts_set, 1)
        for name, m, o in phases():
            if name == "norm":
                tiles, _, chunks, _ = norm_plan(o["what"], o.get("layer", 0))
                if o.get("summed"):
                    continue
                banks_free(m)
                pe.wait_ge(scores_biased, m["scores_biased"])
                for k in range(len(tiles)):
                    sums(m, k, raw[k % 2], chunks, k == 0, k == len(tiles) - 1)
            elif name == "mem":
                banks_free(m)
                pe.wait_ge(normed_lo, m["normed_lo"])
                for n in range(16):
                    layer = n // 4
                    project(m, n, KT, [(0, MEMT)],
                            lambda s_, k, a, w: memh_v[:, s_, (8 * layer + k) * MEMT:(8 * layer + k + 1) * MEMT],
                            n, acc_read_act, m["acc_read_act"])
                pe.wait_ge(squares_added, m["squares_added"] + 7)
                sums(m, 7, raw[0], token_chunks(TOK, CHUNK_TOK), True, True)
            elif name == "gate":
                project_pair(m, h_v, normed_lo, m["normed_lo"] - KT)
            elif name == "memory_jobs":
                per = job_counts("M")
                for j in range(2):
                    job(at_iteration(m, per, j), "M", 4 * j, m["w"])
            elif name == "latents":
                banks_free(m)
                done = 0
                for t in range(6):
                    done = project(m, t, KT, token_chunks(TOK, CHUNK_TOK),
                                   lambda s_, k, a, n: h_v[:, s_, k, a:a + n], done, acc_read_act, m["acc_read_act"])
            elif name == "jobs":
                kind = o["kind"]
                per = job_counts(kind)
                if kind == "C":
                    pe.wait_ge(normed_lo, m["normed_lo"])
                    pe.wait_ge(opnd_lo_made, m["opnd_lo_made"])
                    pe.wait_ge(opnd_hi_made, m["opnd_hi_made"])
                banks_free(m)
                side = SIDE_PROJ[kind]
                n_w, done = len(side), 0
                for t, (kt, chunks) in enumerate(side):
                    x = moving_of(kind, t)
                    done = project(m, t, kt, chunks, lambda s_, k, a, n: x[:, s_, k, a:a + n], done,
                                   acc_read_act, m["acc_read_act"])
                with pe.Fori(0, 2) as it:
                    for u in range(2):
                        job(job_start(m, kind, 2 * it + u), kind, n_w * u + n_w, m["w"] + 2 * n_w * it)
                job(job_start(m, kind, 4), kind, n_w, m["w"] + 4 * n_w)
                job(job_start(m, kind, 5), kind, 0, 0, last=True)
            elif name == "out":
                project_pair(m, h_v, normed, m["normed"])
                done = 6
                for f in range(2, KT):
                    done = project(m, f, KT, token_chunks(TOK, CHUNK_TOK),
                                   lambda s_, k, a, n: h_v[:, s_, k, a:a + n], done, acc_read_dve, m["acc_read_dve"])
                pe.wait_ge(squares_added, m["squares_added"] + 6)
                sums(m, 6, raw[0], token_chunks(TOK, CHUNK_TOK), True, False)
                sums(m, 7, raw[1], token_chunks(TOK, CHUNK_TOK), False, True)

    ctx.close()


def _feature_tiles(x):
    t, f = x.shape
    return x.T.reshape(f // 128, 128, t).transpose(1, 0, 2)


def _weight_tile(w, columns):
    k = w.shape[0] // 128
    return w[:, columns].reshape(k, 128, 128).transpose(1, 0, 2).reshape(128, k * 128)


def _constants():
    q = np.arange(128)[:, None]
    j = np.arange(1024)[None, :]
    hidden = (j - 896) // CHUNK > q // CHUNK
    dist = np.where(hidden, NEG, -np.abs(896 + q - j)).astype(np.float32)
    cmask = np.where(hidden, NEG, 0.0).astype(np.float32)
    half = ROPE // 2
    inv = np.exp(np.float32(-math.log(10000.0)) * np.arange(half, dtype=np.float32) * np.float32(2.0)
                 / np.float32(ROPE)).astype(np.float32)
    pos = np.concatenate([np.arange(SEQ), PAST + np.arange(DEC)]).astype(np.float32)
    ang = (inv[:, None] * pos[None, :]).astype(np.float32)
    rope = np.zeros((128, TOK), np.float32)
    rope[64:96] = np.concatenate([np.cos(ang), np.cos(ang)])
    rope[96:128] = np.concatenate([-np.sin(ang), np.sin(ang)])
    slopes = np.exp2(-8.0 * np.arange(1, 7, dtype=np.float32) / 6).astype(np.float32)
    return dict(ident=np.eye(128, dtype=np.float32), dist=dist, cmask=cmask, rope=rope,
                slopes=np.ascontiguousarray(np.broadcast_to(slopes, (128, 6))))


def kernel(**inputs):
    import numpy as np
    import concourse.bacc as bacc
    from concourse.bass_utils import run_bass_kernel_spmd

    a = {k: np.asarray(v) for k, v in inputs.items()}
    sizes = {"A": 768, "B": 768}
    w_in = [a["w_in_a"][0], a["w_in_b"][0], a["w_in_c"][0], a["w_in_a"][1]]
    cols = lambda first: slice(first, first + 128)
    w8 = []
    for layer in range(DEPTH):
        w8 += [_weight_tile(a["w_mem_kv"][layer], cols(128 * t)) for t in range(4)]
    swapped = np.r_[ROPE // 2:ROPE, 0:ROPE // 2]
    for layer, kind in enumerate(KINDS):
        w = w_in[layer]
        n_mix = w.shape[1] - 256 - D
        gate = lambda first, last: [_weight_tile(w, cols(n_mix + 256 + 128 * t)) for t in range(first, last)]
        memory_q = lambda t: [_weight_tile(w, cols(n_mix + 128 * t))]
        w8 += gate(6, 8) + memory_q(0) + gate(0, 3) + memory_q(1) + gate(3, 6)
        if kind == "C":
            w8 += [_weight_tile(w, cols(128 * t)) for t in range(5)]
            kr = w[:, Q_LORA + KV_LORA:n_mix]
            w8.append(_weight_tile(np.concatenate([np.zeros((D, 64), w.dtype), kr, kr[:, swapped]], axis=1), cols(0)))
        else:
            w8 += [_weight_tile(w, cols(768 * part + 128 * t)) for t in range(6) for part in range(3)]
        w8 += [_weight_tile(a["w_out"][layer], cols(128 * t)) for t in range(KT)]
    uq = a["w_uq_c"][0].reshape(Q_LORA, 12, 96)
    uq = np.concatenate([uq, uq[:, :, 64 + swapped]], axis=2)
    ukv = a["w_ukv_c"][0].reshape(KV_LORA, 6, 2, 2, 64)
    col = lambda x: x.reshape(-1, 128).T
    rel = a["rel_bias_a"].transpose(0, 2, 1)
    c = _constants()
    k_cols = lambda x: x.reshape(x.shape[0], 6, 128).transpose(1, 2, 0)
    v_rows = lambda x: x.reshape(4, 128, 6, 128).transpose(2, 1, 0, 3)
    arrays = dict(
        x_in=_feature_tiles(np.concatenate([a["x_prompt"][0], a["x_sample"][0]])),
        mem_in=_feature_tiles(a["mem_prompt"][0]),
        w8=np.stack(w8),
        wc_q=np.stack([_weight_tile(uq[:, h], cols(0)) for h in range(12)]),
        wc_kv=np.stack([_weight_tile(ukv[:, p, :, part].reshape(KV_LORA, 128), cols(0))
                        for p in range(6) for part in range(2)]),
        gains_in=np.concatenate([col(a["norm_g"]), col(a["final_g"]), col(a["mem_norm_g"]), col(a["subln_g_b"]),
                                 col(a["q_norm_g_c"]), col(a["kv_norm_g_c"])], axis=1),
        lambda_in=a["lambda_b"].reshape(256),
        rel_in=rel[:, :, np.minimum(639 - np.arange(768), 128) + 128],
        kcache=np.concatenate([k_cols(a["cache_a_k"][0, 0]), k_cols(a["cache_b_k"][0, 0]), k_cols(a["cache_a_k"][1, 0])]),
        vcache=np.concatenate([v_rows(a["cache_a_v"][0, 0]), v_rows(a["cache_b_v"][0, 0]), v_rows(a["cache_a_v"][1, 0])]),
        lat_cache=_feature_tiles(a["cache_c_lat"][0, 0]),
        rope_cache=a["cache_c_rope"][0, 0].T,
        memk_cache=a["cache_mem_k"].reshape(DEPTH, MEMT, 2, 128).transpose(0, 2, 3, 1),
        memv_cache=a["cache_mem_v"].reshape(DEPTH, MEMT, 2, 128).transpose(0, 2, 3, 1),
        ident_in=c["ident"], dist_in=c["dist"], cmask_in=c["cmask"], rope_in=c["rope"], slope_in=c["slopes"])
    outs = dict(y_out=(D, TOK), k_a=(2, 6, 128, PAST + DEC), v_a=(2, 6, 128, PAST + DEC), k_b=(6, 128, TOK),
                v_b=(6, 128, TOK), lat_out=(KV_LORA, TOK), rope_out=(ROPE, TOK), memkv_out=(128, 16, MEMT))
    nc = bacc.Bacc("TRN2", target_bir_lowering=False, num_devices=1, dynamic_dma_scratch_size=1024)
    aps = {}
    for name in list(arrays):
        arrays[name] = np.ascontiguousarray(arrays[name])
        aps[name] = nc.dram_tensor(name, arrays[name].shape, F32, kind="ExternalInput").ap()
    for name, shape in outs.items():
        aps[name] = nc.dram_tensor(name, shape, F32, kind="ExternalOutput").ap()
    aps["x_scr"] = [nc.dram_tensor(f"x_scr{i}", (128, KT, TOK), F32, kind="Internal").ap() for i in range(DEPTH - 1)]
    aps["rel_scr"] = nc.dram_tensor("rel_scr", (12, 2, 128, BAND), F32, kind="Internal").ap()
    encoder(nc, **aps)
    r = run_bass_kernel_spmd(nc, [arrays], core_ids=[0]).results[0]
    y = r["y_out"].T
    back = lambda x: x.reshape(-1, x.shape[-1]).T
    k_a, v_a = (np.stack([back(r[n][j]) for j in range(2)]) for n in ("k_a", "v_a"))
    k_b, v_b = back(r["k_b"]), back(r["v_b"])
    lat, rope = r["lat_out"].T, r["rope_out"].T
    mem = r["memkv_out"].reshape(128, DEPTH, 2, 2, MEMT).transpose(1, 2, 4, 3, 0).reshape(DEPTH, 2, 1, MEMT, 4, 64)
    heads = lambda x, *shape: x.reshape(x.shape[0], 1, x.shape[1], *shape)
    return (y[None, :SEQ], y[None, SEQ:],
            heads(k_a[:, :PAST], 12, 64), heads(v_a[:, :PAST], 12, 64),
            heads(k_a[:, PAST:], 12, 64), heads(v_a[:, PAST:], 12, 64),
            heads(k_b[None, :SEQ], 6, 2, 64), heads(v_b[None, :SEQ], 6, 128),
            heads(k_b[None, SEQ:], 6, 2, 64), heads(v_b[None, SEQ:], 6, 128),
            lat[None, None, :SEQ], rope[None, None, :SEQ], lat[None, None, SEQ:], rope[None, None, SEQ:],
            mem[:, 0], mem[:, 1])
```
